# Optimizing a Trainium2 kernel written in Bass

```python
import math
import jax, jax.numpy as jnp
from jax import lax
import numpy as np

D_MODEL = 1024
BATCH = 1
SEQ = 512
DEPTH = 2

N_MIXERS = 2
N_HGRN_LAYERS = (DEPTH + 1) // 2
N_DSA_LAYERS = DEPTH // 2

HGRN_EXPAND = 128
HGRN_HEADS = D_MODEL // HGRN_EXPAND
HGRN_DK = HGRN_EXPAND
HGRN_DV = D_MODEL // HGRN_HEADS
HGRN_CHUNK = 32

ATT_HEADS = 16
ATT_HEAD_DIM = D_MODEL // ATT_HEADS
ATT_KV_HEADS = 2
ATT_GROUP = ATT_HEADS // ATT_KV_HEADS
IDX_HEADS = 8
IDX_HEAD_DIM = 64
TOPK_MAX = 256
Q_BLOCK = 128
DSA_SPLITS = (ATT_HEADS * ATT_HEAD_DIM, ATT_KV_HEADS * ATT_HEAD_DIM, ATT_KV_HEADS * ATT_HEAD_DIM,
              IDX_HEADS * IDX_HEAD_DIM, IDX_HEAD_DIM, IDX_HEADS)
DSA_IN_WIDTH = sum(DSA_SPLITS)

REL_BUCKETS = 32
REL_MAX_DIST = 128

D_FF = 2816
CONV_WIDTH = 3

EPS = 1e-6
NEG_BIG = -1e30
TINY = 1e-30


def rms_norm(x, gain):
    xf = x.astype(jnp.float32)
    y = xf * lax.rsqrt(jnp.mean(xf * xf, axis=-1, keepdims=True) + EPS)
    return (y * gain.astype(jnp.float32)).astype(x.dtype)

def hgrn2_mixer(x, w_in, w_out, gate_norm, lower_bound):
    B, L, _ = x.shape
    n_chunks = L // HGRN_CHUNK
    proj = x @ w_in
    q, f, i, g = jnp.split(proj, 4, axis=-1)
    f32 = f.astype(jnp.float32)
    lb = lower_bound.astype(jnp.float32)
    forget = lb + (1.0 - lb) * jax.nn.sigmoid(f32)
    log_f = jnp.log(jnp.maximum(forget, TINY))
    k = (1.0 - lb) * jax.nn.sigmoid(-f32)

    def to_chunks(t, d):
        t = t.astype(jnp.float32).reshape(B, n_chunks, HGRN_CHUNK, HGRN_HEADS, d)
        return t.transpose(1, 0, 3, 2, 4)

    qc, kc, ic, gc = to_chunks(q, HGRN_DK), to_chunks(k, HGRN_DK), to_chunks(i, HGRN_DV), to_chunks(log_f, HGRN_DK)
    causal = jnp.tril(jnp.ones((HGRN_CHUNK, HGRN_CHUNK), dtype=bool))[None, None, :, :, None]

    def step(S, inp):
        qb, kb, ib, gb = inp
        b = jnp.cumsum(gb, axis=2)
        diff = b[:, :, :, None, :] - b[:, :, None, :, :]
        decay = jnp.where(causal, jnp.exp(jnp.where(causal, diff, 0.0)), 0.0)
        scores = jnp.einsum('bhtd,bhsd,bhtsd->bhts', qb, kb, decay)
        o = jnp.einsum('bhts,bhsv->bhtv', scores, ib) + jnp.einsum('bhtd,bhdv->bhtv', qb * jnp.exp(b), S)
        b_last = b[:, :, -1:, :]
        S_new = jnp.exp(b_last[:, :, 0, :])[..., None] * S + jnp.einsum('bhsd,bhsv->bhdv', kb * jnp.exp(b_last - b), ib)
        return S_new, o

    S0 = jnp.zeros((B, HGRN_HEADS, HGRN_DK, HGRN_DV), jnp.float32)
    _, o = lax.scan(step, S0, (qc, kc, ic, gc))
    o = o.transpose(1, 0, 3, 2, 4).reshape(B, L, HGRN_HEADS, HGRN_DV)
    o = o * lax.rsqrt(jnp.mean(o * o, axis=-1, keepdims=True) + EPS) * gate_norm.astype(jnp.float32)
    o = o * jax.nn.silu(g.astype(jnp.float32)).reshape(B, L, HGRN_HEADS, HGRN_DV)
    return o.reshape(B, L, D_MODEL).astype(x.dtype) @ w_out

def t5_causal_bucket(rel):
    n = jnp.maximum(rel, 0)
    max_exact = REL_BUCKETS // 2
    nf = jnp.maximum(n, max_exact).astype(jnp.float32)
    large = max_exact + (jnp.log(nf / max_exact) / math.log(REL_MAX_DIST / max_exact)
                         * (REL_BUCKETS - max_exact)).astype(jnp.int32)
    large = jnp.minimum(large, REL_BUCKETS - 1)
    return jnp.where(n < max_exact, n, large)

def dsa_mixer(x, w_in, w_out, rel_bias):
    B, L, _ = x.shape
    top_k = min(TOPK_MAX, L // 4)
    n_blocks = L // Q_BLOCK
    proj = x @ w_in
    cuts = np.cumsum(DSA_SPLITS)[:-1].tolist()
    q, k, v, q_idx, k_idx, w_idx = jnp.split(proj, cuts, axis=-1)
    q = q.reshape(B, L, ATT_KV_HEADS, ATT_GROUP, ATT_HEAD_DIM)
    q_idx = q_idx.reshape(B, L, IDX_HEADS, IDX_HEAD_DIM)
    w_idx = w_idx * (IDX_HEADS ** -0.5 * IDX_HEAD_DIM ** -0.5)

    def blockify(t):
        return jnp.moveaxis(t.reshape(B, n_blocks, Q_BLOCK, *t.shape[2:]), 1, 0)

    key_pos = jnp.arange(L, dtype=jnp.int32)
    starts = jnp.arange(n_blocks, dtype=jnp.int32) * Q_BLOCK

    def one_block(args):
        qb, qib, wb, start = args
        q_pos = start + jnp.arange(Q_BLOCK, dtype=jnp.int32)
        dots = jnp.einsum('bthd,bsd->bths', qib, k_idx).astype(jnp.float32)
        scores = jnp.einsum('bths,bth->bts', jax.nn.relu(dots), wb.astype(jnp.float32))
        admissible = key_pos[None, :] <= q_pos[:, None]
        scores = jnp.where(admissible[None], scores, NEG_BIG)
        _, sel = lax.top_k(scores, top_k)
        k_sel = jax.vmap(lambda kk, ii: kk[ii])(k, sel).reshape(B, Q_BLOCK, top_k, ATT_KV_HEADS, ATT_HEAD_DIM)
        v_sel = jax.vmap(lambda vv, ii: vv[ii])(v, sel).reshape(B, Q_BLOCK, top_k, ATT_KV_HEADS, ATT_HEAD_DIM)
        logits = jnp.einsum('btkgd,btskd->btkgs', qb, k_sel).astype(jnp.float32) * (ATT_HEAD_DIM ** -0.5)
        rel = q_pos[None, :, None] - sel
        bias = rel_bias.astype(jnp.float32)[t5_causal_bucket(rel)]
        bias = bias.reshape(B, Q_BLOCK, top_k, ATT_KV_HEADS, ATT_GROUP).transpose(0, 1, 3, 4, 2)
        valid = (rel >= 0)[:, :, None, None, :]
        logits = jnp.where(valid, logits + bias, NEG_BIG)
        probs = jax.nn.softmax(logits, axis=-1)
        out = jnp.einsum('btkgs,btskd->btkgd', probs, v_sel.astype(jnp.float32))
        return out.reshape(B, Q_BLOCK, D_MODEL).astype(x.dtype)

    out = lax.map(one_block, (blockify(q), blockify(q_idx), blockify(w_idx), starts))
    out = jnp.moveaxis(out, 0, 1).reshape(B, L, D_MODEL)
    return out @ w_out

def conv_ffn(x, w_up, conv_w, conv_b, w_down):
    h = x @ w_up
    C = h.shape[-1]
    h = lax.conv_general_dilated(h, conv_w[:, None, :].astype(h.dtype), window_strides=(1,),
                                 padding=[(CONV_WIDTH - 1, 0)],
                                 dimension_numbers=('NWC', 'WIO', 'NWC'),
                                 feature_group_count=C) + conv_b
    gate, up = jnp.split(h, 2, axis=-1)
    return (jax.nn.silu(gate) * up) @ w_down

def first_inputs(seed: int = 0) -> dict:
    key = jax.random.key(seed)
    ks = jax.random.split(key, 16)
    D = D_MODEL

    def dense(k, shape, fan_in):
        return jax.random.normal(k, shape, jnp.float32) * fan_in ** -0.5

    return {
        "x": jax.random.normal(ks[0], (BATCH, SEQ, D), jnp.float32),
        "attn_norm": 1.0 + 0.05 * jax.random.normal(ks[1], (DEPTH, D), jnp.float32),
        "ffn_norm": 1.0 + 0.05 * jax.random.normal(ks[2], (DEPTH, D), jnp.float32),
        "hgrn_w_in": dense(ks[3], (N_HGRN_LAYERS, D, 4 * D), D),
        "hgrn_w_out": dense(ks[4], (N_HGRN_LAYERS, D, D), D),
        "hgrn_gate_norm": 1.0 + 0.05 * jax.random.normal(ks[5], (N_HGRN_LAYERS, HGRN_DV), jnp.float32),
        "hgrn_lower_bounds": 0.1 * jax.random.normal(ks[6], (N_HGRN_LAYERS, D), jnp.float32),
        "dsa_w_in": dense(ks[7], (N_DSA_LAYERS, D, DSA_IN_WIDTH), D),
        "dsa_w_out": dense(ks[8], (N_DSA_LAYERS, D, D), D),
        "rel_bias": 0.1 * jax.random.normal(ks[9], (REL_BUCKETS, ATT_HEADS), jnp.float32),
        "ffn_w_up": dense(ks[10], (DEPTH, D, 2 * D_FF), D),
        "ffn_conv_w": dense(ks[11], (DEPTH, CONV_WIDTH, 2 * D_FF), CONV_WIDTH),
        "ffn_conv_b": 0.01 * jax.random.normal(ks[12], (DEPTH, 2 * D_FF), jnp.float32),
        "ffn_w_down": dense(ks[13], (DEPTH, D_FF, D), D_FF),
        "final_norm": 1.0 + 0.05 * jax.random.normal(ks[14], (D,), jnp.float32),
    }

def first_block(x, attn_norm, ffn_norm, hgrn_w_in, hgrn_w_out, hgrn_gate_norm, hgrn_lower_bounds,
              dsa_w_in, dsa_w_out, rel_bias, ffn_w_up, ffn_conv_w, ffn_conv_b, ffn_w_down, final_norm):
    lb_soft = jax.nn.softmax(hgrn_lower_bounds.astype(jnp.float32), axis=0)
    lower_bounds = jnp.cumsum(lb_soft, axis=0) - lb_soft[0]
    h = x
    for layer in range(DEPTH):
        j = layer // N_MIXERS
        hn = rms_norm(h, attn_norm[layer])
        if layer % N_MIXERS == 0:
            mix = hgrn2_mixer(hn, hgrn_w_in[j], hgrn_w_out[j], hgrn_gate_norm[j], lower_bounds[j])
        else:
            mix = dsa_mixer(hn, dsa_w_in[j], dsa_w_out[j], rel_bias)
        h = h + mix
        h = h + conv_ffn(rms_norm(h, ffn_norm[layer]), ffn_w_up[layer], ffn_conv_w[layer],
                         ffn_conv_b[layer], ffn_w_down[layer])
    return rms_norm(h, final_norm)


N_MIXERS_2 = 3
GRID_W = 64
N_HEADS = 16
HEAD_DIM = D_MODEL // N_HEADS
N_KV_HEADS = 4
ROPE_THETA = 10000.0
HY_ORDER = 2
HY_EMB_DIM = 33
HY_FILTER_WIDTH = 64
HY_FAST_DECAY = 0.3
HY_SLOW_DECAY = 1.5
HY_TARGET = 1e-2
S5_GROUP = 16
S5_GROUPS = D_MODEL // S5_GROUP
S5_STATE = 64
S5_DT_MIN = 1e-3
S5_DT_MAX = 1e-1


def rmsnorm(x, g):
    xf = x.astype(jnp.float32)
    y = xf * lax.rsqrt(jnp.mean(xf * xf, axis=-1, keepdims=True) + EPS)
    return (y * g.astype(jnp.float32)).astype(x.dtype)

def dwconv3(x, w, b):
    L = x.shape[1]
    xp = jnp.pad(x, ((0, 0), (1, 1), (0, 0)))
    return xp[:, :L] * w[0] + xp[:, 1:L + 1] * w[1] + xp[:, 2:] * w[2] + b

def axial_rope_tables(L):
    rows = L // GRID_W
    n_freq = HEAD_DIM // 4
    inv = 1.0 / (ROPE_THETA ** (jnp.arange(n_freq, dtype=jnp.float32) / n_freq))
    r = jnp.arange(rows, dtype=jnp.float32)
    col = jnp.arange(GRID_W, dtype=jnp.float32)
    ang_r = jnp.broadcast_to(r[:, None, None] * inv, (rows, GRID_W, n_freq))
    ang_c = jnp.broadcast_to(col[None, :, None] * inv, (rows, GRID_W, n_freq))
    ang = jnp.concatenate([ang_r, ang_c], axis=-1).reshape(L, 2 * n_freq)
    return jnp.cos(ang), jnp.sin(ang)

def apply_rope(x, cos, sin):
    xf = x.astype(jnp.float32).reshape(x.shape[:-1] + (HEAD_DIM // 2, 2))
    x0, x1 = xf[..., 0], xf[..., 1]
    c = cos[None, :, None, :]
    s = sin[None, :, None, :]
    out = jnp.stack([x0 * c - x1 * s, x0 * s + x1 * c], axis=-1).reshape(x.shape)
    return out.astype(x.dtype)

def attention_mixer(h, w_qkv, w_o, q_gain, k_gain, cos, sin):
    Bsz, L, _ = h.shape
    G = N_HEADS // N_KV_HEADS
    qkv = h @ w_qkv
    q, k, v = jnp.split(qkv, [N_HEADS * HEAD_DIM, (N_HEADS + N_KV_HEADS) * HEAD_DIM], axis=-1)
    q = q.reshape(Bsz, L, N_HEADS, HEAD_DIM)
    k = k.reshape(Bsz, L, N_KV_HEADS, HEAD_DIM)
    v = v.reshape(Bsz, L, N_KV_HEADS, HEAD_DIM)
    q = apply_rope(rmsnorm(q, q_gain), cos, sin)
    k = apply_rope(rmsnorm(k, k_gain), cos, sin)
    nb = L // Q_BLOCK
    qb = q.reshape(Bsz, nb, Q_BLOCK, N_KV_HEADS, G, HEAD_DIM).transpose(1, 0, 2, 3, 4, 5)
    scale = HEAD_DIM ** -0.5

    def block(q_blk):
        s = jnp.einsum('bqkgd,bskd->bkgqs', q_blk, k, preferred_element_type=jnp.float32) * scale
        p = jax.nn.softmax(s, axis=-1).astype(v.dtype)
        return jnp.einsum('bkgqs,bskd->bqkgd', p, v)

    o = lax.map(block, qb)
    o = o.transpose(1, 0, 2, 3, 4, 5).reshape(Bsz, L, N_HEADS * HEAD_DIM)
    return o @ w_o

def hyena_pos_features(L):
    t = jnp.linspace(0.0, 1.0, L, dtype=jnp.float32)[:, None]
    bands = (HY_EMB_DIM - 1) // 2
    w = 2.0 * math.pi * jnp.arange(L, dtype=jnp.float32) / L
    f = jnp.linspace(1e-4, bands - 1, bands, dtype=jnp.float32)
    ang = w[:, None] * f[None, :]
    z = jnp.concatenate([t, jnp.cos(ang), -jnp.sin(ang)], axis=-1)
    deltas = jnp.abs(jnp.linspace(math.log(HY_TARGET) / HY_SLOW_DECAY,
                                  math.log(HY_TARGET) / HY_FAST_DECAY, D_MODEL, dtype=jnp.float32))
    decay = jnp.exp(-t * deltas[None, :])
    return z, decay

def hyena_mixer(h, w_in, conv_w, conv_b, f_w1, f_b1, f_w2, f_b2, f_w3, f_freq, skip, w_out, z, decay):
    Bsz, L, D = h.shape
    u = dwconv3(h @ w_in, conv_w, conv_b)
    v, x1, x2 = jnp.split(u, 3, axis=-1)
    a = jnp.sin(f_freq * (z @ f_w1 + f_b1))
    a = jnp.sin(f_freq * (a @ f_w2 + f_b2))
    filt = (a @ f_w3).astype(jnp.float32).reshape(L, HY_ORDER, 2, D) * decay[:, None, None, :]
    fwd = filt[:, :, 0]
    bwd = filt[:, :, 1]
    k2 = jnp.concatenate([fwd, jnp.zeros_like(fwd[:1]), bwd[1:][::-1]], axis=0)
    k2 = k2 / jnp.sum(jnp.abs(k2), axis=0, keepdims=True)
    kf = jnp.fft.rfft(k2, axis=0)
    gates = (x1, x2)
    zc = v
    for o in range(HY_ORDER):
        zf = jnp.fft.rfft(zc.astype(jnp.float32), n=2 * L, axis=1)
        y = jnp.fft.irfft(zf * kf[None, :, o], n=2 * L, axis=1)[:, :L]
        zc = gates[o] * (y.astype(h.dtype) + skip[o] * zc)
    return zc @ w_out

def s5_direction(u, A_re, A_im, log_dt, B_re, B_im, C_re, C_im, reverse):
    L = u.shape[1]
    lam = lax.complex(jnp.minimum(A_re.astype(jnp.float32), -1e-4), A_im.astype(jnp.float32))
    dt = jnp.exp(log_dt.astype(jnp.float32))[:, None]
    lam_bar = jnp.exp(lam * dt)
    b_c = lax.complex(B_re.astype(jnp.float32), B_im.astype(jnp.float32))
    b_bar = ((lam_bar - 1.0) / lam)[..., None] * b_c
    bu = jnp.einsum('blgh,gph->blgp', u.astype(jnp.complex64), b_bar)
    a = jnp.broadcast_to(lam_bar[None, None], (1, L) + lam_bar.shape)

    def combine(e1, e2):
        a1, b1 = e1
        a2, b2 = e2
        return a2 * a1, a2 * b1 + b2

    _, xs = lax.associative_scan(combine, (a, bu), axis=1, reverse=reverse)
    c_c = lax.complex(C_re.astype(jnp.float32), C_im.astype(jnp.float32))
    return jnp.einsum('blgp,ghp->blgh', xs, c_c).real

def s5_mixer(h, A_re, A_im, log_dt, B_re, B_im, C_re, C_im, d_skip, w_glu):
    Bsz, L, D = h.shape
    hf = h.astype(jnp.float32)
    u = hf.reshape(Bsz, L, S5_GROUPS, S5_GROUP)
    y_f = s5_direction(u, A_re[0], A_im[0], log_dt[0], B_re[0], B_im[0], C_re[0], C_im[0], False)
    y_b = s5_direction(u, A_re[1], A_im[1], log_dt[1], B_re[1], B_im[1], C_re[1], C_im[1], True)
    y = (y_f + y_b).reshape(Bsz, L, D) + d_skip.astype(jnp.float32) * hf
    y = jax.nn.gelu(y.astype(h.dtype))
    g_a, g_b = jnp.split(y @ w_glu, 2, axis=-1)
    return g_a * jax.nn.sigmoid(g_b)

def conv_ffn_2(h, w_up, conv_w, conv_b, w_down):
    gate, val = jnp.split(h @ w_up, 2, axis=-1)
    gate = dwconv3(gate, conv_w, conv_b)
    return (jax.nn.silu(gate) * val) @ w_down

def second_inputs(seed: int = 0) -> dict:
    key = jax.random.key(seed)
    ks = iter(jax.random.split(key, 48))
    f32 = jnp.float32

    def nrm(shape, scale):
        return jax.random.normal(next(ks), shape, f32) * scale

    n_attn = len(range(0, DEPTH, N_MIXERS_2))
    n_hy = len(range(1, DEPTH, N_MIXERS_2))
    n_s5 = len(range(2, DEPTH, N_MIXERS_2))
    D = D_MODEL
    G, P, Hg = S5_GROUPS, S5_STATE, S5_GROUP
    qkv_w = (N_HEADS + 2 * N_KV_HEADS) * HEAD_DIM
    return {
        'x': nrm((BATCH, SEQ, D), 1.0),
        'c': nrm((BATCH, D), 1.0),
        'ada_w': nrm((DEPTH, D, 6 * D), 0.5 * D ** -0.5),
        'ada_b': nrm((DEPTH, 6 * D), 0.02),
        'norm1_g': 1.0 + nrm((DEPTH, D), 0.02),
        'norm2_g': 1.0 + nrm((DEPTH, D), 0.02),
        'final_g': 1.0 + nrm((D,), 0.02),
        'attn_w_qkv': nrm((n_attn, D, qkv_w), D ** -0.5),
        'attn_w_o': nrm((n_attn, N_HEADS * HEAD_DIM, D), D ** -0.5),
        'attn_q_gain': 1.0 + nrm((n_attn, HEAD_DIM), 0.02),
        'attn_k_gain': 1.0 + nrm((n_attn, HEAD_DIM), 0.02),
        'hy_w_in': nrm((n_hy, D, 3 * D), D ** -0.5),
        'hy_conv_w': nrm((n_hy, 3, 3 * D), 3 ** -0.5),
        'hy_conv_b': nrm((n_hy, 3 * D), 0.02),
        'hy_f_w1': nrm((n_hy, HY_EMB_DIM, HY_FILTER_WIDTH), HY_EMB_DIM ** -0.5),
        'hy_f_b1': nrm((n_hy, HY_FILTER_WIDTH), 0.1),
        'hy_f_w2': nrm((n_hy, HY_FILTER_WIDTH, HY_FILTER_WIDTH), HY_FILTER_WIDTH ** -0.5),
        'hy_f_b2': nrm((n_hy, HY_FILTER_WIDTH), 0.1),
        'hy_f_w3': nrm((n_hy, HY_FILTER_WIDTH, HY_ORDER * 2 * D), HY_FILTER_WIDTH ** -0.5),
        'hy_f_freq': 1.0 + nrm((n_hy, HY_FILTER_WIDTH), 0.02),
        'hy_skip': nrm((n_hy, HY_ORDER, D), 1.0),
        'hy_w_out': nrm((n_hy, D, D), D ** -0.5),
        's5_A_re': -0.5 + nrm((n_s5, 2, G, P), 0.01),
        's5_A_im': math.pi * jnp.arange(P, dtype=f32) + nrm((n_s5, 2, G, P), 0.01),
        's5_log_dt': jax.random.uniform(next(ks), (n_s5, 2, G), f32, math.log(S5_DT_MIN), math.log(S5_DT_MAX)),
        's5_B_re': nrm((n_s5, 2, G, P, Hg), (2 * Hg) ** -0.5),
        's5_B_im': nrm((n_s5, 2, G, P, Hg), (2 * Hg) ** -0.5),
        's5_C_re': nrm((n_s5, 2, G, Hg, P), (2 * P) ** -0.5),
        's5_C_im': nrm((n_s5, 2, G, Hg, P), (2 * P) ** -0.5),
        's5_D': nrm((n_s5, D), 1.0),
        's5_w_glu': nrm((n_s5, D, 2 * D), D ** -0.5),
        'ffn_w_up': nrm((DEPTH, D, 2 * D_FF), D ** -0.5),
        'ffn_conv_w': nrm((DEPTH, 3, D_FF), 3 ** -0.5),
        'ffn_conv_b': nrm((DEPTH, D_FF), 0.02),
        'ffn_w_down': nrm((DEPTH, D_FF, D), D_FF ** -0.5),
    }

def second_block(x, c, ada_w, ada_b, norm1_g, norm2_g, final_g,
              attn_w_qkv, attn_w_o, attn_q_gain, attn_k_gain,
              hy_w_in, hy_conv_w, hy_conv_b, hy_f_w1, hy_f_b1, hy_f_w2, hy_f_b2, hy_f_w3, hy_f_freq,
              hy_skip, hy_w_out,
              s5_A_re, s5_A_im, s5_log_dt, s5_B_re, s5_B_im, s5_C_re, s5_C_im, s5_D, s5_w_glu,
              ffn_w_up, ffn_conv_w, ffn_conv_b, ffn_w_down):
    L = x.shape[1]
    cos, sin = axial_rope_tables(L)
    z, decay = hyena_pos_features(L)
    c_act = jax.nn.silu(c)
    for i in range(DEPTH):
        m, j = i % N_MIXERS_2, i // N_MIXERS_2
        mod = (c_act @ ada_w[i] + ada_b[i])[:, None, :]
        sh1, sc1, g1, sh2, sc2, g2 = jnp.split(mod, 6, axis=-1)
        h = rmsnorm(x, norm1_g[i]) * (1.0 + sc1) + sh1
        if m == 0:
            y = attention_mixer(h, attn_w_qkv[j], attn_w_o[j], attn_q_gain[j], attn_k_gain[j], cos, sin)
        elif m == 1:
            y = hyena_mixer(h, hy_w_in[j], hy_conv_w[j], hy_conv_b[j], hy_f_w1[j], hy_f_b1[j],
                            hy_f_w2[j], hy_f_b2[j], hy_f_w3[j], hy_f_freq[j], hy_skip[j], hy_w_out[j],
                            z, decay)
        else:
            y = s5_mixer(h, s5_A_re[j], s5_A_im[j], s5_log_dt[j], s5_B_re[j], s5_B_im[j],
                         s5_C_re[j], s5_C_im[j], s5_D[j], s5_w_glu[j])
        x = x + g1 * y
        h = rmsnorm(x, norm2_g[i]) * (1.0 + sc2) + sh2
        x = x + g2 * conv_ffn_2(h, ffn_w_up[i], ffn_conv_w[i], ffn_conv_b[i], ffn_w_down[i])
    return rmsnorm(x, final_g)


def setup_inputs(seed=0):
    out = dict(first_inputs(seed))
    for name, value in second_inputs(seed + 1).items():
        if name != "x":
            out[name + "_2"] = value
    return out


def reference(
    x, attn_norm, ffn_norm, hgrn_w_in, hgrn_w_out, hgrn_gate_norm, hgrn_lower_bounds, dsa_w_in,
    dsa_w_out, rel_bias, ffn_w_up, ffn_conv_w, ffn_conv_b, ffn_w_down, final_norm, c_2, ada_w_2,
    ada_b_2, norm1_g_2, norm2_g_2, final_g_2, attn_w_qkv_2, attn_w_o_2, attn_q_gain_2,
    attn_k_gain_2, hy_w_in_2, hy_conv_w_2, hy_conv_b_2, hy_f_w1_2, hy_f_b1_2, hy_f_w2_2,
    hy_f_b2_2, hy_f_w3_2, hy_f_freq_2, hy_skip_2, hy_w_out_2, s5_A_re_2, s5_A_im_2, s5_log_dt_2,
    s5_B_re_2, s5_B_im_2, s5_C_re_2, s5_C_im_2, s5_D_2, s5_w_glu_2, ffn_w_up_2, ffn_conv_w_2,
    ffn_conv_b_2, ffn_w_down_2,
):
    x = first_block(
        x, attn_norm, ffn_norm, hgrn_w_in, hgrn_w_out, hgrn_gate_norm, hgrn_lower_bounds,
        dsa_w_in, dsa_w_out, rel_bias, ffn_w_up, ffn_conv_w, ffn_conv_b, ffn_w_down, final_norm,
    )
    return second_block(
        x, c_2, ada_w_2, ada_b_2, norm1_g_2, norm2_g_2, final_g_2, attn_w_qkv_2, attn_w_o_2,
        attn_q_gain_2, attn_k_gain_2, hy_w_in_2, hy_conv_w_2, hy_conv_b_2, hy_f_w1_2, hy_f_b1_2,
        hy_f_w2_2, hy_f_b2_2, hy_f_w3_2, hy_f_freq_2, hy_skip_2, hy_w_out_2, s5_A_re_2,
        s5_A_im_2, s5_log_dt_2, s5_B_re_2, s5_B_im_2, s5_C_re_2, s5_C_im_2, s5_D_2, s5_w_glu_2,
        ffn_w_up_2, ffn_conv_w_2, ffn_conv_b_2, ffn_w_down_2,
    )


_drawn_inputs = setup_inputs


def setup_inputs(seed=0):
    import zlib

    import numpy as np

    out = dict(_drawn_inputs(seed))
    spreads = {}
    factors = {'rel_bias': 4.501,
     'ffn_conv_b': 3.834,
     'norm1_g_2': 4.652,
     'norm2_g_2': 6.547,
     'final_g_2': 2.957,
     'attn_q_gain_2': 8.0,
     'attn_k_gain_2': 8.0,
     'hy_conv_b_2': 4.749,
     'hy_f_b1_2': 4.105,
     'hy_f_b2_2': 3.017,
     'hy_f_freq_2': 8.0,
     'ffn_conv_b_2': 8.0}
    for name, (base, spread) in spreads.items():
        noise = np.random.default_rng([zlib.crc32(name.encode()), seed]).standard_normal(out[name].shape)
        drawn = base * np.exp(spread * noise) if base else spread * noise
        out[name] = __import__('jax').numpy.asarray(drawn.astype(out[name].dtype))
    for name, factor in factors.items():
        out[name] = (out[name] * factor).astype(out[name].dtype)
    return out
```

```python
import math
from contextlib import ExitStack

import numpy as np

import concourse.bass as bass
from concourse import mybir

F = mybir.dt.float32
R = mybir.dt.float32r
ALU = mybir.AluOpType
ACTF = mybir.ActivationFunctionType
AX_X = mybir.AxisListType.X
MUL, ADD, SUB = ALU.mult, ALU.add, ALU.subtract

L = 512
D = 1024
NT = D // 128
DFF = 2816
CW = 2048
NRAW, NW = 3, 3
EPS = 1e-6
TINY = 1e-30
NEG = -1e30
GONE = -3e38
SPLITS = (1024, 128, 128, 512, 64, 8)
TOPK = 128
AF = DFF // 128
GROUPS = ((0, 4), (4, 8), (8, 11))
ACT_RING = 10


VEC = {}


def _vec_layout():
    at = 0
    for name, n in (
        ("attn_norm", 16), ("ffn_norm", 16), ("final_norm", 8), ("gate_norm", 1), ("lower", 8),
        ("c", 8), ("ada_b", 96), ("norm1", 16), ("norm2", 16), ("final2", 8), ("q_gain", 1), ("k_gain", 1),
        ("hy_cw", 72), ("hy_cb", 24), ("skip", 16), ("cw0", 264), ("cb0", 88), ("cw1", 132), ("cb1", 44),
        ("fb1", 1), ("fb2", 1), ("freq", 1),
    ):
        VEC[name] = (at, n)
        at += n
    return at


NVEC = _vec_layout()


def shape_constants():
    f32 = np.float32
    c = {}
    c["ident"] = np.eye(128, dtype=f32)
    s, t = np.meshgrid(np.arange(128), np.arange(128), indexing="ij")
    masks = []
    for n in range(7):
        b = 1 << n
        masks.append((s // (2 * b) == t // (2 * b)) & ((s // b) % 2 == 0) & ((t // b) % 2 == 1))
    masks.append(s == t)
    c["masks"] = np.concatenate(masks, axis=1).astype(f32)
    c["cmin"] = np.where(t <= s, f32(3e38), f32(NEG)).astype(f32)
    c["cadd"] = np.where(t <= s, f32(0), f32(NEG)).astype(f32)
    dist = np.maximum(511 - np.arange(640), 0)
    nf = np.maximum(dist, 16).astype(f32)
    large = 16 + (np.log(nf / f32(16)) / f32(math.log(8.0)) * f32(16)).astype(np.int32)
    bucket = np.where(dist < 16, dist, np.minimum(large, 31))
    c["onehot"] = (np.arange(32)[:, None] == bucket[None, :]).astype(f32)
    n_freq = 16
    inv = (f32(1.0) / (f32(10000.0) ** (np.arange(n_freq, dtype=f32) / f32(n_freq)))).astype(f32)
    pos = np.arange(L)
    ang = np.concatenate([(pos // 64).astype(f32)[:, None] * inv, (pos % 64).astype(f32)[:, None] * inv], axis=1)
    pair = (np.arange(128) % 64) // 2
    c["cos"] = np.cos(ang).astype(f32)[:, pair].T
    c["sin"] = np.sin(ang).astype(f32)[:, pair].T
    perm = np.zeros((128, 128), f32)
    i = np.arange(0, 128, 2)
    perm[i + 1, i] = -1.0
    perm[i, i + 1] = 1.0
    c["perm"] = perm
    g = np.arange(128) // 64
    c["pairs"] = (g[:, None] == g[None, :]).astype(f32)
    order = np.concatenate([np.arange(0, L, 2), np.arange(1, L, 2)])
    tl = np.linspace(0.0, 1.0, L, dtype=f32)
    w = (f32(2.0 * math.pi) * np.arange(L, dtype=f32) / f32(L)).astype(f32)
    fr = np.linspace(1e-4, 15, 16, dtype=f32)
    a2 = (w[:, None] * fr[None, :]).astype(f32)
    z = np.concatenate([tl[:, None], np.cos(a2), -np.sin(a2)], axis=1).astype(f32)
    c["zT"] = z[order].T
    deltas = np.abs(np.linspace(math.log(1e-2) / 1.5, math.log(1e-2) / 0.3, D, dtype=f32))
    decay = np.exp(-tl[:, None] * deltas[None, :]).astype(f32)
    c["decay"] = decay[order].reshape(4, 128, D).transpose(1, 0, 2)
    om = 2 * np.pi * (np.arange(256) + 0.5) / 1024
    ev, od = np.arange(0, L, 2), np.arange(1, L, 2)
    fw = np.concatenate([np.cos(np.outer(ev, om)), np.cos(np.outer(od, om)),
                         np.sin(np.outer(ev, om)), np.sin(np.outer(od, om))], axis=1)
    c["fw"] = fw.astype(f32)
    iv = np.concatenate([np.cos(np.outer(om, ev)), np.cos(np.outer(om, od)),
                         np.sin(np.outer(om, ev)), np.sin(np.outer(om, od))], axis=1)
    c["iv"] = iv.astype(f32)
    return {k: np.ascontiguousarray(v, dtype=f32) for k, v in c.items()}


class Engine:

    def __init__(self, sem):
        self.sem, self.count, self.ops, self.seen = sem, 0, [], {}

    def wait(self, *marks):
        for m in marks:
            if m is None:
                continue
            if isinstance(m, list):
                self.wait(*m)
                continue
            sem, value = m
            if self.seen.get(sem, 0) < value:
                self.seen[sem] = value
                self.ops.append(lambda e, s=sem, v=value: e.wait_ge(s, v))

    def quiet(self, fn, *marks):
        self.wait(*marks)
        self.ops.append(fn)

    def run(self, fn, *marks):
        self.wait(*marks)
        self.count += 1
        self.ops.append(lambda e: fn(e).then_inc(self.sem, 1))
        return (self.sem, self.count)

    def dma(self, sem, total, out, in_, *marks):
        self.wait(*marks)
        self.ops.append(lambda e: e.dma_start(out, in_).then_inc(sem, 16))
        return (sem, total)

    def last(self):
        return (self.sem, self.count) if self.count else None


def stream_plan(A):
    items = []

    def cols(w, c0, n, k0=0, k1=None):
        v = w.rearrange("(k p) n -> p k n", p=128)
        return v[:, k0:(k1 if k1 is not None else v.shape[1]), c0:c0 + n]

    def w(name, *parts):
        placed, at = [], 0
        for p in parts:
            placed.append((p, at))
            at += p.shape[2]
        items.append(dict(kind="w", name=name, parts=placed, kt=parts[0].shape[1], n=at))

    def ada(layer, j):
        items.append(dict(kind="ada", name="ada", parts=[(cols(A["ada_w_2"][layer], 256 * j, 256), 0)], kt=8, n=256,
                          layer=layer, j=j))

    def dense(name, wt):
        for j in range(4):
            w(name, cols(wt, 256 * j, 256))

    def ffn(up, down, spare):
        for gi, (p0, p1) in enumerate(GROUPS):
            for p in range(p0, p1):
                w("gate", cols(up, 256 * p, 256))
                w("up", cols(up, DFF + 256 * p, 256))
                for _ in range(3 if spare else 0):
                    if spare:
                        ada(*spare.pop(0))
                if gi and p == p0:
                    q0, q1 = GROUPS[gi - 1]
                    for j in range(4):
                        w("down", cols(down, 256 * j, 256, 2 * q0, 2 * q1))
        q0, q1 = GROUPS[-1]
        for j in range(4):
            w("down", cols(down, 256 * j, 256, 2 * q0, 2 * q1))

    spare = [(l, j) for l in range(2) for j in range(24)]
    hw = A["hgrn_w_in"][0]
    for j in range(4):
        w("i", cols(hw, 2048 + 256 * j, 256))
    for j in range(4):
        w("g", cols(hw, 3072 + 256 * j, 256))
    for h in range(8):
        w("fq", cols(hw, 1024 + 128 * h, 128), cols(hw, 128 * h, 128))
    dense("out", A["hgrn_w_out"][0])
    ffn(A["ffn_w_up"][0], A["ffn_w_down"][0], spare)
    dw = A["dsa_w_in"][0]
    o = [0]
    for n in SPLITS:
        o.append(o[-1] + n)
    w("ix", cols(dw, o[3], 256))
    w("ix", cols(dw, o[3] + 256, 256))
    w("kw", cols(dw, o[4], 64), cols(dw, o[4], 64), cols(dw, o[5], 8))
    w("kk", cols(dw, o[1], 64), cols(dw, o[1], 64), cols(dw, o[1] + 64, 64), cols(dw, o[1] + 64, 64))
    w("v", cols(dw, o[2], 128))
    dense("q", dw[:, 0:1024])
    dense("out", A["dsa_w_out"][0])
    ffn(A["ffn_w_up"][1], A["ffn_w_down"][1], spare)
    assert not spare
    aw = A["attn_w_qkv_2"][0]
    for g in range(2):
        w("kk", *[cols(aw, 1024 + 64 * (2 * g + i // 2), 64) for i in range(4)])
    w("v", cols(aw, 1280, 256))
    dense("q", aw[:, 0:1024])
    dense("out", A["attn_w_o_2"][0])
    ffn(A["ffn_w_up_2"][0], A["ffn_w_down_2"][0], None)
    yw = A["hy_w_in_2"][0]
    for j in range(12):
        w("hy", cols(yw, 256 * j, 256))
    w("fw", cols(A["c_fw"], 0, 1024))
    w("iv", cols(A["c_iv"], 0, 1024))
    items.append(dict(kind="hold", name="hold"))
    for _ in range(3):
        items.append(dict(kind="rawhold", name="rawhold"))
    dense("out", A["hy_w_out_2"][0])
    ffn(A["ffn_w_up_2"][1], A["ffn_w_down_2"][1], None)
    return items


def build(nc, A, out, stop=99):
    ctx = ExitStack()
    with ctx:
        names = [0]

        def sb(shape, dt=F, stack=ctx):
            names[0] += 1
            return stack.enter_context(nc.sbuf_tensor(f"sb{names[0]}", list(shape), dt))

        def semaphore(name):
            return ctx.enter_context(nc.semaphore(name))

        PE, ACT, DVE, POOL, SP = (Engine(semaphore(f"s_{n}")) for n in ("pe", "act", "dve", "pool", "sp"))
        s_out = semaphore("s_out")
        ps = [ctx.enter_context(nc.psum_tensor(f"ps{b}", [128, 512], F)) for b in range(8)]
        pfree = [[] for _ in range(8)]

        x = sb([128, NT, L])
        hh, hl = sb([128, NT, L], R), sb([128, NT, L], R)
        raw = [sb([128, CW]) for _ in range(NRAW)]
        wh = [sb([128, CW], R) for _ in range(NW)]
        wl = [sb([128, CW], R) for _ in range(NW)]
        vec = sb([128, NVEC])
        ident, ones = sb([128, 128]), sb([128, 128])
        sq = [sb([128, L]) for _ in range(2)]
        rstd = sb([128, L])
        ht = [sb([128, L]) for _ in range(2)]
        eps = sb([128, 1])
        acc = [sb([128, 256]) for _ in range(2)]
        mod = sb([128, 96])
        cact = sb([128, 8])
        g1c = sb([128, 8])

        def v(name, i=0, n=1):
            a, m = VEC[name]
            assert i + n <= m
            return vec[:, a + i:a + i + n]

        def load(dst, src, *marks, eng=None):
            s = semaphore(f"ld{names[0]}_{len(loads)}")
            loads.append(s)
            return (eng or SP).dma(s, 16, dst, src, *marks)

        loads = []

        items = stream_plan(A)
        rsem = [semaphore(f"s_raw{i}") for i in range(NRAW)]
        rcount = [0] * NRAW
        rfree = [[] for _ in range(NRAW)]
        rheld = [False] * NRAW
        wfree = [[] for _ in range(NW)]
        wheld = [False] * NW
        nr = nw = 0
        for it in items:
            it["r"] = it["w"] = None
            if it["kind"] != "hold":
                it["r"] = nr % NRAW
                nr += 1
            if it["kind"] in ("w", "hold"):
                it["w"] = nw % NW
                nw += 1
        at = dict(issue=0, split=0, take=0)

        def pump():
            while True:
                moved = False
                if at["issue"] < len(items):
                    it = items[at["issue"]]
                    r = it["r"]
                    if r is None:
                        at["issue"] += 1
                        moved = True
                    elif not rheld[r]:
                        rheld[r] = True
                        it["raw_free"] = rfree[r]
                        for view, c0 in it.get("parts", ()):
                            kt, n = view.shape[1], view.shape[2]
                            dst = raw[r][:, 0:it["kt"] * it["n"]].rearrange("p (k n) -> p k n", n=it["n"])[:, :, c0:c0 + n]
                            rcount[r] += 16
                            it["landed"] = SP.dma(rsem[r], rcount[r], dst, view, it["raw_free"])
                        at["issue"] += 1
                        moved = True
                if at["split"] < at["issue"]:
                    it = items[at["split"]]
                    if it["kind"] in ("ada", "rawhold"):
                        at["split"] += 1
                        moved = True
                    elif not wheld[it["w"]]:
                        s = it["w"]
                        wheld[s] = True
                        it["free"] = wfree[s]
                        if it["kind"] == "w":
                            n = it["kt"] * it["n"]
                            r = it["r"]
                            hi = ACT.run(lambda e, s=s, r=r, n=n: e.activation(wh[s][:, 0:n], raw[r][:, 0:n], ACTF.Copy),
                                         it["landed"], wfree[s])
                            lo = POOL.run(lambda e, s=s, r=r, n=n: e.tensor_tensor(
                                wl[s][:, 0:n], raw[r][:, 0:n], wh[s][:, 0:n].bitcast(F), SUB), hi)
                            it["ready"] = [hi, lo]
                            rfree[r] = [hi, lo]
                            rheld[r] = False
                        at["split"] += 1
                        moved = True
                if not moved:
                    return

        def take(name):
            while True:
                it = items[at["take"]]
                assert it["name"] == name, (it["name"], name)
                at["take"] += 1
                assert at["split"] >= at["take"], name
                return it

        def release(it, *marks):
            if it["kind"] in ("w", "hold"):
                wfree[it["w"]] = list(marks)
                wheld[it["w"]] = False
            else:
                rfree[it["r"]] = list(marks)
                rheld[it["r"]] = False

        def w_views(it):
            n = it["kt"] * it["n"]
            s = it["w"]
            return [t[s][:, 0:n].rearrange("p (k n) -> p k n", n=it["n"]) for t in (wh, wl)]

        hready = [None] * NT
        hfree = [[] for _ in range(NT)]

        def product(o, pairs, first, last, **kw):
            for i, ((ah, al), (bh, bl)) in enumerate(pairs):
                f, l = first and i == 0, last and i == len(pairs) - 1
                PE.quiet(lambda e, o=o, a=al, b=bh, f=f: e.matmul(o, a, b, start=f, stop=False, **kw))
                PE.quiet(lambda e, o=o, a=ah, b=bl: e.matmul(o, a, b, start=False, stop=False, **kw))
                m = lambda e, o=o, a=ah, b=bh, l=l: e.matmul(o, a, b, start=False, stop=l, **kw)
                if i == len(pairs) - 1 and last:
                    return PE.run(m)
                PE.quiet(m)

        def project(it, banks, xh=None, xl=None, ready=None):
            a, b = w_views(it)
            xh = xh or (lambda k: hh[:, k, :])
            xl = xl or (lambda k: hl[:, k, :])
            ready = ready or (lambda k: hready[k])
            PE.wait(it["ready"])
            for bk in banks:
                PE.wait(pfree[bk])
            marks = []
            for k in range(it["kt"]):
                PE.wait(ready(k))
                for j, bk in enumerate(banks):
                    c = slice(128 * j, 128 * j + 128)
                    m = product(ps[bk][:, :], [((a[:, k, c], b[:, k, c]), (xh(k), xl(k)))],
                                k == 0, k == it["kt"] - 1)
                    marks.append(m)
            return [m for m in marks if m]

        def project_tokens(it, c0, n, o, tt):
            a, b = w_views(it)
            PE.wait(it["ready"])
            for k in range(NT):
                PE.wait(hready[k])
                c = slice(128 * tt, 128 * tt + 128)
                m = product(o, [((hh[:, k, c], hl[:, k, c]), (a[:, k, c0:c0 + n], b[:, k, c0:c0 + n]))],
                            k == 0, k == NT - 1)
            return m

        def mm(o, a, b, start=True, stop=True, **kw):
            return lambda e: e.matmul(o, a, b, start=start, stop=stop, **kw)

        def split(hi, lo, src, *marks, eng=None):
            a = ACT.run(lambda e: e.activation(hi, src, ACTF.Copy), *marks)
            b = (eng or DVE).run(lambda e: e.tensor_tensor(lo, src, hi.bitcast(F), SUB), a)
            return [a, b]

        xready = [None] * NT
        sqfree = [[], []]
        STAT = 7
        stat = {}

        def square_sum(j):
            m = ACT.run(lambda e, j=j: e.activation(sq[j % 2][:, :], x[:, j, :], ACTF.Square), xready[j], sqfree[j % 2])
            if j == 0:
                PE.wait(pfree[STAT])
            p = PE.run(mm(ps[STAT][:, :], ones[:, :], sq[j % 2][:, :], j == 0, j == NT - 1), m)
            sqfree[j % 2] = [p]
            stat["m"] = p

        def inverse_rms(bank, n, done, *free):
            a = ACT.run(lambda e: e.activation(rstd[:, :], ps[bank][:, :], ACTF.Sqrt, bias=eps[:, 0:1], scale=1.0 / n), done, *free)
            pfree[bank] = [a]
            return DVE.run(lambda e: e.reciprocal(rstd[:, :], rstd[:, :]), a)

        rfree_std = []
        htfree = [[], []]

        def normalise(gain, shift=None):
            nonlocal rfree_std
            r = inverse_rms(STAT, D, stat["m"], rfree_std)
            for j in range(NT):
                t = ht[j % 2]
                m = DVE.run(lambda e, j=j, t=t: e.scalar_tensor_tensor(t[:, :], x[:, j, :], gain(j), rstd[:, :], MUL, MUL),
                            r, xready[j], htfree[j % 2])
                rfree_std = [m]
                if shift is not None:
                    m = DVE.run(lambda e, j=j, t=t: e.tensor_scalar(t[:, :], t[:, :], shift(j), None, ADD), m)
                hready[j] = split(hh[:, j, :], hl[:, j, :], t[:, :], m, hfree[j])
                htfree[j % 2] = hready[j]

        def add_residual(it, scale=None, stats=True, **kw):
            for j0 in range(0, NT, 2):
                if j0:
                    it = take(it["name"])
                banks = (4, 5) if (j0 // 2) % 2 else (2, 3)
                if kw.get("banks"):
                    banks = kw["banks"][(j0 // 2) % 2]
                done = project(it, banks, **kw.get("rhs", {}))
                release(it, done[-1])
                for i in range(2):
                    j = j0 + i
                    b = banks[i]
                    if scale is None:
                        xready[j] = DVE.run(lambda e, j=j, b=b: e.tensor_tensor(x[:, j, :], x[:, j, :], ps[b][:, :], ADD),
                                            done[i], xready[j])
                    else:
                        xready[j] = DVE.run(lambda e, j=j, b=b: e.scalar_tensor_tensor(
                            x[:, j, :], ps[b][:, :], scale(j), x[:, j, :], MUL, ADD), done[i], xready[j])
                    pfree[b] = [xready[j]]
                if stats:
                    for i in range(2):
                        square_sum(j0 + i)
                pump()
            return done[-1]

        stores = []

        def fence():
            return [e.last() for e in (PE, ACT, DVE, POOL)] + stores

        m_x = None
        st = ExitStack()
        xt = sb([128, 4, D], stack=st)
        m_xt = [load(xt[:, t, :], A["x"][0].rearrange("(t p) d -> p t d", p=128)[:, t, :]) for t in range(4)]
        m_id = load(ident[:, :], A["c_ident"])
        pump()
        m_vec = load(vec[:, :], A["vec"], eng=ACT)
        m_ones = POOL.run(lambda e: e.memset(ones[:, :], 1.0))
        m_eps = POOL.run(lambda e: e.memset(eps[:, :], EPS))
        ACT.wait(m_eps, m_vec)
        PE.wait(m_ones)
        DVE.wait(m_vec)
        PE.wait(m_id)
        for j in range(NT):
            b = j % 4
            PE.wait(pfree[b])
            for t in range(4):
                fn = lambda e, b=b, t=t, j=j: e.transpose(ps[b][:, 128 * t:128 * t + 128], xt[:, t, 128 * j:128 * j + 128], ident[:, :])
                PE.wait(m_xt[t])
                if t < 3:
                    PE.quiet(fn)
                else:
                    m = PE.run(fn)
            xready[j] = DVE.run(lambda e, b=b, j=j: e.tensor_copy(x[:, j, :], ps[b][:, :]), m)
            pfree[b] = [xready[j]]
            square_sum(j)
        st.close()

        scratch = nc.dram_tensor("bias_by_distance", (16, 128, 640), F, kind="Internal")
        st = ExitStack()
        start = fence()
        oh, rb, bv = sb([32, 640], stack=st), sb([32, 16], stack=st), sb([16, 640], stack=st)
        m_oh = load(oh[:, :], A["c_onehot"], start, eng=ACT)
        m_rb = load(rb[:, :], A["rel_bias"], start, eng=ACT)
        m_bv = []
        for i in range(2):
            b = 4 + i
            m = PE.run(mm(ps[b][0:16, 0:320], rb[:, :], oh[:, 320 * i:320 * i + 320]), m_oh, m_rb, pfree[b])
            m_bv.append(DVE.run(lambda e, b=b, i=i: e.tensor_copy(bv[:, 320 * i:320 * i + 320], ps[b][0:16, 0:320]), m, start))
            pfree[b] = [m_bv[-1]]
        m_scratch = load(scratch.ap(), bv[:, :].unsqueeze(1).broadcast_to([16, 128, 640]), m_bv, eng=ACT)
        stores.append(m_scratch)
        st.close()

        lbt = sb([128, 4, 8])
        m = DVE.run(lambda e: e.tensor_tensor(lbt[:, 0, :], v("lower", 0, 8), v("lower", 0, 8), SUB))
        m = ACT.run(lambda e: e.activation(lbt[:, 1, :], lbt[:, 0, :], ACTF.Exp), m)
        m = DVE.run(lambda e: e.reciprocal(lbt[:, 0, :], lbt[:, 1, :]), m)
        m = DVE.run(lambda e: e.tensor_tensor(lbt[:, 1, :], lbt[:, 1, :], lbt[:, 0, :], MUL), m)
        m = DVE.run(lambda e: e.tensor_tensor(lbt[:, 2, :], lbt[:, 1, :], lbt[:, 1, :], SUB), m)
        m_lb = DVE.run(lambda e: e.tensor_scalar(lbt[:, 3, :], lbt[:, 2, :], -1.0, 1.0, MUL, ADD), m)

        def hgrn():
            st = ExitStack()
            begin = [fence(), m_scratch]
            I = sb([128, 4, D], stack=st)
            M = sb([128, 8, L], stack=st)
            E = sb([128, 9, L], stack=st)
            Q, K, P, X = (sb([128, L], stack=st) for _ in range(4))
            SM = [sb([128, L], stack=st) for _ in range(2)]
            SO = sb([128, 768], stack=st)
            masks = sb([128, 1024], stack=st)
            m_masks = load(masks[:, :], A["c_masks"], *begin)
            i_ready = []
            for c in range(4):
                it = take("i")
                for tt in range(4):
                    b = tt
                    PE.wait(pfree[b])
                    m = project_tokens(it, 0, 256, ps[b][:, 0:256], tt)
                    if tt == 3:
                        release(it, m)
                    m = ACT.run(lambda e, b=b, tt=tt, c=c: e.copy(I[:, tt, 256 * c:256 * c + 256], ps[b][:, 0:256]), m, *begin)
                    pfree[b] = [m]
                    i_ready.append(m)
                pump()
            sg_ready = []
            for c in range(4):
                it = take("g")
                banks = (0, 1) if c % 2 else (2, 3)
                done = project(it, banks)
                release(it, done[-1])
                for i in range(2):
                    j, b = 2 * c + i, banks[i]
                    m = ACT.run(lambda e, j=j, b=b: e.activation(M[:, j, :], ps[b][:, :], ACTF.Sigmoid), done[i], *begin)
                    m = DVE.run(lambda e, j=j, b=b: e.tensor_tensor(M[:, j, :], M[:, j, :], ps[b][:, :], MUL), m)
                    pfree[b] = [m]
                    sg_ready.append(m)
                pump()

            state = dict(gen=None, levels=[], diag=None)
            smfree = [[], []]
            sofree = []

            def project_head(h):
                it = take("fq")
                banks = (0, 1) if h % 2 else (2, 3)
                banks = (0, 1)
                done = project(it, banks)
                release(it, done[-1])
                return banks, done

            def halves(t, n):
                return t.rearrange("p (m two b) -> p m two b", two=2, b=1 << n)

            def generate(h, banks, done):
                free = [state["diag"], state["gen"]]
                f = ACT.run(lambda e: e.activation(P[:, :], ps[banks[0]][:, :], ACTF.Sigmoid), done[0], free, *begin)
                k = ACT.run(lambda e: e.activation(K[:, :], ps[banks[0]][:, :], ACTF.Sigmoid, scale=-1.0))
                q = ACT.run(lambda e: e.copy(Q[:, :], ps[banks[1]][:, :]), done[1])
                pfree[banks[0]], pfree[banks[1]] = [k], [q]
                one = DVE.run(lambda e: e.memset(X[:, :], 1.0), state["gen"], *begin)
                a = DVE.run(lambda e: e.tensor_scalar(P[:, :], P[:, :], lbt[:, 3, h:h + 1], lbt[:, 2, h:h + 1], MUL, ADD), f, m_lb)
                k = DVE.run(lambda e: e.tensor_scalar(K[:, :], K[:, :], lbt[:, 3, h:h + 1], None, MUL), k)
                p = DVE.run(lambda e: e.tensor_scalar(P[:, :], P[:, :], TINY, None, ALU.max), a)
                xm = one
                ready = []
                for n in range(9):
                    Ev, Qv, Kv, Pv, Xv = (halves(t, n) for t in (E[:, n, :], Q[:, :], K[:, :], P[:, :], X[:, :]))
                    a = DVE.run(lambda e, o=Ev, q=Qv, p=Pv: e.tensor_tensor(o[:, :, 1, :], q[:, :, 1, :], p[:, :, 1, :], MUL),
                                q, p, state["levels"])
                    b = DVE.run(lambda e, o=Ev, k=Kv, x_=Xv: e.tensor_tensor(o[:, :, 0, :], k[:, :, 0, :], x_[:, :, 0, :], MUL), k, xm)
                    ready.append(b)
                    if n < 8:
                        bl, nb = 1 << n, 256 >> n
                        xm = DVE.run(lambda e, x_=Xv, p=Pv, bl=bl, nb=nb: e.tensor_tensor(
                            x_[:, :, 0, :], x_[:, :, 0, :], p[:, :, 1, bl - 1:bl].broadcast_to([128, nb, bl]), MUL), p, b)
                        p = DVE.run(lambda e, p=Pv, bl=bl, nb=nb: e.tensor_tensor(
                            p[:, :, 1, :], p[:, :, 1, :], p[:, :, 0, bl - 1:bl].broadcast_to([128, nb, bl]), MUL), xm)
                state["gen"] = b
                return dict(h=h, levels=ready, q=q, k=k)

            def scores(g, between):
                nonlocal sofree
                h = g["h"]
                hc = slice(128 * h, 128 * h + 128)
                OB = 3

                def far_levels():
                    PE.wait(pfree[4], pfree[5], g["levels"][8])
                    for s in range(2):
                        PE.quiet(mm(ps[4][:, 256 * s:256 * s + 256], E[:, 8, 128 * s:128 * s + 128], E[:, 8, 256:512]))
                    for i in range(2):
                        m = mm(ps[5][:, 128 * i:128 * i + 128], E[:, 7, 256 * i:256 * i + 128], E[:, 7, 256 * i + 128:256 * i + 256])
                        if i == 0:
                            PE.quiet(m)
                    m = PE.run(m)
                    a = ACT.run(lambda e: e.copy(SO[:, 0:512], ps[4][:, :]), m, sofree, *begin)
                    b = ACT.run(lambda e: e.copy(SO[:, 512:768], ps[5][:, 0:256]))
                    pfree[4], pfree[5] = [a], [b]
                    return b

                def near_levels(tt):
                    A0, A1 = ((6, 7), (4, 5))[tt % 2]
                    c = slice(128 * tt, 128 * tt + 128)
                    PE.wait(pfree[A0], pfree[A1], g["levels"][8], g["q"], g["k"])
                    for n in range(8):
                        o = ps[A0 if n < 4 else A1][:, 128 * (n % 4):128 * (n % 4) + 128]
                        f = mm(o, E[:, n, c], E[:, n, c]) if n < 7 else mm(o, K[:, c], Q[:, c])
                        if n in (3, 7):
                            m = PE.run(f)
                            if n == 3:
                                m3 = m
                        else:
                            PE.quiet(f)
                    if tt == 3:
                        state["levels"] = [m]
                        state["diag"] = m
                    a = DVE.run(lambda e, A0=A0: e.tensor_tensor(SM[0][:, :], ps[A0][:, :], masks[:, 0:512], MUL), m3, smfree[0], m_masks)
                    b = DVE.run(lambda e, A1=A1: e.tensor_tensor(SM[1][:, :], ps[A1][:, :], masks[:, 512:1024], MUL), m, smfree[1])
                    pfree[A0], pfree[A1] = [a], [b]
                    return a, b

                kw = dict(skip_group_check=True)

                def far_values(m):
                    nonlocal sofree
                    PE.wait(m, pfree[OB], i_ready)
                    for s in range(2):
                        PE.quiet(mm(ps[OB][:, 256:512], I[:, s, hc], SO[:, 256 * s:256 * s + 256], s == 0, False, **kw))
                    PE.quiet(mm(ps[OB][:, 128:256], I[:, 0, hc], SO[:, 512:640], False, False, **kw))
                    sofree = [PE.run(mm(ps[OB][:, 384:512], I[:, 2, hc], SO[:, 640:768], False, False, **kw))]

                def near_values(tt, marks):
                    for n in range(8):
                        f = mm(ps[OB][:, 128 * tt:128 * tt + 128], I[:, tt, hc], SM[n // 4][:, 128 * (n % 4):128 * (n % 4) + 128],
                               False, n == 7, **kw)
                        PE.wait(marks[n // 4])
                        if n in (3, 7):
                            m = PE.run(f)
                            smfree[n // 4] = [m]
                        else:
                            PE.quiet(f)
                    return m

                mo = far_levels()
                m0 = near_levels(0)
                far_values(mo)
                prev = m0
                for tt in range(1, 4):
                    last = near_values(tt - 1, prev)
                    prev = near_levels(tt)
                between()
                last = near_values(3, prev)
                s2 = ACT.run(lambda e: e.activation(sq[0][:, :], ps[OB][:, :], ACTF.Square), last, sqfree[0])
                p = PE.run(mm(ps[6][:, :], ones[:, :], sq[0][:, :]), s2, pfree[6])
                sqfree[0] = [p]
                r = inverse_rms(6, 128, p, rfree_std)
                t = DVE.run(lambda e: e.scalar_tensor_tensor(ht[0][:, :], ps[OB][:, :], v("gate_norm"), rstd[:, :], MUL, MUL),
                            r, htfree[0])
                rfree_std[:] = [t]
                pfree[OB] = [t]
                m = DVE.run(lambda e: e.tensor_tensor(M[:, h, :], M[:, h, :], ht[0][:, :], MUL), t, sg_ready[h])
                htfree[0] = [m]
                return m

            banks, done = project_head(0)
            g = generate(0, banks, done)
            pump()
            m_ready = []
            nxt = {}
            for h in range(8):
                def between():
                    if h < 7:
                        nxt["b"], nxt["d"] = project_head(h + 1)
                m_ready.append(scores(g, between))
                if h < 7:
                    g = generate(h + 1, nxt["b"], nxt["d"])
                pump()
            last = PE.last()
            for j in range(NT):
                hready[j] = split(hh[:, j, :], hl[:, j, :], M[:, j, :], m_ready[j], last, eng=POOL if j % 2 else DVE)
            it = take("out")
            done = add_residual(it)
            for j in range(NT):
                hfree[j] = [done]
            st.close()

        ada_i = [0]
        accfree = [[], []]

        def ada_step():
            it = items[at["take"]]
            if it["kind"] != "ada":
                return
            take("ada")
            s = ada_i[0] % 2
            ada_i[0] += 1
            w = raw[it["r"]][:, :].rearrange("p (k n) -> p k n", n=256)
            m = DVE.run(lambda e: e.tensor_scalar(acc[s][:, :], w[:, 0, :], cact[:, 0:1], None, MUL), it["landed"], accfree[s], m_cact)
            for k in range(1, NT):
                m = DVE.run(lambda e, k=k: e.scalar_tensor_tensor(acc[s][:, :], w[:, k, :], cact[:, k:k + 1], acc[s][:, :], MUL, ADD), m)
            release(it, m)
            pump()
            PE.wait(pfree[6], m)
            PE.quiet(mm(ps[6][:, 0:1], acc[s][:, 0:128], ones[:, 0:1]))
            p = PE.run(mm(ps[6][:, 1:2], acc[s][:, 128:256], ones[:, 0:1]))
            accfree[s] = [p]
            c = 48 * it["layer"] + 2 * it["j"]
            m = DVE.run(lambda e: e.tensor_tensor(mod[:, c:c + 2], ps[6][:, 0:2], v("ada_b", c, 2), ADD), p)
            pfree[6] = [m]
            ada_done.append(m)

        ada_done = []
        m_cact = ACT.run(lambda e: e.activation(cact[:, :], v("c", 0, 8), ACTF.Silu))

        def ffn(convs, width, offset, scale=None):
            st = ExitStack()
            begin = fence()
            ah, al = sb([128, ACT_RING, L], R, st), sb([128, ACT_RING, L], R, st)
            yg, yu, sg, pr = ([sb([128, L], stack=st) for _ in range(2)] for _ in range(4))
            a_ready, a_free = {}, [[] for _ in range(ACT_RING)]
            tfree = [[begin], [begin]]

            def conv(cv, tile, b, done, dst, *free):
                wt, bias = cv
                m = ACT.run(lambda e: e.activation(dst[:, :], ps[b][:, :], ACTF.Identity, bias=bias(tile), scale=wt(offset, tile)), done, *free)
                for tap in range(3):
                    sh = tap - offset
                    if sh < 0:
                        o, i = dst[:, -sh:L], ps[b][:, 0:L + sh]
                    elif sh > 0:
                        o, i = dst[:, 0:L - sh], ps[b][:, sh:L]
                    else:
                        continue
                    m = DVE.run(lambda e, o=o, i=i, tap=tap: e.scalar_tensor_tensor(o, i, wt(tap, tile), o, MUL, ADD), m)
                return m

            def up_pair(p):
                it = take("gate")
                dg = project(it, (0, 1))
                release(it, dg[-1])
                g = []
                for i in range(2):
                    t = 2 * p + i
                    m = conv(convs[0], t, i, dg[i], yg[i], tfree[i])
                    pfree[i] = [m]
                    g.append(ACT.run(lambda e, i=i: e.activation(sg[i][:, :], yg[i][:, :], ACTF.Silu), m, tfree[i]))
                pump()
                it = take("up")
                du = project(it, (2, 3))
                release(it, du[-1])
                for i in range(2):
                    t = 2 * p + i
                    b = 2 + i
                    if convs[1] is not None:
                        m = conv(convs[1], t, b, du[i], yu[i], tfree[i])
                        pfree[b] = [m]
                        m = DVE.run(lambda e, i=i: e.tensor_tensor(pr[i][:, :], sg[i][:, :], yu[i][:, :], MUL), m, g[i], tfree[i])
                    else:
                        m = DVE.run(lambda e, i=i, b=b: e.tensor_tensor(pr[i][:, :], sg[i][:, :], ps[b][:, :], MUL), du[i], g[i], tfree[i])
                        pfree[b] = [m]
                    s = t % ACT_RING
                    a_ready[t] = split(ah[:, s, :], al[:, s, :], pr[i][:, :], m, a_free[s], begin, eng=POOL)
                    tfree[i] = [m] + a_ready[t]
                pump()

            def down(gi):
                q0, q1 = GROUPS[gi]
                t0 = 2 * q0
                rhs = dict(xh=lambda k: ah[:, (t0 + k) % ACT_RING, :], xl=lambda k: al[:, (t0 + k) % ACT_RING, :],
                           ready=lambda k: a_ready[t0 + k])
                it = take("down")
                done = add_residual(it, scale, stats=gi == len(GROUPS) - 1, rhs=rhs, banks=((4, 5), (4, 5)))
                for t in range(t0, 2 * q1):
                    a_free[t % ACT_RING] = [done]

            for gi, (p0, p1) in enumerate(GROUPS):
                for p in range(p0, p1):
                    up_pair(p)
                    for _ in range(3):
                        ada_step()
                    if gi and p == p0:
                        down(gi - 1)
            last = PE.last()
            for j in range(NT):
                hfree[j] = [last]
            down(len(GROUPS) - 1)
            st.close()

        def ffn1(layer):
            def wt(tap, tile):
                return v("cw0", 132 * layer + 44 * tap + tile)

            def bias(tile):
                return v("cb0", 44 * layer + tile)

            normalise(lambda j: v("ffn_norm", 8 * layer + j))
            ffn([(wt, bias), (lambda tap, tile: wt(tap, AF + tile), lambda tile: bias(AF + tile))], 3, 2)

        def ffn2(layer):
            def wt(tap, tile):
                return v("cw1", 66 * layer + 22 * tap + tile)

            m = modulated(layer, "norm2", 3)
            ffn([(wt, lambda tile: v("cb1", 22 * layer + tile)), None], 3, 1, scale=m)

        def modulated(layer, gain, first):
            base = 48 * layer + 8 * first
            m = DVE.run(lambda e: e.tensor_scalar(g1c[:, :], mod[:, base + 8:base + 16], 1.0, None, ADD), ada_done)
            m = DVE.run(lambda e: e.tensor_tensor(g1c[:, :], g1c[:, :], v(gain, 8 * layer, 8), MUL), m)
            DVE.wait(m)
            normalise(lambda j: g1c[:, j:j + 1], lambda j: mod[:, base + j:base + j + 1])
            return lambda j: mod[:, base + 16 + j:base + 17 + j]

        def attend(units, logits, soften, value, o_of, finish, pool):
            P, PT, mx, nm, sm, rs = pool
            pf, ptf = [[] for _ in P], [[] for _ in PT]
            LB, TB = (0, 1, 2), (3, 4)
            info = {}

            def first(u):
                b = LB[u % 3]
                PE.wait(pfree[b])
                m = logits(units[u], b)
                k = u % len(P)
                c = slice(u % 8, u % 8 + 1)
                e = soften(units[u], b, m, P[k], mx[:, c], nm[:, c], sm[:, c], pf[k])
                S = units[u][2]
                r = DVE.run(lambda e_: e_.reciprocal(rs[:, c], sm[:, c]), e)
                n = POOL.run(lambda e_: e_.tensor_scalar(P[k][:, 0:S], P[k][:, 0:S], rs[:, c], 1.0, MUL, MUL), r, e)
                info[u] = n

            def second(u):
                k, S, b = u % len(P), units[u][2], TB[u % 2]
                PE.wait(pfree[b], info[u])
                for s in range(S // 128):
                    f = lambda e, s=s: e.transpose(ps[b][:, 128 * s:128 * s + 128], P[k][:, 128 * s:128 * s + 128], ident[:, :])
                    if s < S // 128 - 1:
                        PE.quiet(f)
                m = PE.run(f)
                pf[k] = [m]
                q = u % len(PT)
                a = ACT.run(lambda e: e.copy(PT[q][:, 0:S], ps[b][:, 0:S]), m, ptf[q])
                pfree[b] = [a]
                info[u] = a

            def third(u):
                q, S = u % len(PT), units[u][2]
                o = o_of(units[u])
                PE.wait(info[u])
                n = S // 128
                for s in range(n):
                    f = mm(o, value(units[u], s), PT[q][:, 128 * s:128 * s + 128], s == 0, s == n - 1, skip_group_check=True)
                    if s < n - 1:
                        PE.quiet(f)
                m = PE.run(f)
                ptf[q] = [m]
                finish(u, units[u], m)

            n = len(units)
            for i in range(n + 4):
                if i < n:
                    first(i)
                if 0 <= i - 2 < n:
                    second(i - 2)
                if 0 <= i - 3 < n:
                    third(i - 3)

        def softmax_pool(st):
            return ([sb([128, L], stack=st) for _ in range(3)], [sb([128, L], stack=st) for _ in range(2)],
                    *(sb([128, 8], stack=st) for _ in range(4)))

        OBANK = (5, 6)

        def finish_heads(u, unit, m):
            h, tt, S = unit
            if h % 2 == 1 and tt == 3:
                j, b = h // 2, OBANK[(h // 2) % 2]
                hi = ACT.run(lambda e: e.activation(hh[:, j, :], ps[b][:, :], ACTF.Copy), m, hfree[j])
                lo = DVE.run(lambda e: e.tensor_tensor(hl[:, j, :], ps[b][:, :], hh[:, j, :].bitcast(F), SUB), hi)
                hready[j] = [hi, lo]
                pfree[b] = [hi, lo]

        def o_region(unit):
            h, tt, S = unit
            b = OBANK[(h // 2) % 2]
            if h % 2 == 0 and tt == 0:
                PE.wait(pfree[b])
            return ps[b][64 * (h % 2):64 * (h % 2) + 64, 128 * tt:128 * tt + 128]

        def dsa():
            st = ExitStack()
            begin = fence()
            q = sb([128, 8, L], stack=st)
            k2 = sb([128, 2, L], stack=st)
            V = sb([128, 4, 128], stack=st)
            qi = sb([128, 4, L], stack=st)
            ki = sb([128, L], stack=st)
            wi = sb([128, 4, 8], stack=st)
            work = sb([128, 1280], stack=st)
            relu = [sb([128, L], stack=st) for _ in range(2)]
            T = [sb([128, L], stack=st) for _ in range(4)]
            Lg = [sb([128, L], stack=st) for _ in range(2)]
            cmin, cadd = sb([128, 128], stack=st), sb([128, 128], stack=st)
            m8 = sb([128, 8], stack=st)
            pool = softmax_pool(st)
            m_c = [load(cmin[:, :], A["c_cmin"], begin), load(cadd[:, :], A["c_cadd"], begin)]
            sel = [work[:, 128 * (tt * (tt + 1) // 2):128 * (tt * (tt + 1) // 2) + 128 * (tt + 1)] for tt in range(4)]
            Tsem = [semaphore(f"s_T{i}") for i in range(4)]
            Tfree = [[] for _ in range(4)]
            Tland = {}

            def load_bias(h):
                s = h % 4
                src = bass.AP(tensor=scratch, offset=128 * 640 * h + 127, ap=[[639, 128], [1, 512]])
                Tland[h] = ACT.dma(Tsem[s], 16 * (h // 4 + 1), T[s][:, :], src, Tfree[s], begin, m_scratch)

            for h in range(3):
                load_bias(h)

            qi_ready = []
            for c in range(2):
                it = take("ix")
                banks = (0, 1) if c else (2, 3)
                done = project(it, banks)
                release(it, done[-1])
                for i in range(2):
                    j, b = 2 * c + i, banks[i]
                    m = ACT.run(lambda e, j=j, b=b: e.copy(qi[:, j, :], ps[b][:, :]), done[i], begin)
                    pfree[b] = [m]
                    qi_ready.append(m)
                pump()
            it = take("kw")
            done = project(it, (4,))
            m_ki = ACT.run(lambda e: e.copy(ki[:, :], ps[4][:, :]), done[0], begin)
            pfree[4] = [m_ki]
            PE.wait(pfree[5])
            for tt in range(4):
                m = project_tokens(it, 128, 8, ps[5][:, 8 * tt:8 * tt + 8], tt)
            release(it, m)
            m_wi = DVE.run(lambda e: e.tensor_scalar(wi[:, :, :].rearrange("p a b -> p (a b)"), ps[5][:, 0:32],
                                                     float(8 ** -0.5 * 64 ** -0.5), None, MUL), m, begin)
            pfree[5] = [m_wi]
            pump()
            rl = [[], []]
            n = 0
            m_sc = [None] * 4
            for tt in range(1, 4):
                S = 128 * (tt + 1)
                for h in range(8):
                    b = (4, 5, 6)[n % 3]
                    pr = slice(64 * (h % 2), 64 * (h % 2) + 64)
                    m = PE.run(mm(ps[b][:, 0:S], qi[pr, h // 2, 128 * tt:128 * tt + 128], ki[pr, 0:S]), qi_ready, m_ki, pfree[b])
                    s = n % 2
                    m = ACT.run(lambda e, b=b, s=s, S=S: e.activation(relu[s][:, 0:S], ps[b][:, 0:S], ACTF.Relu), m, rl[s], begin)
                    pfree[b] = [m]
                    o = sel[tt]
                    if h == 0:
                        m = DVE.run(lambda e, o=o, s=s, S=S, tt=tt, h=h: e.tensor_scalar(
                            o, relu[s][:, 0:S], wi[:, tt, h:h + 1], 0.0, MUL, ADD), m, m_wi)
                    else:
                        m = DVE.run(lambda e, o=o, s=s, S=S, tt=tt, h=h: e.scalar_tensor_tensor(
                            o, relu[s][:, 0:S], wi[:, tt, h:h + 1], o, MUL, ADD), m, m_sc[tt])
                    rl[s] = [m]
                    m_sc[tt] = m
                    n += 1
            m_sel = [DVE.run(lambda e: e.tensor_copy(sel[0], cadd[:, :]), m_c, begin)]
            m8m = None
            for tt in range(1, 4):
                o = sel[tt]
                m = DVE.run(lambda e, o=o, tt=tt: e.tensor_tensor(o[:, 128 * tt:128 * tt + 128], o[:, 128 * tt:128 * tt + 128],
                                                                cmin[:, :], ALU.min), m_sc[tt])
                for _ in range(TOPK // 8):
                    a = DVE.run(lambda e, o=o: e.max(m8[:, :], o), m)
                    m = DVE.run(lambda e, o=o: e.match_replace(o, m8[:, :], o, GONE), a)
                m = DVE.run(lambda e, o=o: e.tensor_scalar(o, o, GONE, NEG, ALU.is_gt, MUL), m)
                m_sel.append(m)
            it = take("kk")
            done = project(it, (0, 1))
            release(it, done[-1])
            m_k = []
            for i in range(2):
                m_k.append(ACT.run(lambda e, i=i: e.copy(k2[:, i, :], ps[i][:, :]), done[i], begin))
                pfree[i] = [m_k[-1]]
            pump()
            it = take("v")
            PE.wait(pfree[2])
            for tt in range(4):
                m = project_tokens(it, 0, 128, ps[2][:, 128 * tt:128 * tt + 128], tt)
            release(it, m)
            m_v = ACT.run(lambda e: e.copy(V[:, :, :].rearrange("p a b -> p (a b)"), ps[2][:, :]), m, begin)
            pfree[2] = [m_v]
            pump()
            m_q = []
            for c in range(4):
                it = take("q")
                banks = (0, 1) if c % 2 else (2, 3)
                done = project(it, banks)
                release(it, done[-1])
                for i in range(2):
                    j, b = 2 * c + i, banks[i]
                    m = ACT.run(lambda e, j=j, b=b: e.copy(q[:, j, :], ps[b][:, :]), done[i], begin)
                    pfree[b] = [m]
                    m_q.append(m)
                pump()
            for j in range(NT):
                hfree[j] = [done[-1]]
            lgf = [[], []]
            nun = [0]

            def logits(unit, b):
                h, tt, S = unit
                pr = slice(64 * (h % 2), 64 * (h % 2) + 64)
                return PE.run(mm(ps[b][:, 0:S], q[pr, h // 2, 128 * tt:128 * tt + 128], k2[pr, h // 8, 0:S]), m_q[h // 2], m_k)

            def soften(unit, b, m, P, mx, nm, sm, free):
                h, tt, S = unit
                if tt == 0 and h + 3 < 16:
                    load_bias(h + 3)
                s = nun[0] % 2
                nun[0] += 1
                lg = Lg[s][:, 0:S]
                Tv = T[h % 4][:, 384 - 128 * tt:512]
                m = DVE.run(lambda e: e.scalar_tensor_tensor(lg, ps[b][:, 0:S], 0.125, Tv, MUL, ADD), m, Tland[h], lgf[s])
                pfree[b] = [m]
                if tt == 3:
                    Tfree[h % 4] = [m]
                m = DVE.run(lambda e: e.tensor_tensor_reduce(lg, lg, sel[tt], 1.0, -3e38, ADD, ALU.max, mx), m, m_sel[tt])
                m2 = DVE.run(lambda e: e.tensor_scalar(nm, mx, -1.0, None, MUL), m)
                a = ACT.run(lambda e: e.activation(P[:, 0:S], lg, ACTF.Exp, bias=nm, scale=1.0, accum_out=sm), m2, free)
                lgf[s] = [a]
                return a

            def value(unit, s):
                g = unit[0] // 8
                return V[:, s, 64 * g:64 * g + 64]

            PE.wait(m_v)
            attend([(h, tt, 128 * (tt + 1)) for h in range(16) for tt in range(4)], logits, soften, value, o_region,
                   finish_heads, pool)
            it = take("out")
            done = add_residual(it)
            for j in range(NT):
                hfree[j] = [done]
            st.close()

        def attention(scale):
            st = ExitStack()
            begin = fence()
            q = sb([128, 8, L], stack=st)
            kr = sb([128, 4, L], stack=st)
            V = sb([128, 4, 256], stack=st)
            cos, sin = sb([128, L], stack=st), sb([128, L], stack=st)
            perm, pairs = sb([128, 128], stack=st), sb([128, 128], stack=st)
            qg = [sb([128, L], stack=st) for _ in range(2)]
            t2 = [sb([128, L], stack=st) for _ in range(2)]
            pool = softmax_pool(st)
            m_c = [load(d[:, :], A[n], begin) for d, n in ((cos, "c_cos"), (sin, "c_sin"), (perm, "c_perm"), (pairs, "c_pairs"))]
            gf, tf = [[], []], [[], []]
            n = [0]

            def rotate(dst, b, done, gain):
                nonlocal rfree_std
                i = n[0] % 2
                n[0] += 1
                B1, B2 = ((4, 5), (6, 7))[i]
                a = ACT.run(lambda e: e.activation(qg[i][:, :], ps[b][:, :], ACTF.Copy, scale=gain), done, gf[i], begin)
                s = ACT.run(lambda e: e.activation(sq[i][:, :], ps[b][:, :], ACTF.Square), sqfree[i])
                pfree[b] = [s]
                p1 = PE.run(mm(ps[B1][:, :], pairs[:, :], sq[i][:, :]), s, m_c, pfree[B1])
                sqfree[i] = [p1]
                p2 = PE.run(mm(ps[B2][:, :], perm[:, :], qg[i][:, :]), a, pfree[B2])
                r = inverse_rms(B1, 64, p1, rfree_std)
                m = DVE.run(lambda e: e.tensor_tensor(t2[i][:, :], ps[B2][:, :], sin[:, :], MUL), p2, tf[i], m_c, begin)
                pfree[B2] = [m]
                m1 = DVE.run(lambda e: e.tensor_tensor(qg[i][:, :], qg[i][:, :], cos[:, :], MUL), p2)
                m = DVE.run(lambda e: e.tensor_tensor(t2[i][:, :], t2[i][:, :], qg[i][:, :], ADD), m, m1)
                gf[i] = [m]
                m = DVE.run(lambda e: e.tensor_tensor(dst, t2[i][:, :], rstd[:, :], MUL), m, r, begin)
                tf[i] = [m]
                rfree_std = [m]
                return m

            m_k = []
            for g in range(2):
                it = take("kk")
                banks = (0, 1) if g else (2, 3)
                done = project(it, banks)
                release(it, done[-1])
                for i in range(2):
                    m_k.append(rotate(kr[:, 2 * g + i, :], banks[i], done[i], v("k_gain")))
                pump()
            it = take("v")
            m_v = []
            for tt in range(4):
                b = tt % 2
                PE.wait(pfree[b])
                m = project_tokens(it, 0, 256, ps[b][:, 0:256], tt)
                m_v.append(ACT.run(lambda e, b=b, tt=tt: e.copy(V[:, tt, :], ps[b][:, 0:256]), m, begin))
                pfree[b] = [m_v[-1]]
            release(it, m)
            pump()
            m_q = []
            for c in range(4):
                it = take("q")
                banks = (0, 1) if c % 2 else (2, 3)
                done = project(it, banks)
                release(it, done[-1])
                for i in range(2):
                    m_q.append(rotate(q[:, 2 * c + i, :], banks[i], done[i], v("q_gain")))
                pump()
            for j in range(NT):
                hfree[j] = [done[-1]]

            def logits(unit, b):
                h, tt, S = unit
                pr = slice(64 * (h % 2), 64 * (h % 2) + 64)
                return PE.run(mm(ps[b][:, :], q[pr, h // 2, 128 * tt:128 * tt + 128], kr[pr, h // 4, :]), m_q[h // 2], m_k)

            def soften(unit, b, m, P, mx, nm, sm, free):
                m = DVE.run(lambda e: e.tensor_reduce(mx, ps[b][:, :], AX_X, ALU.max), m)
                m = DVE.run(lambda e: e.tensor_scalar(nm, mx, -0.125, None, MUL), m)
                a = ACT.run(lambda e: e.activation(P[:, :], ps[b][:, :], ACTF.Exp, bias=nm, scale=0.125, accum_out=sm), m, free)
                pfree[b] = [a]
                return a

            def value(unit, s):
                g = unit[0] // 4
                return V[:, s, 64 * g:64 * g + 64]

            PE.wait(m_v)
            attend([(h, tt, L) for h in range(16) for tt in range(4)], logits, soften, value, o_region, finish_heads, pool)
            it = take("out")
            done = add_residual(it, scale)
            for j in range(NT):
                hfree[j] = [done]
            st.close()

        def hyena(scale):
            st = ExitStack()
            begin = fence()
            u = sb([128, 24, L], stack=st)
            aT = sb([64, L], stack=st)
            w1, w2 = sb([33, 64], stack=st), sb([64, 64], stack=st)
            w3 = sb([64, 512], stack=st)
            dec = sb([128, 4, 256], stack=st)
            sf, df = sb([128, 1024], stack=st), sb([128, 1024], stack=st)
            Yt = sb([128, 1024], stack=st)
            inv = sb([128, 4], stack=st)
            m_w1 = load(w1[:, :], A["hy_f_w1_2"][0], begin)
            m_w2 = load(w2[:, :], A["hy_f_w2_2"][0], begin)

            u_ready = []
            for c in range(12):
                it = take("hy")
                banks = ((0, 1), (2, 3))[c % 2]
                done = project(it, banks)
                release(it, done[-1])
                for i in range(2):
                    t, b = 2 * c + i, banks[i]
                    m = ACT.run(lambda e, t=t, b=b: e.activation(u[:, t, :], ps[b][:, :], ACTF.Identity, bias=v("hy_cb", t),
                                                                 scale=v("hy_cw", 24 + t)), done[i], begin)
                    m = DVE.run(lambda e, t=t, b=b: e.scalar_tensor_tensor(u[:, t, 1:L], ps[b][:, 0:L - 1], v("hy_cw", t),
                                                                          u[:, t, 1:L], MUL, ADD), m)
                    m = DVE.run(lambda e, t=t, b=b: e.scalar_tensor_tensor(u[:, t, 0:L - 1], ps[b][:, 1:L], v("hy_cw", 48 + t),
                                                                          u[:, t, 0:L - 1], MUL, ADD), m)
                    pfree[b] = [m]
                    u_ready.append(m)
                pump()
            all_h = done[-1]

            zt = sf[0:33, 0:L]
            m_z = load(zt, A["c_zT"], begin)
            C1 = 6.28125
            C2 = float(np.float32(2 * math.pi - C1))
            C3 = 2 * math.pi - C1 - C2
            MAGIC = 12582912.0

            def sine(dst, b, bias, m):
                t, k = df[0:64, 0:L], df[0:64, L:2 * L]
                m = DVE.run(lambda e: e.tensor_scalar(t, ps[b][0:64, :], bias, v("freq")[0:64], ADD, MUL), m, begin)
                pfree[b] = [m]
                n = DVE.run(lambda e: e.tensor_scalar(k, t, 1.0 / (2 * math.pi), MAGIC, MUL, ADD), m)
                n = DVE.run(lambda e: e.tensor_scalar(k, k, -MAGIC, None, ADD), n)
                for cst in (C1, C2, C3):
                    n = DVE.run(lambda e, cst=cst: e.scalar_tensor_tensor(t, k, -cst, t, MUL, ADD), n)
                n = DVE.run(lambda e: e.tensor_scalar(t, t, 3.1415925, -3.1415925, ALU.min, ALU.max), n)
                return ACT.run(lambda e: e.activation(dst, t, ACTF.Sin), n, begin)

            m = PE.run(mm(ps[4][0:64, :], w1[:, :], zt), m_z, m_w1, pfree[4])
            m = sine(aT[:, :], 4, v("fb1")[0:64], m)
            m = PE.run(mm(ps[4][0:64, :], w2[:, :], aT[:, :]), m, m_w2, pfree[4])
            m_a = sine(aT[:, :], 4, v("fb2")[0:64], m)

            fw_it, iv_it, hold = take("fw"), take("iv"), take("hold")
            held = [take("rawhold") for _ in range(3)]
            fwh, fwl = w_views(fw_it)
            ivh, ivl = w_views(iv_it)
            yh = wh[hold["w"]][:, :].rearrange("p (f q c) -> p f q c", f=2, q=4)
            yl = wl[hold["w"]][:, :].rearrange("p (f q c) -> p f q c", f=2, q=4)
            DVE.wait(*[h["raw_free"] for h in held])
            POOL.wait(*[h["raw_free"] for h in held])
            ACT.wait(hold["free"])
            POOL.wait(hold["free"])
            Fb = raw[held[0]["r"]][:, :].rearrange("p (t c) -> p t c", t=4)
            KK = raw[held[1]["r"]][:, :].rearrange("p (f q c) -> p f q c", f=2, q=4)
            XX = raw[held[2]["r"]][:, 0:1024].rearrange("p (q c) -> p q c", q=4)
            A4 = raw[held[2]["r"]][:, 1024:2048].rearrange("p (q c) -> p q c", q=4)
            hv, lv = (t[:, 0:6, :].rearrange("p a l -> p (a l)").rearrange("p (w t c) -> p w t c", w=3, t=4) for t in (hh, hl))
            Yv = Yt[:, :].rearrange("p (w f c) -> p w f c", w=2, f=2)
            sv, dv = (t[:, :].rearrange("p (t c) -> p t c", t=4) for t in (sf, df))
            ef, tv = [sq[0], sq[1]], [ht[0], ht[1]]
            efree, tfree = [sqfree[0], sqfree[1]], [htfree[0], htfree[1]]
            free = dict(w3=[], dec=[], Fb=[], s=[], d=[], sh=[all_h], dh=[all_h], zh=[all_h], KK=[], XX=[], A4=[], Yt=[], y=[])
            nld = [0, 0]
            s_w3, s_dec = semaphore("s_w3"), semaphore("s_dec")
            cnt = [0]

            def filters(o, cq):
                nld[0] += 2
                nld[1] += 1
                src = A["hy_f_w3_2"][0]
                for d_ in range(2):
                    c = 2048 * o + 1024 * d_ + 256 * cq
                    mw = ACT.dma(s_w3, 16 * nld[0], w3[:, 256 * d_:256 * d_ + 256], src[:, c:c + 256], free["w3"], begin)
                md = ACT.dma(s_dec, 16 * nld[1], dec[:, :, :], A["c_decay"][:, :, 256 * cq:256 * cq + 256], free["dec"], begin)
                ev = []
                for lt in range(4):
                    b = lt % 2
                    PE.wait(mw, m_a, pfree[b])
                    p = PE.run(mm(ps[b][:, :], aT[:, 128 * lt:128 * lt + 128], w3[:, :]))
                    m = None
                    for d_ in range(2):
                        m = DVE.run(lambda e, b=b, lt=lt, d_=d_: e.tensor_tensor(
                            Fb[:, lt, 256 * d_:256 * d_ + 256], ps[b][:, 256 * d_:256 * d_ + 256], dec[:, lt, :], MUL), p, md, free["Fb"])
                    pfree[b] = [m]
                    ev.append(m)
                free["w3"], free["dec"] = [p], [m]
                z0 = DVE.run(lambda e: e.memset(Fb[0:1, 0, 256:512], 0.0), ev)
                a = DVE.run(lambda e: e.tensor_tensor(sv, Fb[:, :, 0:256], Fb[:, :, 256:512], ADD), z0, free["s"])
                b_ = POOL.run(lambda e: e.tensor_tensor(dv, Fb[:, :, 0:256], Fb[:, :, 256:512], SUB), z0, free["d"])
                s_r = split(hv[:, 0], lv[:, 0], sv, a, free["sh"], eng=POOL)
                d_r = split(hv[:, 1], lv[:, 1], dv, b_, free["dh"], eng=POOL)
                free["s"], free["d"] = s_r, d_r
                ab = ACT.run(lambda e: e.activation(Fb[:, :, :], Fb[:, :, :], ACTF.Abs), a, b_)
                PE.wait(ab, pfree[2])
                for ct in range(2):
                    for i in range(8):
                        lt, d_ = i // 2, i % 2
                        c = 256 * d_ + 128 * ct
                        f = mm(ps[2][:, ct:ct + 1], Fb[:, lt, c:c + 128], ones[:, 0:1], i == 0, i == 7)
                        if ct == 1 and i == 7:
                            p = PE.run(f)
                        else:
                            PE.quiet(f)
                free["Fb"] = [p]
                c = 2 * (cnt[0] % 2)
                cnt[0] += 1
                m = DVE.run(lambda e: e.reciprocal(inv[:, c:c + 2], ps[2][:, 0:2]), p)
                pfree[2] = [m]
                m = DVE.run(lambda e: e.tensor_scalar(inv[:, c:c + 2], inv[:, c:c + 2], 2.0 ** -9, None, MUL), m)
                return dict(s=s_r, d=d_r, inv=inv[:, c:c + 2], minv=m)

            def transform(srcs, ready, ft, dst, dfree, bA, bB):
                PE.wait(fw_it["ready"], *ready)
                out_marks = []
                for half, b in ((0, bA), (1, bB)):
                    PE.wait(pfree[b])
                    for q, sc in ((half, srcs[0]), (2 + half, srcs[1])):
                        cols = slice(256 * q + 128 * ft, 256 * q + 128 * ft + 128)
                        o = ps[b][:, 0:256] if q < 2 else ps[b][:, 256:512]
                        m = product(o, [((fwh[:, kt, cols], fwl[:, kt, cols]), (hv[:, sc, 2 * half + kt, :], lv[:, sc, 2 * half + kt, :]))
                                        for kt in range(2)], True, True)
                    out_marks.append(m)
                i = ft
                a = ACT.run(lambda e: e.copy(ef[i][:, :], ps[bA][:, :]), out_marks[0], efree[i])
                pfree[bA] = [a]
                m = DVE.run(lambda e: e.tensor_tensor(dst[:, 0:2, :].rearrange("p a c -> p (a c)"), ef[i][:, :], ps[bB][:, :], ADD),
                            a, out_marks[1], dfree)
                m2 = DVE.run(lambda e: e.tensor_tensor(dst[:, 2, :], ef[i][:, 0:256], ps[bB][:, 0:256], SUB), a)
                m3 = DVE.run(lambda e: e.tensor_tensor(dst[:, 3, :], ps[bB][:, 256:512], ef[i][:, 256:512], SUB))
                pfree[bB] = [m3]
                efree[i] = [m3]
                return m3, out_marks[1]

            def filter_transform(fl):
                r = []
                for ft in range(2):
                    m, p = transform((0, 1), (fl["s"], fl["d"]), ft, KK[:, ft], free["KK"], 0, 1)
                    r.append(m)
                free["sh"], free["dh"] = [p], [p]
                fl["K"] = r

            def tokens(cq):
                ready = []
                for half in range(2):
                    b = 2 + half
                    PE.wait(pfree[b])
                    for t in range(2):
                        for ct in range(2):
                            j = 2 * cq + ct
                            src = u[:, j, half + 256 * t:256 * t + 256:2]
                            o = ps[b][:, 256 * t + 128 * ct:256 * t + 128 * ct + 128]
                            f = lambda e, o=o, src=src: e.transpose(o, src, ident[:, :])
                            PE.wait(u_ready[j])
                            if t == 1 and ct == 1:
                                p = PE.run(f)
                            else:
                                PE.quiet(f)
                    o = slice(2 * half, 2 * half + 2)
                    src = ps[b][:, :].rearrange("p (t c) -> p t c", t=2)
                    a = split(hv[:, 2, o, :], lv[:, 2, o, :], src, p, free["zh"])
                    pfree[b] = a
                    ready += a
                return ready

            def convolve(o, cq, fl):
                z = tokens(cq)
                yr = []
                for ft in range(2):
                    m, p = transform((2, 2), (z,), ft, XX, free["XX"], 4, 5)
                    Kv = KK[:, ft].rearrange("p (f w) c -> p f w c", w=2)
                    Xv = XX.rearrange("p (f w) c -> p f w c", w=2)
                    Av = A4.rearrange("p (f w) c -> p f w c", w=2)
                    a, b = [], []
                    for f_ in range(2):
                        kc = Kv[:, f_, 0:1, :].broadcast_to([128, 2, 256])
                        ks = Kv[:, f_, 1:2, :].broadcast_to([128, 2, 256])
                        a.append(DVE.run(lambda e, f_=f_, kc=kc: e.tensor_tensor(Av[:, f_], Xv[:, f_], kc, MUL), m, fl["K"], free["A4"]))
                        b.append(DVE.run(lambda e, f_=f_, ks=ks: e.tensor_tensor(Xv[:, f_], Xv[:, f_], ks, MUL), a))
                    c_ = DVE.run(lambda e: e.tensor_tensor(Yv[:, 0], Av[:, :, 0, :], Xv[:, :, 1, :], SUB), a, b, free["Yt"])
                    s_ = DVE.run(lambda e: e.tensor_tensor(Yv[:, 1], Av[:, :, 1, :], Xv[:, :, 0, :], ADD), a, b)
                    free["XX"] = [s_]
                    UV = A4.rearrange("p (k w) c -> p k w c", w=2)
                    x1 = POOL.run(lambda e: e.tensor_tensor(UV[:, 0], Yv[:, :, 0, :], Yv[:, :, 1, :], ADD), c_, s_)
                    x2 = POOL.run(lambda e: e.tensor_tensor(UV[:, 1], Yv[:, :, 0, :], Yv[:, :, 1, :], SUB))
                    free["Yt"] = [x2]
                    r = split(yh[:, ft], yl[:, ft], A4, x1, x2, free["y"], eng=POOL)
                    free["A4"] = r
                    yr += r
                free["zh"] = [p]
                free["KK"] = [b[-1]]
                PE.wait(iv_it["ready"], yr)
                for ct in range(2):
                    b = 6 + ct
                    j = 2 * cq + ct
                    PE.wait(pfree[b])
                    for half, (qc, qs) in enumerate(((0, 3), (2, 1))):
                        pairs = []
                        for ft in range(2):
                            for q, g in ((qc, half), (qs, 2 + half)):
                                cs = slice(128 * ct, 128 * ct + 128)
                                pairs.append(((yh[:, ft, q, cs], yl[:, ft, q, cs]),
                                              (ivh[:, ft, 256 * g:256 * g + 256], ivl[:, ft, 256 * g:256 * g + 256])))
                        p = product(ps[b][:, 256 * half:256 * half + 256], pairs, True, True)
                    t = tv[ct]
                    a = ACT.run(lambda e, j=j, t=t: e.activation(t[:, :], u[:, j, :], ACTF.Copy, scale=v("skip", 8 * o + j)),
                                u_ready[j], tfree[ct])
                    tw = t[:, :].rearrange("p (t two) -> p two t", two=2)
                    m = DVE.run(lambda e, b=b, ct=ct, tw=tw: e.scalar_tensor_tensor(
                        tw, ps[b][:, :].rearrange("p (two t) -> p two t", two=2), fl["inv"][:, ct:ct + 1], tw, MUL, ADD),
                        a, p, fl["minv"])
                    pfree[b] = [m]
                    u_ready[j] = DVE.run(lambda e, j=j, t=t: e.tensor_tensor(u[:, j, :], t[:, :], u[:, 8 * (o + 1) + j, :], MUL),
                                         m, u_ready[8 * (o + 1) + j])
                    tfree[ct] = [u_ready[j]]
                free["y"] = [p]
                return p

            todo = [(o, cq) for o in range(2) for cq in range(4)]
            fl = filters(*todo[0])
            for i, (o, cq) in enumerate(todo):
                filter_transform(fl)
                nxt = filters(*todo[i + 1]) if i + 1 < len(todo) else None
                last = convolve(o, cq, fl)
                fl = nxt
            sqfree[0], sqfree[1] = efree
            htfree[0], htfree[1] = tfree
            end = fence()
            for it in (fw_it, iv_it, hold):
                release(it, last)
            for it in held:
                release(it, *[m for m in end if m])
            pump()
            for j in range(NT):
                hready[j] = split(hh[:, j, :], hl[:, j, :], u[:, j, :], u_ready[j], last, free["zh"], free["sh"],
                                  eng=POOL if j % 2 else DVE)
            it = take("out")
            done = add_residual(it, scale)
            for j in range(NT):
                hfree[j] = [done]
            st.close()

        def plain_norm(gain):
            nonlocal rfree_std
            r = inverse_rms(STAT, D, stat["m"], rfree_std)
            for j in range(NT):
                xready[j] = DVE.run(lambda e, j=j: e.scalar_tensor_tensor(x[:, j, :], x[:, j, :], gain(j), rstd[:, :], MUL, MUL),
                                    r, xready[j])
            rfree_std = [xready[NT - 1]]

        def block1_end():
            plain_norm(lambda j: v("final_norm", j))
            for j in range(NT):
                square_sum(j)

        steps = [
            lambda: (normalise(lambda j: v("attn_norm", j)), hgrn()),
            lambda: ffn1(0),
            lambda: (normalise(lambda j: v("attn_norm", 8 + j)), dsa()),
            lambda: ffn1(1),
            lambda: block1_end(),
            lambda: attention(modulated(0, "norm1", 0)),
            lambda: ffn2(0),
            lambda: hyena(modulated(1, "norm1", 0)),
            lambda: ffn2(1),
            lambda: plain_norm(lambda j: v("final2", j)),
        ]
        for step in steps[:stop]:
            step()

        begin = fence()
        st = ExitStack()
        ot = sb([128, 4, D], stack=st)
        for tt in range(4):
            stored = []
            for half in range(2):
                b = (2 * tt + half) % 4
                PE.wait(pfree[b])
                for i in range(4):
                    j = 4 * half + i
                    f = lambda e, b=b, i=i, j=j, tt=tt: e.transpose(ps[b][:, 128 * i:128 * i + 128], x[:, j, 128 * tt:128 * tt + 128], ident[:, :])
                    PE.wait(xready[j])
                    if i < 3:
                        PE.quiet(f)
                    else:
                        m = PE.run(f)
                eng = DVE if half else ACT
                o = ot[:, tt, 512 * half:512 * half + 512]
                fn = (lambda e, o=o, b=b: e.tensor_copy(o, ps[b][:, :])) if half else (lambda e, o=o, b=b: e.copy(o, ps[b][:, :]))
                m = eng.run(fn, m, begin)
                pfree[b] = [m]
                stored.append(m)
            SP.dma(s_out, 16 * (tt + 1), out[0, 128 * tt:128 * tt + 128, :], ot[:, tt, :], stored)
        SP.wait((s_out, 64))
        st.close()

        block = ctx.enter_context(nc.Block())

        @block.sync
        def _(e):
            for op in SP.ops:
                op(e)

        @block.scalar
        def _(e):
            for op in ACT.ops:
                op(e)

        @block.vector
        def _(e):
            for op in DVE.ops:
                op(e)

        @block.gpsimd
        def _(e):
            for op in POOL.ops:
                op(e)

        @block.tensor
        def _(e):
            for op in PE.ops:
                op(e)


_WEIGHTS = ["x", "hgrn_w_in", "hgrn_w_out", "dsa_w_in", "dsa_w_out", "rel_bias", "ffn_w_up", "ffn_w_down", "ada_w_2",
            "attn_w_qkv_2", "attn_w_o_2", "hy_w_in_2", "hy_f_w1_2", "hy_f_w2_2", "hy_f_w3_2", "hy_w_out_2",
            "ffn_w_up_2", "ffn_w_down_2"]


def lay_out(inputs):
    def by_feature(name):
        a = np.asarray(inputs[name])
        return a.reshape(-1, 128).T

    def twice(name):
        return np.tile(np.asarray(inputs[name]).reshape(-1, 1), (2, 1))

    parts = {
        "attn_norm": by_feature("attn_norm"), "ffn_norm": by_feature("ffn_norm"), "final_norm": by_feature("final_norm"),
        "gate_norm": by_feature("hgrn_gate_norm"), "lower": by_feature("hgrn_lower_bounds"), "c": by_feature("c_2"),
        "ada_b": by_feature("ada_b_2"), "norm1": by_feature("norm1_g_2"), "norm2": by_feature("norm2_g_2"),
        "final2": by_feature("final_g_2"), "q_gain": twice("attn_q_gain_2"), "k_gain": twice("attn_k_gain_2"),
        "hy_cw": by_feature("hy_conv_w_2"), "hy_cb": by_feature("hy_conv_b_2"), "skip": by_feature("hy_skip_2"),
        "cw0": by_feature("ffn_conv_w"), "cb0": by_feature("ffn_conv_b"), "cw1": by_feature("ffn_conv_w_2"),
        "cb1": by_feature("ffn_conv_b_2"), "fb1": twice("hy_f_b1_2"), "fb2": twice("hy_f_b2_2"), "freq": twice("hy_f_freq_2"),
    }
    arrays = {n: np.ascontiguousarray(inputs[n]) for n in _WEIGHTS}
    arrays["vec"] = np.ascontiguousarray(np.concatenate([parts[n] for n in VEC], axis=1))
    for n, a in shape_constants().items():
        arrays[f"c_{n}"] = a
    return arrays


def kernel(**inputs):
    import concourse.bacc as _bacc
    from concourse.bass_utils import run_bass_kernel_spmd as _run

    nc = _bacc.Bacc("TRN2", target_bir_lowering=False, num_devices=1)
    arrays, aps = {}, {}
    for name, a in lay_out(inputs).items():
        arrays[f"in_{name}"] = a
        aps[name] = nc.dram_tensor(f"in_{name}", a.shape, mybir.dt.from_np(a.dtype), kind="ExternalInput").ap()
    out = nc.dram_tensor("out_0", (1, L, D), F, kind="ExternalOutput").ap()
    build(nc, aps, out)
    r = _run(nc, [arrays], core_ids=[0])
    return r.results[0]["out_0"]
```

```python
import math
from contextlib import ExitStack

import numpy as np

import concourse.bass as bass
from concourse import mybir

F = mybir.dt.float32
R = mybir.dt.float32r
ALU = mybir.AluOpType
ACTF = mybir.ActivationFunctionType
AX_X = mybir.AxisListType.X
MUL, ADD, SUB = ALU.mult, ALU.add, ALU.subtract

L = 512
D = 1024
NT = D // 128
DFF = 2816
CW = 2048
NRAW, NW = 3, 3
EPS = 1e-6
TINY = 1e-30
NEG = -1e30
GONE = -3e38
SPLITS = (1024, 128, 128, 512, 64, 8)
TOPK = 128
AF = DFF // 128
GROUPS = ((0, 4), (4, 8), (8, 11))
ACT_RING = 10


VEC = {}


def _vec_layout():
    at = 0
    for name, n in (
        ("attn_norm", 16), ("ffn_norm", 16), ("final_norm", 8), ("gate_norm", 1), ("lower", 8),
        ("c", 8), ("ada_b", 96), ("norm1", 16), ("norm2", 16), ("final2", 8), ("q_gain", 1), ("k_gain", 1),
        ("hy_cw", 72), ("hy_cb", 24), ("skip", 16), ("cw0", 264), ("cb0", 88), ("cw1", 132), ("cb1", 44),
        ("fb1", 1), ("fb2", 1), ("freq", 1),
    ):
        VEC[name] = (at, n)
        at += n
    return at


NVEC = _vec_layout()


def shape_constants():
    f32 = np.float32
    c = {}
    c["ident"] = np.eye(128, dtype=f32)
    s, t = np.meshgrid(np.arange(128), np.arange(128), indexing="ij")
    masks = []
    for n in range(7):
        b = 1 << n
        masks.append((s // (2 * b) == t // (2 * b)) & ((s // b) % 2 == 0) & ((t // b) % 2 == 1))
    c["masks"] = np.concatenate(masks, axis=1).astype(f32)
    c["cmin"] = np.where(t <= s, f32(3e38), f32(NEG)).astype(f32)
    c["cadd"] = np.where(t <= s, f32(0), f32(NEG)).astype(f32)
    dist = np.maximum(511 - np.arange(640), 0)
    nf = np.maximum(dist, 16).astype(f32)
    large = 16 + (np.log(nf / f32(16)) / f32(math.log(8.0)) * f32(16)).astype(np.int32)
    bucket = np.where(dist < 16, dist, np.minimum(large, 31))
    c["onehot"] = (np.arange(32)[:, None] == bucket[None, :]).astype(f32)
    n_freq = 16
    inv = (f32(1.0) / (f32(10000.0) ** (np.arange(n_freq, dtype=f32) / f32(n_freq)))).astype(f32)
    pos = np.arange(L)
    ang = np.concatenate([(pos // 64).astype(f32)[:, None] * inv, (pos % 64).astype(f32)[:, None] * inv], axis=1)
    pair = (np.arange(128) % 64) // 2
    c["cos"] = np.cos(ang).astype(f32)[:, pair].T
    c["sin"] = np.sin(ang).astype(f32)[:, pair].T
    perm = np.zeros((128, 128), f32)
    i = np.arange(0, 128, 2)
    perm[i + 1, i] = -1.0
    perm[i, i + 1] = 1.0
    c["perm"] = perm
    g = np.arange(128) // 64
    c["pairs"] = (g[:, None] == np.arange(2)[None, :]).astype(f32)
    order = np.concatenate([np.arange(0, L, 2), np.arange(1, L, 2)])
    tl = np.linspace(0.0, 1.0, L, dtype=f32)
    w = (f32(2.0 * math.pi) * np.arange(L, dtype=f32) / f32(L)).astype(f32)
    fr = np.linspace(1e-4, 15, 16, dtype=f32)
    a2 = (w[:, None] * fr[None, :]).astype(f32)
    z = np.concatenate([tl[:, None], np.cos(a2), -np.sin(a2)], axis=1).astype(f32)
    c["zT"] = z[order].T
    deltas = np.abs(np.linspace(math.log(1e-2) / 1.5, math.log(1e-2) / 0.3, D, dtype=f32))
    decay = np.exp(-tl[:, None] * deltas[None, :]).astype(f32)
    c["decay"] = decay[order].reshape(4, 128, D).transpose(1, 0, 2)
    om = 2 * np.pi * (np.arange(256) + 0.5) / 1024
    ev, od = np.arange(0, L, 2), np.arange(1, L, 2)
    fw = np.concatenate([np.cos(np.outer(ev, om)), np.cos(np.outer(od, om)),
                         np.sin(np.outer(ev, om)), np.sin(np.outer(od, om))], axis=1)
    c["fw"] = fw.astype(f32)
    iv = np.concatenate([np.cos(np.outer(om, ev)), np.cos(np.outer(om, od)),
                         np.sin(np.outer(om, ev)), np.sin(np.outer(om, od))], axis=1)
    c["iv"] = iv.astype(f32)
    return {k: np.ascontiguousarray(v, dtype=f32) for k, v in c.items()}


class Engine:

    def __init__(self, sem):
        self.sem, self.count, self.ops, self.seen = sem, 0, [], {}

    def wait(self, *marks):
        for m in marks:
            if m is None:
                continue
            if isinstance(m, list):
                self.wait(*m)
                continue
            sem, value = m
            if self.seen.get(sem, 0) < value:
                self.seen[sem] = value
                self.ops.append(lambda e, s=sem, v=value: e.wait_ge(s, v))

    def quiet(self, fn, *marks):
        self.wait(*marks)
        self.ops.append(fn)

    def run(self, fn, *marks):
        self.wait(*marks)
        self.count += 1
        self.ops.append(lambda e: fn(e).then_inc(self.sem, 1))
        return (self.sem, self.count)

    def dma(self, sem, total, out, in_, *marks):
        self.wait(*marks)
        self.ops.append(lambda e: e.dma_start(out, in_).then_inc(sem, 16))
        return (sem, total)

    def last(self):
        return (self.sem, self.count) if self.count else None


def stream_plan(A):
    items = []

    def cols(w, c0, n, k0=0, k1=None):
        v = w.rearrange("(k p) n -> p k n", p=128)
        return v[:, k0:(k1 if k1 is not None else v.shape[1]), c0:c0 + n]

    def w(name, *parts):
        placed, at = [], 0
        for p in parts:
            placed.append((p, at))
            at += p.shape[2]
        items.append(dict(kind="w", name=name, parts=placed, kt=parts[0].shape[1], n=at))

    def dense(name, wt):
        for j in range(4):
            w(name, cols(wt, 256 * j, 256))

    def ffn(up, down):
        for gi, (p0, p1) in enumerate(GROUPS):
            for p in range(p0, p1):
                w("gate", cols(up, 256 * p, 256))
                w("up", cols(up, DFF + 256 * p, 256))
                if gi and p == p0:
                    q0, q1 = GROUPS[gi - 1]
                    for j in range(4):
                        w("down", cols(down, 256 * j, 256, 2 * q0, 2 * q1))
        q0, q1 = GROUPS[-1]
        for j in range(4):
            w("down", cols(down, 256 * j, 256, 2 * q0, 2 * q1))

    hw = A["hgrn_w_in"][0]
    for j in range(4):
        w("i", cols(hw, 2048 + 256 * j, 256))
    for j in range(4):
        w("g", cols(hw, 3072 + 256 * j, 256))
    for h in range(8):
        w("fq", cols(hw, 1024 + 128 * h, 128), cols(hw, 128 * h, 128))
    dense("out", A["hgrn_w_out"][0])
    ffn(A["ffn_w_up"][0], A["ffn_w_down"][0])
    dw = A["dsa_w_in"][0]
    o = [0]
    for n in SPLITS:
        o.append(o[-1] + n)
    w("ix", cols(dw, o[3], 256))
    w("ix", cols(dw, o[3] + 256, 256))
    w("kw", cols(dw, o[4], 64), cols(dw, o[4], 64), cols(dw, o[5], 8))
    w("kk", cols(dw, o[1], 64), cols(dw, o[1], 64), cols(dw, o[1] + 64, 64), cols(dw, o[1] + 64, 64))
    w("v", cols(dw, o[2], 128))
    dense("q", dw[:, 0:1024])
    dense("out", A["dsa_w_out"][0])
    ffn(A["ffn_w_up"][1], A["ffn_w_down"][1])
    aw = A["attn_w_qkv_2"][0]
    for g in range(2):
        w("kk", *[cols(aw, 1024 + 64 * (2 * g + i // 2), 64) for i in range(4)])
    w("v", cols(aw, 1280, 256))
    dense("q", aw[:, 0:1024])
    dense("out", A["attn_w_o_2"][0])
    ffn(A["ffn_w_up_2"][0], A["ffn_w_down_2"][0])
    yw = A["hy_w_in_2"][0]
    for j in range(12):
        w("hy", cols(yw, 256 * j, 256))
    w("fw", cols(A["c_fw"], 0, 1024))
    w("iv", cols(A["c_iv"], 0, 1024))
    items.append(dict(kind="hold", name="hold"))
    for _ in range(3):
        items.append(dict(kind="rawhold", name="rawhold"))
    dense("out", A["hy_w_out_2"][0])
    ffn(A["ffn_w_up_2"][1], A["ffn_w_down_2"][1])
    return items


def build(nc, A, out, stop=99):
    ctx = ExitStack()
    with ctx:
        names = [0]

        def sb(shape, dt=F, stack=ctx):
            names[0] += 1
            return stack.enter_context(nc.sbuf_tensor(f"sb{names[0]}", list(shape), dt))

        def semaphore(name):
            return ctx.enter_context(nc.semaphore(name))

        PE, ACT, DVE, POOL, SP = (Engine(semaphore(f"s_{n}")) for n in ("pe", "act", "dve", "pool", "sp"))
        s_out = semaphore("s_out")
        ps = [ctx.enter_context(nc.psum_tensor(f"ps{b}", [128, 512], F)) for b in range(8)]
        pfree = [[] for _ in range(8)]

        x = sb([128, NT, L])
        hh, hl = sb([128, NT, L], R), sb([128, NT, L], R)
        raw = [sb([128, CW]) for _ in range(NRAW)]
        wh = [sb([128, CW], R) for _ in range(NW)]
        wl = [sb([128, CW], R) for _ in range(NW)]
        vec = sb([128, NVEC])
        ident, ones = sb([128, 128]), sb([128, 128])
        sq = [sb([128, L]) for _ in range(2)]
        rb = [sb([128, L]) for _ in range(2)]
        rc = [sb([128, 8]) for _ in range(2)]
        ht = [sb([128, L]) for _ in range(2)]
        eps = sb([128, 1])
        acc4 = sb([128, 1024])
        acc = [acc4[:, 256 * i:256 * i + 256] for i in range(4)]
        mod = sb([128, 96])
        cact = sb([128, 8])
        g1c = sb([128, 8])

        def v(name, i=0, n=1):
            a, m = VEC[name]
            assert i + n <= m
            return vec[:, a + i:a + i + n]

        def load(dst, src, *marks, eng=None):
            s = semaphore(f"ld{names[0]}_{len(loads)}")
            loads.append(s)
            return (eng or SP).dma(s, 16, dst, src, *marks)

        loads = []

        items = stream_plan(A)
        rsem = [semaphore(f"s_raw{i}") for i in range(NRAW)]
        rcount = [0] * NRAW
        rfree = [[] for _ in range(NRAW)]
        rheld = [False] * NRAW
        wfree = [[] for _ in range(NW)]
        wheld = [False] * NW
        nr = nw = 0
        for it in items:
            it["r"] = it["w"] = None
            if it["kind"] != "hold":
                it["r"] = nr % NRAW
                nr += 1
            if it["kind"] in ("w", "hold"):
                it["w"] = nw % NW
                nw += 1
        at = dict(issue=0, split=0, take=0)

        def pump():
            while True:
                moved = False
                if at["issue"] < len(items):
                    it = items[at["issue"]]
                    r = it["r"]
                    if r is None:
                        at["issue"] += 1
                        moved = True
                    elif not rheld[r]:
                        rheld[r] = True
                        it["raw_free"] = rfree[r]
                        for view, c0 in it.get("parts", ()):
                            kt, n = view.shape[1], view.shape[2]
                            dst = raw[r][:, 0:it["kt"] * it["n"]].rearrange("p (k n) -> p k n", n=it["n"])[:, :, c0:c0 + n]
                            rcount[r] += 16
                            it["landed"] = SP.dma(rsem[r], rcount[r], dst, view, it["raw_free"])
                        at["issue"] += 1
                        moved = True
                if at["split"] < at["issue"]:
                    it = items[at["split"]]
                    if it["kind"] == "rawhold":
                        at["split"] += 1
                        moved = True
                    elif not wheld[it["w"]]:
                        s = it["w"]
                        wheld[s] = True
                        it["free"] = wfree[s]
                        if it["kind"] == "w":
                            n = it["kt"] * it["n"]
                            r = it["r"]
                            hi = ACT.run(lambda e, s=s, r=r, n=n: e.activation(wh[s][:, 0:n], raw[r][:, 0:n], ACTF.Copy),
                                         it["landed"], wfree[s])
                            lo = POOL.run(lambda e, s=s, r=r, n=n: e.tensor_tensor(
                                wl[s][:, 0:n], raw[r][:, 0:n], wh[s][:, 0:n].bitcast(F), SUB), hi)
                            it["ready"] = [hi, lo]
                            rfree[r] = [hi, lo]
                            rheld[r] = False
                        at["split"] += 1
                        moved = True
                if not moved:
                    return

        def take(name):
            while True:
                it = items[at["take"]]
                assert it["name"] == name, (it["name"], name)
                at["take"] += 1
                assert at["split"] >= at["take"], name
                return it

        def release(it, *marks):
            if it["kind"] in ("w", "hold"):
                wfree[it["w"]] = list(marks)
                wheld[it["w"]] = False
            else:
                rfree[it["r"]] = list(marks)
                rheld[it["r"]] = False

        def w_views(it):
            n = it["kt"] * it["n"]
            s = it["w"]
            return [t[s][:, 0:n].rearrange("p (k n) -> p k n", n=it["n"]) for t in (wh, wl)]

        hready = [None] * NT
        hfree = [[] for _ in range(NT)]

        def product(o, pairs, first, last, **kw):
            for i, ((ah, al), (bh, bl)) in enumerate(pairs):
                f, l = first and i == 0, last and i == len(pairs) - 1
                PE.quiet(lambda e, o=o, a=al, b=bh, f=f: e.matmul(o, a, b, start=f, stop=False, **kw))
                PE.quiet(lambda e, o=o, a=ah, b=bl: e.matmul(o, a, b, start=False, stop=False, **kw))
                m = lambda e, o=o, a=ah, b=bh, l=l: e.matmul(o, a, b, start=False, stop=l, **kw)
                if i == len(pairs) - 1 and last:
                    return PE.run(m)
                PE.quiet(m)

        def project(it, banks, xh=None, xl=None, ready=None):
            a, b = w_views(it)
            xh = xh or (lambda k: hh[:, k, :])
            xl = xl or (lambda k: hl[:, k, :])
            ready = ready or (lambda k: hready[k])
            PE.wait(it["ready"])
            for bk in banks:
                PE.wait(pfree[bk])
            marks = []
            for k in range(it["kt"]):
                PE.wait(ready(k))
                for j, bk in enumerate(banks):
                    c = slice(128 * j, 128 * j + 128)
                    m = product(ps[bk][:, :], [((a[:, k, c], b[:, k, c]), (xh(k), xl(k)))],
                                k == 0, k == it["kt"] - 1)
                    marks.append(m)
            return [m for m in marks if m]

        def project_tokens(it, c0, n, o, tt):
            a, b = w_views(it)
            PE.wait(it["ready"])
            for k in range(NT):
                PE.wait(hready[k])
                c = slice(128 * tt, 128 * tt + 128)
                m = product(o, [((hh[:, k, c], hl[:, k, c]), (a[:, k, c0:c0 + n], b[:, k, c0:c0 + n]))],
                            k == 0, k == NT - 1)
            return m

        def mm(o, a, b, start=True, stop=True, **kw):
            return lambda e: e.matmul(o, a, b, start=start, stop=stop, **kw)

        def split(hi, lo, src, *marks, eng=None):
            a = ACT.run(lambda e: e.activation(hi, src, ACTF.Copy), *marks)
            b = (eng or DVE).run(lambda e: e.tensor_tensor(lo, src, hi.bitcast(F), SUB), a)
            return [a, b]

        xready = [None] * NT
        sqfree = [[], []]
        STAT = 7
        stat = {}

        def token_sums(bank, src, cols, first, last, *marks):
            n = cols.shape[1]
            PE.wait(*marks)
            for tt in range(4):
                f = mm(ps[bank][:, n * tt:n * tt + n], src[:, 128 * tt:128 * tt + 128], cols, first and tt == 0, last,
                       skip_group_check=True)
                if tt == 3:
                    return PE.run(f)
                PE.quiet(f)

        def square_sum(j):
            m = ACT.run(lambda e, j=j: e.activation(sq[j % 2][:, :], x[:, j, :], ACTF.Square), xready[j], sqfree[j % 2])
            if j == 0:
                PE.wait(pfree[STAT])
            p = token_sums(STAT, sq[j % 2], ones[:, 0:1], j == 0, j == NT - 1, m)
            sqfree[j % 2] = [p]
            stat["m"] = p

        rbfree = [[], []]
        rb_n = [0]

        def inverse_rms(bank, n, done, heads=1):
            i = rb_n[0] % 2
            rb_n[0] += 1
            w = 4 * heads
            a = ACT.run(lambda e: e.activation(rc[i][:, 0:w], ps[bank][:, 0:w], ACTF.Sqrt, bias=eps[:, 0:1], scale=1.0 / n), done)
            pfree[bank] = [a]
            m = DVE.run(lambda e: e.reciprocal(rc[i][:, 0:w], rc[i][:, 0:w]), a)
            wide = rb[i][:, :].rearrange("p (c f) -> p c f", c=w)
            m = DVE.run(lambda e: e.tensor_copy(wide, rc[i][:, 0:w].unsqueeze(2).broadcast_to([128, w, 128 // heads])), m, rbfree[i])
            return i, m

        def spread_rms(bank, im):
            i, m = im
            PE.wait(m, pfree[bank])
            for tt in range(4):
                f = mm(ps[bank][:, 128 * tt:128 * tt + 128], rb[i][:, 128 * tt:128 * tt + 128], ident[:, :], skip_group_check=True)
                if tt < 3:
                    PE.quiet(f)
            p = PE.run(f)
            rbfree[i] = [p]
            return p

        htfree = [[], []]

        def normalise(gain, shift=None):
            r = spread_rms(STAT, inverse_rms(STAT, D, stat["m"]))
            for j in range(NT):
                t = ht[j % 2]
                m = DVE.run(lambda e, j=j, t=t: e.scalar_tensor_tensor(t[:, :], x[:, j, :], gain(j), ps[STAT][:, :], MUL, MUL),
                            r, xready[j], htfree[j % 2])
                pfree[STAT] = [m]
                if shift is not None:
                    m = DVE.run(lambda e, j=j, t=t: e.tensor_scalar(t[:, :], t[:, :], shift(j), None, ADD), m)
                hready[j] = split(hh[:, j, :], hl[:, j, :], t[:, :], m, hfree[j])
                htfree[j % 2] = hready[j]

        def add_residual(it, scale=None, stats=True, **kw):
            for j0 in range(0, NT, 2):
                if j0:
                    it = take(it["name"])
                banks = (4, 5) if (j0 // 2) % 2 else (2, 3)
                if kw.get("banks"):
                    banks = kw["banks"][(j0 // 2) % 2]
                done = project(it, banks, **kw.get("rhs", {}))
                release(it, done[-1])
                for i in range(2):
                    j = j0 + i
                    b = banks[i]
                    if scale is None:
                        xready[j] = DVE.run(lambda e, j=j, b=b: e.tensor_tensor(x[:, j, :], x[:, j, :], ps[b][:, :], ADD),
                                            done[i], xready[j])
                    else:
                        xready[j] = DVE.run(lambda e, j=j, b=b: e.scalar_tensor_tensor(
                            x[:, j, :], ps[b][:, :], scale(j), x[:, j, :], MUL, ADD), done[i], xready[j])
                    pfree[b] = [xready[j]]
                if stats:
                    for i in range(2):
                        square_sum(j0 + i)
                pump()
            return done[-1]

        stores = []

        def fence():
            return [e.last() for e in (PE, ACT, DVE, POOL)] + stores

        m_ones = POOL.run(lambda e: e.memset(ones[:, :], 1.0))
        m_eps = POOL.run(lambda e: e.memset(eps[:, :], EPS))
        st = ExitStack()
        xt = sb([128, 4, D], stack=st)
        oh, relb, bv = sb([32, 640], stack=st), sb([32, 16], stack=st), sb([16, 640], stack=st)
        m_oh = load(oh[:, :], A["c_onehot"], eng=ACT)
        m_rb = load(relb[:, :], A["rel_bias"], eng=ACT)
        m_vec = load(vec[:, :], A["vec"], eng=ACT)
        m_id = load(ident[:, :], A["c_ident"])
        m_xt = [load(xt[:, t, :], A["x"][0].rearrange("(t p) d -> p t d", p=128)[:, t, :]) for t in range(4)]
        pump()

        scratch = nc.dram_tensor("bias_by_distance", (16, 128, 640), F, kind="Internal")
        m_bv = []
        for i in range(2):
            b = 5 + i
            m = PE.run(mm(ps[b][0:16, 0:320], relb[:, :], oh[:, 320 * i:320 * i + 320]), m_oh, m_rb, pfree[b])
            m_bv.append(DVE.run(lambda e, b=b, i=i: e.tensor_copy(bv[:, 320 * i:320 * i + 320], ps[b][0:16, 0:320]), m))
            pfree[b] = [m_bv[-1]]
        m_scratch = load(scratch.ap(), bv[:, :].unsqueeze(1).broadcast_to([16, 128, 640]), m_bv)
        stores.append(m_scratch)

        ACT.wait(m_eps, m_vec)
        PE.wait(m_ones)
        DVE.wait(m_vec)
        PE.wait(m_id)
        for j in range(NT + 2):
            if j >= 2:
                square_sum(j - 2)
            if j == NT or j == NT + 1:
                continue
            b = j % 4
            PE.wait(pfree[b])
            for t in range(4):
                fn = lambda e, b=b, t=t, j=j: e.transpose(ps[b][:, 128 * t:128 * t + 128], xt[:, t, 128 * j:128 * j + 128], ident[:, :])
                PE.wait(m_xt[t])
                if t < 3:
                    PE.quiet(fn)
                else:
                    m = PE.run(fn)
            xready[j] = DVE.run(lambda e, b=b, j=j: e.tensor_copy(x[:, j, :], ps[b][:, :]), m)
            pfree[b] = [xready[j]]
        st.close()

        lbt = sb([128, 4, 8])

        def hgrn():
            st = ExitStack()
            begin = [fence(), m_scratch]
            NE = 4
            I = sb([128, 4, D], stack=st)
            M = sb([128, 8, L], stack=st)
            E = [sb([128, L], stack=st) for _ in range(NE)]
            Q, K, P, X = ([sb([128, L], stack=st) for _ in range(2)] for _ in range(4))
            S = [sb([128, L], stack=st) for _ in range(2)]
            SO = sb([128, 768], stack=st)
            masks = sb([128, 896], stack=st)
            m_masks = load(masks[:, :], A["c_masks"], *begin)

            m = DVE.run(lambda e: e.tensor_tensor(lbt[:, 0, :], v("lower", 0, 8), v("lower", 0, 8), SUB))
            m = ACT.run(lambda e: e.activation(lbt[:, 1, :], lbt[:, 0, :], ACTF.Exp), m)
            m = DVE.run(lambda e: e.reciprocal(lbt[:, 0, :], lbt[:, 1, :]), m)
            m = DVE.run(lambda e: e.tensor_tensor(lbt[:, 1, :], lbt[:, 1, :], lbt[:, 0, :], MUL), m)
            m = DVE.run(lambda e: e.tensor_tensor(lbt[:, 2, :], lbt[:, 1, :], lbt[:, 1, :], SUB), m)
            m_lb = DVE.run(lambda e: e.tensor_scalar(lbt[:, 3, :], lbt[:, 2, :], -1.0, 1.0, MUL, ADD), m)

            i_ready = []
            for c in range(4):
                it = take("i")
                for tt in range(4):
                    b = tt
                    PE.wait(pfree[b])
                    m = project_tokens(it, 0, 256, ps[b][:, 0:256], tt)
                    if tt == 3:
                        release(it, m)
                    m = ACT.run(lambda e, b=b, tt=tt, c=c: e.copy(I[:, tt, 256 * c:256 * c + 256], ps[b][:, 0:256]), m, *begin)
                    pfree[b] = [m]
                    i_ready.append(m)
                pump()
            sg_ready = []
            for c in range(4):
                it = take("g")
                banks = (0, 1) if c % 2 else (2, 3)
                done = project(it, banks)
                release(it, done[-1])
                for i in range(2):
                    j, b = 2 * c + i, banks[i]
                    m = ACT.run(lambda e, j=j, b=b: e.activation(M[:, j, :], ps[b][:, :], ACTF.Sigmoid), done[i], *begin)
                    m = DVE.run(lambda e, j=j, b=b: e.tensor_tensor(M[:, j, :], M[:, j, :], ps[b][:, :], MUL), m)
                    pfree[b] = [m]
                    sg_ready.append(m)
                pump()

            LEVEL_BANKS = (2, 4, 5, 6)
            OB, HB = 3, 7
            nlevel, nslot = [0], [0]
            efree = [[] for _ in range(NE)]
            qk_free, px_free, s_free, so_free = [[], []], [[], []], [[], []], []
            kw = dict(skip_group_check=True)

            def project_head(h):
                it = take("fq")
                done = project(it, (0, 1))
                release(it, done[-1])
                return done

            def halves(t, n):
                return t[:, :].rearrange("p (m two b) -> p m two b", two=2, b=1 << n)

            def head_inputs(h, done):
                i = h % 2
                f = ACT.run(lambda e: e.activation(P[i][:, :], ps[0][:, :], ACTF.Sigmoid), done[0], px_free[i], *begin)
                k = ACT.run(lambda e: e.activation(K[i][:, :], ps[0][:, :], ACTF.Sigmoid, scale=-1.0), qk_free[i])
                q = ACT.run(lambda e: e.copy(Q[i][:, :], ps[1][:, :]), done[1])
                pfree[0], pfree[1] = [k], [q]
                return dict(h=h, f=f, k=k, q=q)

            def prepare(g):
                h, i = g["h"], g["h"] % 2
                g["x"] = POOL.run(lambda e: e.memset(X[i][:, :], 1.0), px_free[i], *begin)
                a = DVE.run(lambda e: e.tensor_scalar(P[i][:, :], P[i][:, :], lbt[:, 3, h:h + 1], lbt[:, 2, h:h + 1], MUL, ADD), g["f"], m_lb)
                g["k"] = DVE.run(lambda e: e.tensor_scalar(K[i][:, :], K[i][:, :], lbt[:, 3, h:h + 1], None, MUL), g["k"])
                g["p"] = DVE.run(lambda e: e.tensor_scalar(P[i][:, :], P[i][:, :], TINY, None, ALU.max), a)

            def level(g, n):
                i = g["h"] % 2
                s = nslot[0] % NE
                nslot[0] += 1
                Ev, Qv, Kv, Pv, Xv = (halves(t, n) for t in (E[s], Q[i], K[i], P[i], X[i]))
                a = DVE.run(lambda e: e.tensor_tensor(Ev[:, :, 1, :], Qv[:, :, 1, :], Pv[:, :, 1, :], MUL), g["q"], g["p"], efree[s])
                b = DVE.run(lambda e: e.tensor_tensor(Ev[:, :, 0, :], Kv[:, :, 0, :], Xv[:, :, 0, :], MUL), g["k"], g["x"])
                if n < 8:
                    bl, nb = 1 << n, 256 >> n
                    g["x"] = POOL.run(lambda e: e.tensor_tensor(
                        Xv[:, :, 0, :], Xv[:, :, 0, :], Pv[:, :, 1, bl - 1:bl].broadcast_to([128, nb, bl]), MUL), g["p"], b)
                    g["p"] = POOL.run(lambda e: e.tensor_tensor(
                        Pv[:, :, 1, :], Pv[:, :, 1, :], Pv[:, :, 0, bl - 1:bl].broadcast_to([128, nb, bl]), MUL), a, g["x"])
                else:
                    px_free[i] = [b]
                return s, b

            def level_scores(g, n, sm):
                i = g["h"] % 2
                bk = LEVEL_BANKS[nlevel[0] % 4]
                nlevel[0] += 1
                PE.wait(pfree[bk])
                if n is None:
                    PE.wait(g["q"], g["k"])
                    a_, b_ = K[i], Q[i]
                else:
                    s, m = sm
                    PE.wait(m)
                    a_ = b_ = E[s]
                if n == 8:
                    fs = [mm(ps[bk][:, 256 * t:256 * t + 256], a_[:, 128 * t:128 * t + 128], b_[:, 256:512]) for t in range(2)]
                elif n == 7:
                    fs = [mm(ps[bk][:, 128 * t:128 * t + 128], a_[:, 256 * t:256 * t + 128], b_[:, 256 * t + 128:256 * t + 256]) for t in range(2)]
                else:
                    fs = [mm(ps[bk][:, 128 * t:128 * t + 128], a_[:, 128 * t:128 * t + 128], b_[:, 128 * t:128 * t + 128]) for t in range(4)]
                for f in fs[:-1]:
                    PE.quiet(f)
                p = PE.run(fs[-1])
                if n is None:
                    qk_free[i] = [p, g["last"]]
                else:
                    efree[s] = [p]
                return bk, p

            def collect(g, n, bk, p):
                i = g["h"] % 2
                if n == 8:
                    m = ACT.run(lambda e: e.copy(SO[:, 0:512], ps[bk][:, :]), p, so_free, *begin)
                    g["far"].append(m)
                elif n == 7:
                    m = ACT.run(lambda e: e.copy(SO[:, 512:768], ps[bk][:, 0:256]), p, so_free, *begin)
                    g["far"].append(m)
                else:
                    mask = (ident[:, :] if n is None else masks[:, 128 * n:128 * n + 128]).unsqueeze(1).broadcast_to([128, 4, 128])
                    o = S[i][:, :].rearrange("p (t q) -> p t q", t=4)
                    src = ps[bk][:, :].rearrange("p (t q) -> p t q", t=4)
                    if n == 0:
                        m = DVE.run(lambda e: e.tensor_tensor(o, src, mask, MUL), p, s_free[i], m_masks)
                    else:
                        m = DVE.run(lambda e: e.copy_predicated(o, mask.bitcast(mybir.dt.uint32), src), p, g["near"])
                    g["near"] = m
                pfree[bk] = [m]

            def values(g):
                h = g["h"]
                i = h % 2
                hc = slice(128 * h, 128 * h + 128)
                PE.wait(pfree[OB], i_ready, g["far"])
                for s in range(2):
                    PE.quiet(mm(ps[OB][:, 256:512], I[:, s, hc], SO[:, 256 * s:256 * s + 256], s == 0, False, **kw))
                PE.quiet(mm(ps[OB][:, 128:256], I[:, 0, hc], SO[:, 512:640], False, False, **kw))
                so_free[:] = [PE.run(mm(ps[OB][:, 384:512], I[:, 2, hc], SO[:, 640:768], False, False, **kw))]
                PE.wait(g["near"])
                for tt in range(4):
                    c = slice(128 * tt, 128 * tt + 128)
                    f = mm(ps[OB][:, c], I[:, tt, hc], S[i][:, c], False, tt == 3, **kw)
                    if tt < 3:
                        PE.quiet(f)
                p = PE.run(f)
                s_free[i] = [p]
                s2 = ACT.run(lambda e: e.activation(sq[i][:, :], ps[OB][:, :], ACTF.Square), p, sqfree[i])
                og = ACT.run(lambda e: e.activation(ht[i][:, :], ps[OB][:, :], ACTF.Copy, scale=v("gate_norm")), htfree[i])
                pfree[OB] = [og]
                g["sq"], g["og"] = s2, og

            def head_sums(g):
                i = g["h"] % 2
                PE.wait(pfree[HB])
                p = token_sums(HB, sq[i], ones[:, 0:1], True, True, g["sq"])
                sqfree[i] = [p]
                g["im"] = inverse_rms(HB, 128, p)

            def head_output(g):
                h, i = g["h"], g["h"] % 2
                r = spread_rms(HB, g["im"])
                m = DVE.run(lambda e: e.tensor_tensor(M[:, h, :], M[:, h, :], ht[i][:, :], MUL), g["og"], sg_ready[h])
                htfree[i] = [m]
                m = DVE.run(lambda e: e.tensor_tensor(M[:, h, :], M[:, h, :], ps[HB][:, :], MUL), m, r)
                pfree[HB] = [m]
                m_ready.append(m)

            m_ready = []
            done = project_head(0)
            g = head_inputs(0, done)
            pump()
            prev = None
            ORDER = [0, 1, 2, 3, 4, 5, 6, None, 7, 8]
            for h in range(8):
                g["far"], g["near"] = [], None
                prepare(g)
                if h < 7:
                    done = project_head(h + 1)
                if prev:
                    head_sums(prev)
                made = {}
                LAG = 2
                queue = []
                for i, n in enumerate(ORDER):
                    if n is not None:
                        made[n] = level(g, n)
                        g["last"] = made[n][1]
                    bk, p = level_scores(g, n, made.get(n))
                    queue.append((n, bk, p))
                    if len(queue) > LAG:
                        collect(g, *queue.pop(0))
                for c in queue:
                    collect(g, *c)
                if prev:
                    head_output(prev)
                if h < 7:
                    nxt = head_inputs(h + 1, done)
                values(g)
                pump()
                prev = g
                g = nxt
            head_sums(prev)
            head_output(prev)
            last = PE.last()
            for j in range(NT):
                hready[j] = split(hh[:, j, :], hl[:, j, :], M[:, j, :], m_ready[j], last, eng=POOL if j % 2 else DVE)
            it = take("out")
            done = add_residual(it)
            for j in range(NT):
                hfree[j] = [done]
            st.close()

        ADA = [(l, j, half) for l in range(2) for j in range(24) for half in range(2)]
        NADA = 3
        s_ada = [semaphore(f"s_ada{i}") for i in range(NADA)]
        ada_at = dict(load=0, use=0, limit=0)
        ada_land, ada_free = {}, [[] for _ in range(NADA)]
        accfree = [[] for _ in acc]

        def ada_load(slots):
            n = ada_at["load"]
            if n == ada_at["limit"] or n - ada_at["use"] >= NADA:
                return
            ada_at["load"] += 1
            l, j, half = ADA[n]
            s = n % NADA
            view = A["ada_w_2"][l].rearrange("(k p) n -> p k n", p=128)[:, 4 * half:4 * half + 4, 256 * j:256 * j + 256]
            ada_land[n] = ACT.dma(s_ada[s], 16 * (n // NADA + 1), slots[s][:, :].rearrange("p (k n) -> p k n", n=256), view, ada_free[s])

        def ada_step(slots):
            n = ada_at["use"]
            if n == ada_at["load"]:
                return
            ada_at["use"] += 1
            l, j, half = ADA[n]
            a = acc[j % 4]
            w = slots[n % NADA][:, :].rearrange("p (k n) -> p k n", n=256)
            m = None
            for i in range(4):
                k = 4 * half + i
                if k == 0:
                    m = DVE.run(lambda e: e.tensor_scalar(a[:, :], w[:, 0, :], cact[:, 0:1], None, MUL), ada_land[n], accfree[j % 4], m_cact)
                else:
                    m = DVE.run(lambda e, k=k, i=i: e.scalar_tensor_tensor(a[:, :], w[:, i, :], cact[:, k:k + 1], a[:, :], MUL, ADD),
                                ada_land[n], m or ada_last[0])
            ada_last[0] = m
            ada_free[n % NADA] = [m]
            if half:
                ada_sum.append((l, j, m))

        def ada_finish():
            while ada_sum:
                l, j, m = ada_sum.pop(0)
                c = 48 * l + 2 * j
                a = acc[j % 4]
                PE.wait(pfree[6], m)
                PE.quiet(mm(ps[6][:, c:c + 1], a[:, 0:128], ones[:, 0:1], skip_group_check=True))
                p = PE.run(mm(ps[6][:, c + 1:c + 2], a[:, 128:256], ones[:, 0:1], skip_group_check=True))
                accfree[j % 4] = [p]

        def ada_collect(l):
            c = slice(48 * l, 48 * l + 48)
            m = DVE.run(lambda e: e.tensor_tensor(mod[:, c], ps[6][:, c], v("ada_b", 48 * l, 48), ADD), PE.last())
            pfree[6] = [m]
            ada_done.append(m)

        ada_last, ada_sum = [None], []
        ada_done = []
        m_cact = ACT.run(lambda e: e.activation(cact[:, :], v("c", 0, 8), ACTF.Silu))

        def ffn(convs, offset, scale=None, spare=False):
            st = ExitStack()
            begin = fence()
            ah, al = sb([128, ACT_RING, L], R, st), sb([128, ACT_RING, L], R, st)
            yg, yu, sg = ([sb([128, L], stack=st) for _ in range(2)] for _ in range(3))
            a_ready, a_free = {}, [[] for _ in range(ACT_RING)]
            tfree = [[begin], [begin]]
            slots = []
            if spare:
                ada_at["limit"] += len(ADA) // 2
                slots += [sb([128, 1024], stack=st) for _ in range(NADA)]
                for i in range(NADA):
                    ada_free[i] = [begin]
                    ada_load(slots)

            def conv(cv, tile, b, done, dst, *free):
                wt, bias = cv
                m = ACT.run(lambda e: e.activation(dst[:, :], ps[b][:, :], ACTF.Identity, bias=bias(tile), scale=wt(offset, tile)), done, *free)
                for tap in range(3):
                    sh = tap - offset
                    if sh < 0:
                        o, i = dst[:, -sh:L], ps[b][:, 0:L + sh]
                    elif sh > 0:
                        o, i = dst[:, 0:L - sh], ps[b][:, sh:L]
                    else:
                        continue
                    m = DVE.run(lambda e, o=o, i=i, tap=tap: e.scalar_tensor_tensor(o, i, wt(tap, tile), o, MUL, ADD), m)
                return m

            def ada_steps(count):
                for _ in range(count if spare else 0):
                    ada_step(slots)
                    ada_load(slots)

            def up_pair(p):
                it = take("gate")
                dg = project(it, (0, 1))
                release(it, dg[-1])
                g = []
                for i in range(2):
                    t = 2 * p + i
                    m = conv(convs[0], t, i, dg[i], yg[i], tfree[i])
                    pfree[i] = [m]
                    g.append(ACT.run(lambda e, i=i: e.activation(sg[i][:, :], yg[i][:, :], ACTF.Silu), m, tfree[i]))
                pump()
                ada_steps(2)
                it = take("up")
                du = project(it, (2, 3))
                release(it, du[-1])
                for i in range(2):
                    t = 2 * p + i
                    b = 2 + i
                    if convs[1] is not None:
                        m = conv(convs[1], t, b, du[i], yu[i], tfree[i])
                        pfree[b] = [m]
                        m = DVE.run(lambda e, i=i: e.tensor_tensor(yu[i][:, :], sg[i][:, :], yu[i][:, :], MUL), m, g[i], tfree[i])
                    else:
                        m = DVE.run(lambda e, i=i, b=b: e.tensor_tensor(yu[i][:, :], sg[i][:, :], ps[b][:, :], MUL), du[i], g[i], tfree[i])
                        pfree[b] = [m]
                    s = t % ACT_RING
                    a_ready[t] = split(ah[:, s, :], al[:, s, :], yu[i][:, :], m, a_free[s], begin, eng=POOL)
                    tfree[i] = [m] + a_ready[t]
                pump()

            def down(gi):
                q0, q1 = GROUPS[gi]
                t0 = 2 * q0
                rhs = dict(xh=lambda k: ah[:, (t0 + k) % ACT_RING, :], xl=lambda k: al[:, (t0 + k) % ACT_RING, :],
                           ready=lambda k: a_ready[t0 + k])
                it = take("down")
                done = add_residual(it, scale, stats=gi == len(GROUPS) - 1, rhs=rhs, banks=((4, 5), (4, 5)))
                for t in range(t0, 2 * q1):
                    a_free[t % ACT_RING] = [done]

            for gi, (p0, p1) in enumerate(GROUPS):
                for p in range(p0, p1):
                    up_pair(p)
                    if spare:
                        ada_finish()
                    ada_steps(3)
                    if gi and p == p0:
                        down(gi - 1)
            last = PE.last()
            for j in range(NT):
                hfree[j] = [last]
            if spare:
                while ada_at["use"] < ada_at["load"]:
                    ada_step(slots)
            down(len(GROUPS) - 1)
            if spare:
                ada_finish()
                ada_collect(ada_at["limit"] // (len(ADA) // 2) - 1)
            st.close()

        def ffn1(layer):
            def wt(tap, tile):
                return v("cw0", 132 * layer + 44 * tap + tile)

            def bias(tile):
                return v("cb0", 44 * layer + tile)

            normalise(lambda j: v("ffn_norm", 8 * layer + j))
            ffn([(wt, bias), (lambda tap, tile: wt(tap, AF + tile), lambda tile: bias(AF + tile))], 2, spare=True)

        def ffn2(layer):
            def wt(tap, tile):
                return v("cw1", 66 * layer + 22 * tap + tile)

            m = modulated(layer, "norm2", 3)
            ffn([(wt, lambda tile: v("cb1", 22 * layer + tile)), None], 1, scale=m)

        def modulated(layer, gain, first):
            base = 48 * layer + 8 * first
            m = DVE.run(lambda e: e.tensor_scalar(g1c[:, :], mod[:, base + 8:base + 16], 1.0, None, ADD), ada_done)
            m = DVE.run(lambda e: e.tensor_tensor(g1c[:, :], g1c[:, :], v(gain, 8 * layer, 8), MUL), m)
            DVE.wait(m)
            normalise(lambda j: g1c[:, j:j + 1], lambda j: mod[:, base + j:base + j + 1])
            return lambda j: mod[:, base + 16 + j:base + 17 + j]

        def attend(units, logits, soften, value, o_of, finish, pool):
            P, PT, mx, nm, sm, rs = pool
            pf, ptf = [[] for _ in P], [[] for _ in PT]
            LB, TB = (0, 1, 2), (3, 4)
            info = {}

            def first(u):
                b = LB[u % 3]
                PE.wait(pfree[b])
                m = logits(units[u], b)
                k = u % len(P)
                c = slice(u % 8, u % 8 + 1)
                e = soften(units[u], b, m, P[k], mx[:, c], nm[:, c], sm[:, c], pf[k])
                S = units[u][2]
                r = DVE.run(lambda e_: e_.reciprocal(rs[:, c], sm[:, c]), e)
                n = POOL.run(lambda e_: e_.tensor_scalar(P[k][:, 0:S], P[k][:, 0:S], rs[:, c], 1.0, MUL, MUL), r, e)
                info[u] = n

            def second(u):
                k, S, b = u % len(P), units[u][2], TB[u % 2]
                PE.wait(pfree[b], info[u])
                for s in range(S // 128):
                    f = lambda e, s=s: e.transpose(ps[b][:, 128 * s:128 * s + 128], P[k][:, 128 * s:128 * s + 128], ident[:, :])
                    if s < S // 128 - 1:
                        PE.quiet(f)
                m = PE.run(f)
                pf[k] = [m]
                q = u % len(PT)
                a = ACT.run(lambda e: e.copy(PT[q][:, 0:S], ps[b][:, 0:S]), m, ptf[q])
                pfree[b] = [a]
                info[u] = a

            def third(u):
                q, S = u % len(PT), units[u][2]
                o = o_of(units[u])
                PE.wait(info[u])
                n = S // 128
                for s in range(n):
                    f = mm(o, value(units[u], s), PT[q][:, 128 * s:128 * s + 128], s == 0, s == n - 1, skip_group_check=True)
                    if s < n - 1:
                        PE.quiet(f)
                m = PE.run(f)
                ptf[q] = [m]
                finish(u, units[u], m)

            n = len(units)
            for i in range(n + 4):
                if i < n:
                    first(i)
                if 0 <= i - 2 < n:
                    second(i - 2)
                if 0 <= i - 3 < n:
                    third(i - 3)

        def softmax_pool(st):
            return ([sb([128, L], stack=st) for _ in range(3)], [sb([128, L], stack=st) for _ in range(2)],
                    *(sb([128, 8], stack=st) for _ in range(4)))

        OBANK = (5, 6)

        def finish_heads(u, unit, m):
            h, tt, S = unit
            if h % 2 == 1 and tt == 3:
                j, b = h // 2, OBANK[(h // 2) % 2]
                hi = ACT.run(lambda e: e.activation(hh[:, j, :], ps[b][:, :], ACTF.Copy), m, hfree[j])
                lo = DVE.run(lambda e: e.tensor_tensor(hl[:, j, :], ps[b][:, :], hh[:, j, :].bitcast(F), SUB), hi)
                hready[j] = [hi, lo]
                pfree[b] = [hi, lo]

        def o_region(unit):
            h, tt, S = unit
            b = OBANK[(h // 2) % 2]
            if h % 2 == 0 and tt == 0:
                PE.wait(pfree[b])
            return ps[b][64 * (h % 2):64 * (h % 2) + 64, 128 * tt:128 * tt + 128]

        def dsa():
            st = ExitStack()
            begin = fence()
            q = sb([128, 8, L], stack=st)
            k2 = sb([128, 2, L], stack=st)
            V = sb([128, 4, 128], stack=st)
            qi = sb([128, 4, L], stack=st)
            ki = sb([128, L], stack=st)
            wi = sb([128, 4, 8], stack=st)
            work = sb([128, 1280], stack=st)
            relu = [sb([128, L], stack=st) for _ in range(2)]
            T = [sb([128, L], stack=st) for _ in range(4)]
            Lg = [sb([128, L], stack=st) for _ in range(2)]
            cmin, cadd = sb([128, 128], stack=st), sb([128, 128], stack=st)
            m8 = sb([128, 8], stack=st)
            pool = softmax_pool(st)
            m_c = [load(cmin[:, :], A["c_cmin"], begin), load(cadd[:, :], A["c_cadd"], begin)]
            sel = [work[:, 128 * (tt * (tt + 1) // 2):128 * (tt * (tt + 1) // 2) + 128 * (tt + 1)] for tt in range(4)]
            Tsem = [semaphore(f"s_T{i}") for i in range(4)]
            Tfree = [[] for _ in range(4)]
            Tland = {}

            def load_bias(h):
                s = h % 4
                src = bass.AP(tensor=scratch, offset=128 * 640 * h + 127, ap=[[639, 128], [1, 512]])
                Tland[h] = ACT.dma(Tsem[s], 16 * (h // 4 + 1), T[s][:, :], src, Tfree[s], begin, m_scratch)

            for h in range(3):
                load_bias(h)

            qi_ready = []
            for c in range(2):
                it = take("ix")
                banks = (0, 1) if c else (2, 3)
                done = project(it, banks)
                release(it, done[-1])
                for i in range(2):
                    j, b = 2 * c + i, banks[i]
                    m = ACT.run(lambda e, j=j, b=b: e.copy(qi[:, j, :], ps[b][:, :]), done[i], begin)
                    pfree[b] = [m]
                    qi_ready.append(m)
                pump()
            it = take("kw")
            done = project(it, (4,))
            m_ki = ACT.run(lambda e: e.copy(ki[:, :], ps[4][:, :]), done[0], begin)
            pfree[4] = [m_ki]
            PE.wait(pfree[5])
            for tt in range(4):
                m = project_tokens(it, 128, 8, ps[5][:, 8 * tt:8 * tt + 8], tt)
            release(it, m)
            m_wi = DVE.run(lambda e: e.tensor_scalar(wi[:, :, :].rearrange("p a b -> p (a b)"), ps[5][:, 0:32],
                                                     float(8 ** -0.5 * 64 ** -0.5), None, MUL), m, begin)
            pfree[5] = [m_wi]
            pump()
            rl = [[], []]
            n = 0
            m_sc = [None] * 4
            for tt in range(1, 4):
                S = 128 * (tt + 1)
                for h in range(8):
                    b = (4, 5, 6)[n % 3]
                    pr = slice(64 * (h % 2), 64 * (h % 2) + 64)
                    m = PE.run(mm(ps[b][:, 0:S], qi[pr, h // 2, 128 * tt:128 * tt + 128], ki[pr, 0:S]), qi_ready, m_ki, pfree[b])
                    s = n % 2
                    m = ACT.run(lambda e, b=b, s=s, S=S: e.activation(relu[s][:, 0:S], ps[b][:, 0:S], ACTF.Relu), m, rl[s], begin)
                    pfree[b] = [m]
                    o = sel[tt]
                    if h == 0:
                        m = DVE.run(lambda e, o=o, s=s, S=S, tt=tt, h=h: e.tensor_scalar(
                            o, relu[s][:, 0:S], wi[:, tt, h:h + 1], 0.0, MUL, ADD), m, m_wi)
                    else:
                        m = DVE.run(lambda e, o=o, s=s, S=S, tt=tt, h=h: e.scalar_tensor_tensor(
                            o, relu[s][:, 0:S], wi[:, tt, h:h + 1], o, MUL, ADD), m, m_sc[tt])
                    rl[s] = [m]
                    m_sc[tt] = m
                    n += 1
            m_sel = [DVE.run(lambda e: e.tensor_copy(sel[0], cadd[:, :]), m_c, begin)]
            m8m = None
            for tt in range(1, 4):
                o = sel[tt]
                m = DVE.run(lambda e, o=o, tt=tt: e.tensor_tensor(o[:, 128 * tt:128 * tt + 128], o[:, 128 * tt:128 * tt + 128],
                                                                cmin[:, :], ALU.min), m_sc[tt])
                for _ in range(TOPK // 8):
                    a = DVE.run(lambda e, o=o: e.max(m8[:, :], o), m)
                    m = DVE.run(lambda e, o=o: e.match_replace(o, m8[:, :], o, GONE), a)
                m = DVE.run(lambda e, o=o: e.tensor_scalar(o, o, GONE, NEG, ALU.is_gt, MUL), m)
                m_sel.append(m)
            it = take("kk")
            done = project(it, (0, 1))
            release(it, done[-1])
            m_k = []
            for i in range(2):
                m_k.append(ACT.run(lambda e, i=i: e.copy(k2[:, i, :], ps[i][:, :]), done[i], begin))
                pfree[i] = [m_k[-1]]
            pump()
            it = take("v")
            PE.wait(pfree[2])
            for tt in range(4):
                m = project_tokens(it, 0, 128, ps[2][:, 128 * tt:128 * tt + 128], tt)
            release(it, m)
            m_v = ACT.run(lambda e: e.copy(V[:, :, :].rearrange("p a b -> p (a b)"), ps[2][:, :]), m, begin)
            pfree[2] = [m_v]
            pump()
            m_q = []
            for c in range(4):
                it = take("q")
                banks = (0, 1) if c % 2 else (2, 3)
                done = project(it, banks)
                release(it, done[-1])
                for i in range(2):
                    j, b = 2 * c + i, banks[i]
                    m = ACT.run(lambda e, j=j, b=b: e.copy(q[:, j, :], ps[b][:, :]), done[i], begin)
                    pfree[b] = [m]
                    m_q.append(m)
                pump()
            for j in range(NT):
                hfree[j] = [done[-1]]
            lgf = [[], []]
            nun = [0]

            def logits(unit, b):
                h, tt, S = unit
                pr = slice(64 * (h % 2), 64 * (h % 2) + 64)
                return PE.run(mm(ps[b][:, 0:S], q[pr, h // 2, 128 * tt:128 * tt + 128], k2[pr, h // 8, 0:S]), m_q[h // 2], m_k)

            def soften(unit, b, m, P, mx, nm, sm, free):
                h, tt, S = unit
                if tt == 0 and h + 3 < 16:
                    load_bias(h + 3)
                s = nun[0] % 2
                nun[0] += 1
                lg = Lg[s][:, 0:S]
                Tv = T[h % 4][:, 384 - 128 * tt:512]
                m = DVE.run(lambda e: e.scalar_tensor_tensor(lg, ps[b][:, 0:S], 0.125, Tv, MUL, ADD), m, Tland[h], lgf[s])
                pfree[b] = [m]
                if tt == 3:
                    Tfree[h % 4] = [m]
                m = DVE.run(lambda e: e.tensor_tensor_reduce(lg, lg, sel[tt], 1.0, -3e38, ADD, ALU.max, mx), m, m_sel[tt])
                m2 = DVE.run(lambda e: e.tensor_scalar(nm, mx, -1.0, None, MUL), m)
                a = ACT.run(lambda e: e.activation(P[:, 0:S], lg, ACTF.Exp, bias=nm, scale=1.0, accum_out=sm), m2, free)
                lgf[s] = [a]
                return a

            def value(unit, s):
                g = unit[0] // 8
                return V[:, s, 64 * g:64 * g + 64]

            PE.wait(m_v)
            attend([(h, tt, 128 * (tt + 1)) for h in range(16) for tt in range(4)], logits, soften, value, o_region,
                   finish_heads, pool)
            it = take("out")
            done = add_residual(it)
            for j in range(NT):
                hfree[j] = [done]
            st.close()

        def attention(scale):
            st = ExitStack()
            begin = fence()
            q = sb([128, 8, L], stack=st)
            kr = sb([128, 4, L], stack=st)
            V = sb([128, 4, 256], stack=st)
            cos, sin = sb([128, L], stack=st), sb([128, L], stack=st)
            perm, pairs = sb([128, 128], stack=st), sb([128, 2], stack=st)
            qg = [sb([128, L], stack=st) for _ in range(2)]
            t2 = [sb([128, L], stack=st) for _ in range(2)]
            pool = softmax_pool(st)
            m_c = [load(d[:, :], A[n], begin) for d, n in ((cos, "c_cos"), (sin, "c_sin"), (perm, "c_perm"), (pairs, "c_pairs"))]
            gf, tf = [[], []], [[], []]
            n = [0]

            def rotate(dst, b, done, gain):
                i = n[0] % 2
                n[0] += 1
                B1, B2 = ((4, 5), (6, 7))[i]
                a = ACT.run(lambda e: e.activation(qg[i][:, :], ps[b][:, :], ACTF.Copy, scale=gain), done, gf[i], begin)
                s = ACT.run(lambda e: e.activation(sq[i][:, :], ps[b][:, :], ACTF.Square), sqfree[i])
                pfree[b] = [s]
                PE.wait(pfree[B1], m_c)
                p1 = token_sums(B1, sq[i], pairs[:, :], True, True, s)
                sqfree[i] = [p1]
                p2 = PE.run(mm(ps[B2][:, :], perm[:, :], qg[i][:, :]), a, pfree[B2])
                im = inverse_rms(B1, 64, p1, heads=2)
                m = DVE.run(lambda e: e.tensor_tensor(t2[i][:, :], ps[B2][:, :], sin[:, :], MUL), p2, tf[i], m_c, begin)
                pfree[B2] = [m]
                m1 = DVE.run(lambda e: e.tensor_tensor(qg[i][:, :], qg[i][:, :], cos[:, :], MUL), p2)
                m = DVE.run(lambda e: e.tensor_tensor(t2[i][:, :], t2[i][:, :], qg[i][:, :], ADD), m, m1)
                gf[i] = [m]
                r = spread_rms(B1, im)
                m = DVE.run(lambda e: e.tensor_tensor(dst, t2[i][:, :], ps[B1][:, :], MUL), m, r, begin)
                pfree[B1] = [m]
                tf[i] = [m]
                return m

            m_k = []
            for g in range(2):
                it = take("kk")
                banks = (0, 1) if g else (2, 3)
                done = project(it, banks)
                release(it, done[-1])
                for i in range(2):
                    m_k.append(rotate(kr[:, 2 * g + i, :], banks[i], done[i], v("k_gain")))
                pump()
            it = take("v")
            m_v = []
            for tt in range(4):
                b = tt % 2
                PE.wait(pfree[b])
                m = project_tokens(it, 0, 256, ps[b][:, 0:256], tt)
                m_v.append(ACT.run(lambda e, b=b, tt=tt: e.copy(V[:, tt, :], ps[b][:, 0:256]), m, begin))
                pfree[b] = [m_v[-1]]
            release(it, m)
            pump()
            m_q = []
            for c in range(4):
                it = take("q")
                banks = (0, 1) if c % 2 else (2, 3)
                done = project(it, banks)
                release(it, done[-1])
                for i in range(2):
                    m_q.append(rotate(q[:, 2 * c + i, :], banks[i], done[i], v("q_gain")))
                pump()
            for j in range(NT):
                hfree[j] = [done[-1]]

            def logits(unit, b):
                h, tt, S = unit
                pr = slice(64 * (h % 2), 64 * (h % 2) + 64)
                return PE.run(mm(ps[b][:, :], q[pr, h // 2, 128 * tt:128 * tt + 128], kr[pr, h // 4, :]), m_q[h // 2], m_k)

            def soften(unit, b, m, P, mx, nm, sm, free):
                m = DVE.run(lambda e: e.tensor_reduce(mx, ps[b][:, :], AX_X, ALU.max), m)
                m = DVE.run(lambda e: e.tensor_scalar(nm, mx, -0.125, None, MUL), m)
                a = ACT.run(lambda e: e.activation(P[:, :], ps[b][:, :], ACTF.Exp, bias=nm, scale=0.125, accum_out=sm), m, free)
                pfree[b] = [a]
                return a

            def value(unit, s):
                g = unit[0] // 4
                return V[:, s, 64 * g:64 * g + 64]

            PE.wait(m_v)
            attend([(h, tt, L) for h in range(16) for tt in range(4)], logits, soften, value, o_region, finish_heads, pool)
            it = take("out")
            done = add_residual(it, scale)
            for j in range(NT):
                hfree[j] = [done]
            st.close()

        def hyena(scale):
            st = ExitStack()
            begin = fence()
            u = sb([128, 24, L], stack=st)
            aT, w3 = rb[0][0:64, :], rb[1][0:64, :]
            w1, w2 = sb([33, 64], stack=st), sb([64, 64], stack=st)
            dec = sb([128, 4, 256], stack=st)
            sf, df = sb([128, 1024], stack=st), sb([128, 1024], stack=st)
            Yt = acc4
            A4b = sb([128, 1024], stack=st)
            inv = sb([128, 8], stack=st)
            m_w1 = load(w1[:, :], A["hy_f_w1_2"][0], begin)
            m_w2 = load(w2[:, :], A["hy_f_w2_2"][0], begin)

            zt = sf[0:33, 0:L]
            m_z = load(zt, A["c_zT"], begin)
            C1 = 6.28125
            C2 = float(np.float32(2 * math.pi - C1))
            C3 = 2 * math.pi - C1 - C2
            MAGIC = 12582912.0

            def sine(dst, b, bias, m):
                t, k = df[0:64, 0:L], df[0:64, L:2 * L]
                m = DVE.run(lambda e: e.tensor_scalar(t, ps[b][0:64, :], bias, v("freq")[0:64], ADD, MUL), m, begin)
                pfree[b] = [m]
                n = DVE.run(lambda e: e.tensor_scalar(k, t, 1.0 / (2 * math.pi), MAGIC, MUL, ADD), m)
                n = DVE.run(lambda e: e.tensor_scalar(k, k, -MAGIC, None, ADD), n)
                for cst in (C1, C2, C3):
                    n = DVE.run(lambda e, cst=cst: e.scalar_tensor_tensor(t, k, -cst, t, MUL, ADD), n)
                n = DVE.run(lambda e: e.tensor_scalar(t, t, 3.1415925, -3.1415925, ALU.min, ALU.max), n)
                return ACT.run(lambda e: e.activation(dst, t, ACTF.Sin), n, begin)

            u_ready = []
            for c in range(12):
                it = take("hy")
                banks = ((0, 1), (2, 3))[c % 2]
                done = project(it, banks)
                release(it, done[-1])
                for i in range(2):
                    t, b = 2 * c + i, banks[i]
                    m = ACT.run(lambda e, t=t, b=b: e.activation(u[:, t, :], ps[b][:, :], ACTF.Identity, bias=v("hy_cb", t),
                                                                 scale=v("hy_cw", 24 + t)), done[i], begin)
                    m = DVE.run(lambda e, t=t, b=b: e.scalar_tensor_tensor(u[:, t, 1:L], ps[b][:, 0:L - 1], v("hy_cw", t),
                                                                          u[:, t, 1:L], MUL, ADD), m)
                    m = DVE.run(lambda e, t=t, b=b: e.scalar_tensor_tensor(u[:, t, 0:L - 1], ps[b][:, 1:L], v("hy_cw", 48 + t),
                                                                          u[:, t, 0:L - 1], MUL, ADD), m)
                    pfree[b] = [m]
                    u_ready.append(m)
                if c == 3:
                    m = PE.run(mm(ps[4][0:64, :], w1[:, :], zt), m_z, m_w1, pfree[4])
                    m_a = sine(aT[:, :], 4, v("fb1")[0:64], m)
                if c == 6:
                    m = PE.run(mm(ps[4][0:64, :], w2[:, :], aT[:, :]), m_a, m_w2, pfree[4])
                    m_a = sine(aT[:, :], 4, v("fb2")[0:64], m)
                pump()
            all_h = done[-1]

            fw_it, iv_it, hold = take("fw"), take("iv"), take("hold")
            held = [take("rawhold") for _ in range(3)]
            fwh, fwl = w_views(fw_it)
            ivh, ivl = w_views(iv_it)
            yh = wh[hold["w"]][:, :].rearrange("p (f q c) -> p f q c", f=2, q=4)
            yl = wl[hold["w"]][:, :].rearrange("p (f q c) -> p f q c", f=2, q=4)
            DVE.wait(*[h["raw_free"] for h in held])
            POOL.wait(*[h["raw_free"] for h in held])
            ACT.wait(hold["free"])
            POOL.wait(hold["free"])
            Fb = raw[held[0]["r"]][:, :].rearrange("p (t c) -> p t c", t=4)
            KK = raw[held[1]["r"]][:, :].rearrange("p (f q c) -> p f q c", f=2, q=4)
            XX = raw[held[2]["r"]][:, 0:1024].rearrange("p (q c) -> p q c", q=4)
            A4s = [raw[held[2]["r"]][:, 1024:2048].rearrange("p (q c) -> p q c", q=4), A4b[:, :].rearrange("p (q c) -> p q c", q=4)]
            hv, lv = (t[:, 0:6, :].rearrange("p a l -> p (a l)").rearrange("p (w t c) -> p w t c", w=3, t=4) for t in (hh, hl))
            Yv = Yt[:, :].rearrange("p (w f c) -> p w f c", w=2, f=2)
            sv, dv = (t[:, :].rearrange("p (t c) -> p t c", t=4) for t in (sf, df))
            ef, tv = [sq[0], sq[1]], [ht[0], ht[1]]
            efree, tfree = [sqfree[0], sqfree[1]], [htfree[0], htfree[1]]
            free = dict(w3=[], dec=[], Fb=[], s=[], d=[], sh=[all_h], dh=[all_h], zh=[all_h], KK=[[], []], XX=[], A4=[[], [begin]], Yt=[begin], y=[])
            nld = [0, 0]
            s_w3, s_dec = semaphore("s_w3"), semaphore("s_dec")
            cnt = [0]

            def filters(o, cq):
                nld[0] += 2
                nld[1] += 1
                src = A["hy_f_w3_2"][0]
                for d_ in range(2):
                    c = 2048 * o + 1024 * d_ + 256 * cq
                    mw = SP.dma(s_w3, 16 * nld[0], w3[:, 256 * d_:256 * d_ + 256], src[:, c:c + 256], free["w3"], begin)
                md = SP.dma(s_dec, 16 * nld[1], dec[:, :, :], A["c_decay"][:, :, 256 * cq:256 * cq + 256], free["dec"], begin)
                ev = []
                for lt in range(4):
                    b = lt % 2
                    PE.wait(mw, m_a, pfree[b])
                    p = PE.run(mm(ps[b][:, :], aT[:, 128 * lt:128 * lt + 128], w3[:, :]))
                    m = DVE.run(lambda e, b=b, lt=lt: e.tensor_tensor(
                        Fb[:, lt, :].rearrange("p (d c) -> p d c", d=2), ps[b][:, :].rearrange("p (d c) -> p d c", d=2),
                        dec[:, lt:lt + 1, :].broadcast_to([128, 2, 256]), MUL), p, md, free["Fb"])
                    pfree[b] = [m]
                    ev.append(m)
                free["w3"], free["dec"] = [p], [m]
                z0 = DVE.run(lambda e: e.memset(Fb[0:1, 0, 256:512], 0.0), ev)
                a = DVE.run(lambda e: e.tensor_tensor(sv, Fb[:, :, 0:256], Fb[:, :, 256:512], ADD), z0, free["s"])
                b_ = POOL.run(lambda e: e.tensor_tensor(dv, Fb[:, :, 0:256], Fb[:, :, 256:512], SUB), z0, free["d"])
                s_r = split(hv[:, 0], lv[:, 0], sv, a, free["sh"], eng=POOL)
                d_r = split(hv[:, 1], lv[:, 1], dv, b_, free["dh"], eng=POOL)
                free["s"], free["d"] = s_r, d_r
                ab = ACT.run(lambda e: e.activation(Fb[:, :, :], Fb[:, :, :], ACTF.Abs), a, b_)
                return dict(s=s_r, d=d_r, ab=ab, K={})

            def filter_norm(fl):
                PE.wait(fl["ab"], pfree[2])
                for ct in range(2):
                    for i in range(8):
                        lt, d_ = i // 2, i % 2
                        c = 256 * d_ + 128 * ct
                        f = mm(ps[2][:, ct:ct + 1], Fb[:, lt, c:c + 128], ones[:, 0:1], i == 0, i == 7)
                        if ct == 1 and i == 7:
                            p = PE.run(f)
                        else:
                            PE.quiet(f)
                free["Fb"] = [p]
                c = 2 * (cnt[0] % 4)
                cnt[0] += 1
                m = DVE.run(lambda e: e.reciprocal(inv[:, c:c + 2], ps[2][:, 0:2]), p)
                pfree[2] = [m]
                m = DVE.run(lambda e: e.tensor_scalar(inv[:, c:c + 2], inv[:, c:c + 2], 2.0 ** -9, None, MUL), m)
                fl["inv"], fl["minv"] = inv[:, c:c + 2], m

            def transform(srcs, ready, ft, dst, dfree, bA, bB):
                PE.wait(fw_it["ready"], *ready)
                out_marks = []
                for half, b in ((0, bA), (1, bB)):
                    PE.wait(pfree[b])
                    for q, sc in ((half, srcs[0]), (2 + half, srcs[1])):
                        cols = slice(256 * q + 128 * ft, 256 * q + 128 * ft + 128)
                        o = ps[b][:, 0:256] if q < 2 else ps[b][:, 256:512]
                        m = product(o, [((fwh[:, kt, cols], fwl[:, kt, cols]), (hv[:, sc, 2 * half + kt, :], lv[:, sc, 2 * half + kt, :]))
                                        for kt in range(2)], True, True)
                    out_marks.append(m)
                i = ft
                a = ACT.run(lambda e: e.copy(ef[i][:, :], ps[bA][:, :]), out_marks[0], efree[i])
                pfree[bA] = [a]
                m = DVE.run(lambda e: e.tensor_tensor(dst[:, 0:2, :].rearrange("p a c -> p (a c)"), ef[i][:, :], ps[bB][:, :], ADD),
                            a, out_marks[1], dfree)
                m2 = DVE.run(lambda e: e.tensor_tensor(dst[:, 2, :], ef[i][:, 0:256], ps[bB][:, 0:256], SUB), a)
                m3 = DVE.run(lambda e: e.tensor_tensor(dst[:, 3, :], ps[bB][:, 256:512], ef[i][:, 256:512], SUB))
                pfree[bB] = [m3]
                efree[i] = [m3]
                return m3, out_marks[1]

            def filter_transform(fl, ft):
                m, p = transform((0, 1), (fl["s"], fl["d"]), ft, KK[:, ft], free["KK"][ft], 0, 1)
                fl["K"][ft] = m
                if ft:
                    free["sh"], free["dh"] = [p], [p]

            def tokens(cq):
                ready = []
                for half in range(2):
                    b = 2 + half
                    PE.wait(pfree[b])
                    for t in range(2):
                        for ct in range(2):
                            j = 2 * cq + ct
                            src = u[:, j, half + 256 * t:256 * t + 256:2]
                            o = ps[b][:, 256 * t + 128 * ct:256 * t + 128 * ct + 128]
                            f = lambda e, o=o, src=src: e.transpose(o, src, ident[:, :])
                            PE.wait(u_ready[j])
                            if t == 1 and ct == 1:
                                p = PE.run(f)
                            else:
                                PE.quiet(f)
                    o = slice(2 * half, 2 * half + 2)
                    src = ps[b][:, :].rearrange("p (t c) -> p t c", t=2)
                    a = split(hv[:, 2, o, :], lv[:, 2, o, :], src, p, free["zh"])
                    pfree[b] = a
                    ready += a
                return ready

            def convolve(o, cq, fl, z, between):
                yr = []
                for ft in range(2):
                    m, p = transform((2, 2), (z,), ft, XX, free["XX"], 4, 5)
                    A4 = A4s[ft]
                    Kv = KK[:, ft].rearrange("p (f w) c -> p f w c", w=2)
                    Xv = XX.rearrange("p (f w) c -> p f w c", w=2)
                    Av = A4.rearrange("p (f w) c -> p f w c", w=2)
                    kc = Kv[:, :, 0:1, :].broadcast_to([128, 2, 2, 256])
                    ks = Kv[:, :, 1:2, :].broadcast_to([128, 2, 2, 256])
                    a = DVE.run(lambda e, Av=Av, kc=kc: e.tensor_tensor(Av, Xv, kc, MUL), m, fl["K"][ft], free["A4"][ft])
                    b = DVE.run(lambda e, ks=ks: e.tensor_tensor(Xv, Xv, ks, MUL), a)
                    c_ = DVE.run(lambda e, Av=Av: e.tensor_tensor(Yv[:, 0], Av[:, :, 0, :], Xv[:, :, 1, :], SUB), a, b, free["Yt"])
                    s_ = DVE.run(lambda e, Av=Av: e.tensor_tensor(Yv[:, 1], Av[:, :, 1, :], Xv[:, :, 0, :], ADD), a, b)
                    free["XX"] = [s_]
                    UV = A4.rearrange("p (k w) c -> p k w c", w=2)
                    x1 = POOL.run(lambda e, UV=UV: e.tensor_tensor(UV[:, 0], Yv[:, :, 0, :], Yv[:, :, 1, :], ADD), c_, s_)
                    x2 = POOL.run(lambda e, UV=UV: e.tensor_tensor(UV[:, 1], Yv[:, :, 0, :], Yv[:, :, 1, :], SUB))
                    free["Yt"] = [x2]
                    free["KK"][ft] = [b]
                    between(ft)
                    r = split(yh[:, ft], yl[:, ft], A4, x1, x2, free["y"], eng=POOL)
                    free["A4"][ft] = r
                    yr += r
                free["zh"] = [p]
                return yr

            def invert(o, cq, fl, yr):
                PE.wait(iv_it["ready"], yr)
                for ct in range(2):
                    b = 6 + ct
                    j = 2 * cq + ct
                    PE.wait(pfree[b])
                    for half, (qc, qs) in enumerate(((0, 3), (2, 1))):
                        pairs = []
                        for ft in range(2):
                            for q, g in ((qc, half), (qs, 2 + half)):
                                cs = slice(128 * ct, 128 * ct + 128)
                                pairs.append(((yh[:, ft, q, cs], yl[:, ft, q, cs]),
                                              (ivh[:, ft, 256 * g:256 * g + 256], ivl[:, ft, 256 * g:256 * g + 256])))
                        p = product(ps[b][:, 256 * half:256 * half + 256], pairs, True, True)
                    t = tv[ct]
                    a = ACT.run(lambda e, j=j, t=t: e.activation(t[:, :], u[:, j, :], ACTF.Copy, scale=v("skip", 8 * o + j)),
                                u_ready[j], tfree[ct])
                    tw = t[:, :].rearrange("p (t two) -> p two t", two=2)
                    m = DVE.run(lambda e, b=b, ct=ct, tw=tw: e.scalar_tensor_tensor(
                        tw, ps[b][:, :].rearrange("p (two t) -> p two t", two=2), fl["inv"][:, ct:ct + 1], tw, MUL, ADD),
                        a, p, fl["minv"])
                    pfree[b] = [m]
                    u_ready[j] = DVE.run(lambda e, j=j, t=t: e.tensor_tensor(u[:, j, :], t[:, :], u[:, 8 * (o + 1) + j, :], MUL),
                                         m, u_ready[8 * (o + 1) + j])
                    tfree[ct] = [u_ready[j]]
                free["y"] = [p]
                return p

            todo = [(o, cq) for o in range(2) for cq in range(4)]
            n = len(todo)
            fl, zr, yr = {}, {}, {}
            def ahead(i):
                return lambda ft: filter_transform(fl[i], ft) if i < n else None

            fl[0] = filters(*todo[0])
            for ft in range(2):
                ahead(0)(ft)
            filter_norm(fl[0])
            fl[1] = filters(*todo[1])
            zr[0] = tokens(todo[0][1])
            for i in range(n):
                if i:
                    invert(*todo[i - 1], fl[i - 1], yr[i - 1])
                yr[i] = convolve(*todo[i], fl[i], zr[i], ahead(i + 1))
                if i + 1 < n:
                    filter_norm(fl[i + 1])
                if i == n - 2:
                    release(held[0], *free["Fb"])
                    pump()
                if i + 2 < n:
                    fl[i + 2] = filters(*todo[i + 2])
                if i + 1 < n:
                    zr[i + 1] = tokens(todo[i + 1][1])
            release(held[1], free["KK"])
            release(held[2], free["XX"], free["A4"])
            release(fw_it, free["zh"])
            pump()
            for j in range(6):
                hready[j] = split(hh[:, j, :], hl[:, j, :], u[:, j, :], u_ready[j], free["zh"], free["sh"], free["dh"],
                                  eng=POOL if j % 2 else DVE)
            last = invert(*todo[n - 1], fl[n - 1], yr[n - 1])
            sqfree[0], sqfree[1] = efree
            htfree[0], htfree[1] = tfree
            end = fence()
            rbfree[0], rbfree[1] = [end], [end]
            release(iv_it, last)
            release(hold, last)
            pump()
            for j in (6, 7):
                hready[j] = split(hh[:, j, :], hl[:, j, :], u[:, j, :], u_ready[j], all_h, eng=POOL if j % 2 else DVE)
            it = take("out")
            done = add_residual(it, scale)
            for j in range(NT):
                hfree[j] = [done]
            st.close()

        def plain_norm(gain):
            r = spread_rms(STAT, inverse_rms(STAT, D, stat["m"]))
            for j in range(NT):
                xready[j] = DVE.run(lambda e, j=j: e.scalar_tensor_tensor(x[:, j, :], x[:, j, :], gain(j), ps[STAT][:, :], MUL, MUL),
                                    r, xready[j])
                pfree[STAT] = [xready[j]]

        def block1_end():
            plain_norm(lambda j: v("final_norm", j))
            for j in range(NT):
                square_sum(j)

        steps = [
            lambda: (normalise(lambda j: v("attn_norm", j)), hgrn()),
            lambda: ffn1(0),
            lambda: (normalise(lambda j: v("attn_norm", 8 + j)), dsa()),
            lambda: ffn1(1),
            lambda: block1_end(),
            lambda: attention(modulated(0, "norm1", 0)),
            lambda: ffn2(0),
            lambda: hyena(modulated(1, "norm1", 0)),
            lambda: ffn2(1),
            lambda: plain_norm(lambda j: v("final2", j)),
        ]
        for step in steps[:stop]:
            step()

        begin = fence()
        st = ExitStack()
        ot = sb([128, 4, D], stack=st)
        for tt in range(4):
            stored = []
            for half in range(2):
                b = (2 * tt + half) % 4
                PE.wait(pfree[b])
                for i in range(4):
                    j = 4 * half + i
                    f = lambda e, b=b, i=i, j=j, tt=tt: e.transpose(ps[b][:, 128 * i:128 * i + 128], x[:, j, 128 * tt:128 * tt + 128], ident[:, :])
                    PE.wait(xready[j])
                    if i < 3:
                        PE.quiet(f)
                    else:
                        m = PE.run(f)
                eng = DVE if half else ACT
                o = ot[:, tt, 512 * half:512 * half + 512]
                fn = (lambda e, o=o, b=b: e.tensor_copy(o, ps[b][:, :])) if half else (lambda e, o=o, b=b: e.copy(o, ps[b][:, :]))
                m = eng.run(fn, m, begin)
                pfree[b] = [m]
                stored.append(m)
            SP.dma(s_out, 16 * (tt + 1), out[0, 128 * tt:128 * tt + 128, :], ot[:, tt, :], stored)
        SP.wait((s_out, 64))
        st.close()

        block = ctx.enter_context(nc.Block())

        @block.sync
        def _(e):
            for op in SP.ops:
                op(e)

        @block.scalar
        def _(e):
            for op in ACT.ops:
                op(e)

        @block.vector
        def _(e):
            for op in DVE.ops:
                op(e)

        @block.gpsimd
        def _(e):
            for op in POOL.ops:
                op(e)

        @block.tensor
        def _(e):
            for op in PE.ops:
                op(e)


_WEIGHTS = ["x", "hgrn_w_in", "hgrn_w_out", "dsa_w_in", "dsa_w_out", "rel_bias", "ffn_w_up", "ffn_w_down", "ada_w_2",
            "attn_w_qkv_2", "attn_w_o_2", "hy_w_in_2", "hy_f_w1_2", "hy_f_w2_2", "hy_f_w3_2", "hy_w_out_2",
            "ffn_w_up_2", "ffn_w_down_2"]


def lay_out(inputs):
    def by_feature(name):
        a = np.asarray(inputs[name])
        return a.reshape(-1, 128).T

    def twice(name):
        return np.tile(np.asarray(inputs[name]).reshape(-1, 1), (2, 1))

    parts = {
        "attn_norm": by_feature("attn_norm"), "ffn_norm": by_feature("ffn_norm"), "final_norm": by_feature("final_norm"),
        "gate_norm": by_feature("hgrn_gate_norm"), "lower": by_feature("hgrn_lower_bounds"), "c": by_feature("c_2"),
        "ada_b": by_feature("ada_b_2"), "norm1": by_feature("norm1_g_2"), "norm2": by_feature("norm2_g_2"),
        "final2": by_feature("final_g_2"), "q_gain": twice("attn_q_gain_2"), "k_gain": twice("attn_k_gain_2"),
        "hy_cw": by_feature("hy_conv_w_2"), "hy_cb": by_feature("hy_conv_b_2"), "skip": by_feature("hy_skip_2"),
        "cw0": by_feature("ffn_conv_w"), "cb0": by_feature("ffn_conv_b"), "cw1": by_feature("ffn_conv_w_2"),
        "cb1": by_feature("ffn_conv_b_2"), "fb1": twice("hy_f_b1_2"), "fb2": twice("hy_f_b2_2"), "freq": twice("hy_f_freq_2"),
    }
    arrays = {n: np.ascontiguousarray(inputs[n]) for n in _WEIGHTS}
    arrays["vec"] = np.ascontiguousarray(np.concatenate([parts[n] for n in VEC], axis=1))
    for n, a in shape_constants().items():
        arrays[f"c_{n}"] = a
    return arrays


def kernel(**inputs):
    import concourse.bacc as _bacc
    from concourse.bass_utils import run_bass_kernel_spmd as _run

    nc = _bacc.Bacc("TRN2", target_bir_lowering=False, num_devices=1)
    arrays, aps = {}, {}
    for name, a in lay_out(inputs).items():
        arrays[f"in_{name}"] = a
        aps[name] = nc.dram_tensor(f"in_{name}", a.shape, mybir.dt.from_np(a.dtype), kind="ExternalInput").ap()
    out = nc.dram_tensor("out_0", (1, L, D), F, kind="ExternalOutput").ap()
    build(nc, aps, out)
    r = _run(nc, [arrays], core_ids=[0])
    return r.results[0]["out_0"]
```

```python
import math
from contextlib import ExitStack

import numpy as np

import concourse.bass as bass
from concourse import mybir

F = mybir.dt.float32
R = mybir.dt.float32r
ALU = mybir.AluOpType
ACTF = mybir.ActivationFunctionType
AX_X = mybir.AxisListType.X
MUL, ADD, SUB = ALU.mult, ALU.add, ALU.subtract

L = 512
D = 1024
NT = D // 128
DFF = 2816
CW = 2048
NRAW, NW = 3, 3
EPS = 1e-6
TINY = 1e-30
NEG = -1e30
GONE = -3e38
SPLITS = (1024, 128, 128, 512, 64, 8)
TOPK = 128
AF = DFF // 128
GROUPS = ((0, 4), (4, 8), (8, 11))
ACT_RING = 10


VEC = {}


def _vec_layout():
    at = 0
    for name, n in (
        ("attn_norm", 16), ("ffn_norm", 16), ("final_norm", 8), ("gate_norm", 1), ("lower", 8),
        ("c", 8), ("ada_b", 96), ("norm1", 16), ("norm2", 16), ("final2", 8), ("q_gain", 1), ("k_gain", 1),
        ("hy_cw", 72), ("hy_cb", 24), ("skip", 16), ("cw0", 264), ("cb0", 88), ("cw1", 132), ("cb1", 44),
        ("fb1", 1), ("fb2", 1), ("freq", 1),
    ):
        VEC[name] = (at, n)
        at += n
    return at


NVEC = _vec_layout()


def shape_constants():
    f32 = np.float32
    c = {}
    c["ident"] = np.eye(128, dtype=f32)
    s, t = np.meshgrid(np.arange(128), np.arange(128), indexing="ij")
    masks = []
    for n in range(7):
        b = 1 << n
        masks.append((s // (2 * b) == t // (2 * b)) & ((s // b) % 2 == 0) & ((t // b) % 2 == 1))
    c["masks"] = np.concatenate(masks, axis=1).astype(f32)
    c["cmin"] = np.where(t <= s, f32(3e38), f32(NEG)).astype(f32)
    c["cadd"] = np.where(t <= s, f32(0), f32(NEG)).astype(f32)
    dist = np.maximum(511 - np.arange(640), 0)
    nf = np.maximum(dist, 16).astype(f32)
    large = 16 + (np.log(nf / f32(16)) / f32(math.log(8.0)) * f32(16)).astype(np.int32)
    bucket = np.where(dist < 16, dist, np.minimum(large, 31))
    c["onehot"] = (np.arange(32)[:, None] == bucket[None, :]).astype(f32)
    n_freq = 16
    inv = (f32(1.0) / (f32(10000.0) ** (np.arange(n_freq, dtype=f32) / f32(n_freq)))).astype(f32)
    pos = np.arange(L)
    ang = np.concatenate([(pos // 64).astype(f32)[:, None] * inv, (pos % 64).astype(f32)[:, None] * inv], axis=1)
    pair = (np.arange(128) % 64) // 2
    c["cos"] = np.cos(ang).astype(f32)[:, pair].T
    c["sin"] = np.sin(ang).astype(f32)[:, pair].T
    perm = np.zeros((128, 128), f32)
    i = np.arange(0, 128, 2)
    perm[i + 1, i] = -1.0
    perm[i, i + 1] = 1.0
    c["perm"] = perm
    g = np.arange(128) // 64
    c["pairs"] = (g[:, None] == np.arange(2)[None, :]).astype(f32)
    order = np.concatenate([np.arange(0, L, 2), np.arange(1, L, 2)])
    tl = np.linspace(0.0, 1.0, L, dtype=f32)
    w = (f32(2.0 * math.pi) * np.arange(L, dtype=f32) / f32(L)).astype(f32)
    fr = np.linspace(1e-4, 15, 16, dtype=f32)
    a2 = (w[:, None] * fr[None, :]).astype(f32)
    z = np.concatenate([tl[:, None], np.cos(a2), -np.sin(a2)], axis=1).astype(f32)
    c["zT"] = z[order].T
    deltas = np.abs(np.linspace(math.log(1e-2) / 1.5, math.log(1e-2) / 0.3, D, dtype=f32))
    decay = np.exp(-tl[:, None] * deltas[None, :]).astype(f32)
    c["decay"] = decay[order].reshape(4, 128, D).transpose(1, 0, 2)
    om = 2 * np.pi * (np.arange(256) + 0.5) / 1024
    ev, od = np.arange(0, L, 2), np.arange(1, L, 2)
    fw = np.concatenate([np.cos(np.outer(ev, om)), np.cos(np.outer(od, om)),
                         np.sin(np.outer(ev, om)), np.sin(np.outer(od, om))], axis=1)
    c["fw"] = fw.astype(f32)
    iv = np.concatenate([np.cos(np.outer(om, ev)), np.cos(np.outer(om, od)),
                         np.sin(np.outer(om, ev)), np.sin(np.outer(om, od))], axis=1)
    c["iv"] = iv.astype(f32)
    return {k: np.ascontiguousarray(v, dtype=f32) for k, v in c.items()}


class Engine:

    def __init__(self, sem):
        self.sem, self.count, self.ops, self.seen = sem, 0, [], {}

    def wait(self, *marks):
        for m in marks:
            if m is None:
                continue
            if isinstance(m, list):
                self.wait(*m)
                continue
            sem, value = m
            if self.seen.get(sem, 0) < value:
                self.seen[sem] = value
                self.ops.append(lambda e, s=sem, v=value: e.wait_ge(s, v))

    def quiet(self, fn, *marks):
        self.wait(*marks)
        self.ops.append(fn)

    def run(self, fn, *marks):
        self.wait(*marks)
        self.count += 1
        self.ops.append(lambda e: fn(e).then_inc(self.sem, 1))
        return (self.sem, self.count)

    def dma(self, sem, total, out, in_, *marks):
        self.wait(*marks)
        self.ops.append(lambda e: e.dma_start(out, in_).then_inc(sem, 16))
        return (sem, total)

    def last(self):
        return (self.sem, self.count) if self.count else None


def stream_plan(A):
    items = []

    def cols(w, c0, n, k0=0, k1=None):
        v = w.rearrange("(k p) n -> p k n", p=128)
        return v[:, k0:(k1 if k1 is not None else v.shape[1]), c0:c0 + n]

    def w(name, *parts):
        placed, at = [], 0
        for p in parts:
            placed.append((p, at))
            at += p.shape[2]
        items.append(dict(kind="w", name=name, parts=placed, kt=parts[0].shape[1], n=at))

    def dense(name, wt):
        for j in range(4):
            w(name, cols(wt, 256 * j, 256))

    def ffn(up, down):
        for gi, (p0, p1) in enumerate(GROUPS):
            for p in range(p0, p1):
                w("gate", cols(up, 256 * p, 256))
                w("up", cols(up, DFF + 256 * p, 256))
                if gi and p == p0:
                    q0, q1 = GROUPS[gi - 1]
                    for j in range(4):
                        w("down", cols(down, 256 * j, 256, 2 * q0, 2 * q1))
        q0, q1 = GROUPS[-1]
        for j in range(4):
            w("down", cols(down, 256 * j, 256, 2 * q0, 2 * q1))

    hw = A["hgrn_w_in"][0]
    for j in range(4):
        w("i", cols(hw, 2048 + 256 * j, 256))
    for j in range(4):
        w("g", cols(hw, 3072 + 256 * j, 256))
    for h in range(8):
        w("fq", cols(hw, 1024 + 128 * h, 128), cols(hw, 128 * h, 128))
    dense("out", A["hgrn_w_out"][0])
    ffn(A["ffn_w_up"][0], A["ffn_w_down"][0])
    dw = A["dsa_w_in"][0]
    o = [0]
    for n in SPLITS:
        o.append(o[-1] + n)
    w("ix", cols(dw, o[3], 256))
    w("ix", cols(dw, o[3] + 256, 256))
    w("kw", cols(dw, o[4], 64), cols(dw, o[4], 64), cols(dw, o[5], 8))
    w("kk", cols(dw, o[1], 64), cols(dw, o[1], 64), cols(dw, o[1] + 64, 64), cols(dw, o[1] + 64, 64))
    w("v", cols(dw, o[2], 128))
    dense("q", dw[:, 0:1024])
    dense("out", A["dsa_w_out"][0])
    ffn(A["ffn_w_up"][1], A["ffn_w_down"][1])
    aw = A["attn_w_qkv_2"][0]
    for g in range(2):
        w("kk", *[cols(aw, 1024 + 64 * (2 * g + i // 2), 64) for i in range(4)])
    w("v", cols(aw, 1280, 256))
    dense("q", aw[:, 0:1024])
    dense("out", A["attn_w_o_2"][0])
    ffn(A["ffn_w_up_2"][0], A["ffn_w_down_2"][0])
    yw = A["hy_w_in_2"][0]
    for j in range(12):
        w("hy", cols(yw, 256 * j, 256))
    w("fw", cols(A["c_fw"], 0, 1024))
    w("iv", cols(A["c_iv"], 0, 1024))
    items.append(dict(kind="hold", name="hold"))
    for _ in range(3):
        items.append(dict(kind="rawhold", name="rawhold"))
    dense("out", A["hy_w_out_2"][0])
    ffn(A["ffn_w_up_2"][1], A["ffn_w_down_2"][1])
    return items


def build(nc, A, out, stop=99):
    ctx = ExitStack()
    with ctx:
        names = [0]

        def sb(shape, dt=F, stack=ctx):
            names[0] += 1
            return stack.enter_context(nc.sbuf_tensor(f"sb{names[0]}", list(shape), dt))

        def semaphore(name):
            return ctx.enter_context(nc.semaphore(name))

        PE, ACT, DVE, POOL, SP = (Engine(semaphore(f"s_{n}")) for n in ("pe", "act", "dve", "pool", "sp"))
        s_out = semaphore("s_out")
        ps = [ctx.enter_context(nc.psum_tensor(f"ps{b}", [128, 512], F)) for b in range(8)]
        pfree = [[] for _ in range(8)]

        x = sb([128, NT, L])
        hh, hl = sb([128, NT, L], R), sb([128, NT, L], R)
        raw = [sb([128, CW]) for _ in range(NRAW)]
        wh = [sb([128, CW], R) for _ in range(NW)]
        wl = [sb([128, CW], R) for _ in range(NW)]
        vec = sb([128, NVEC])
        ident, ones = sb([128, 128]), sb([128, 128])
        sq = [sb([128, L]) for _ in range(2)]
        rb = [sb([128, L]) for _ in range(2)]
        rc = [sb([128, 8]) for _ in range(2)]
        ht = [sb([128, L]) for _ in range(2)]
        eps, warm = sb([128, 1]), sb([128, 1])
        acc4 = sb([128, 1024])
        acc = [acc4[:, 256 * i:256 * i + 256] for i in range(4)]
        mod = sb([128, 96])
        cact = sb([128, 8])
        g1c = sb([128, 8])

        def v(name, i=0, n=1):
            a, m = VEC[name]
            assert i + n <= m
            return vec[:, a + i:a + i + n]

        def load(dst, src, *marks, eng=None):
            s = semaphore(f"ld{names[0]}_{len(loads)}")
            loads.append(s)
            return (eng or SP).dma(s, 16, dst, src, *marks)

        loads = []

        items = stream_plan(A)
        rsem = [semaphore(f"s_raw{i}") for i in range(NRAW)]
        rcount = [0] * NRAW
        rfree = [[] for _ in range(NRAW)]
        rheld = [False] * NRAW
        wfree = [[] for _ in range(NW)]
        wheld = [False] * NW
        nr = nw = 0
        for it in items:
            it["r"] = it["w"] = None
            if it["kind"] != "hold":
                it["r"] = nr % NRAW
                nr += 1
            if it["kind"] in ("w", "hold"):
                it["w"] = nw % NW
                nw += 1
        at = dict(issue=0, split=0, take=0)
        low_by = [POOL]

        def pump():
            while True:
                moved = False
                if at["issue"] < len(items):
                    it = items[at["issue"]]
                    r = it["r"]
                    if r is None:
                        at["issue"] += 1
                        moved = True
                    elif not rheld[r]:
                        rheld[r] = True
                        it["raw_free"] = rfree[r]
                        for view, c0 in it.get("parts", ()):
                            kt, n = view.shape[1], view.shape[2]
                            dst = raw[r][:, 0:it["kt"] * it["n"]].rearrange("p (k n) -> p k n", n=it["n"])[:, :, c0:c0 + n]
                            rcount[r] += 16
                            it["landed"] = SP.dma(rsem[r], rcount[r], dst, view, it["raw_free"])
                        at["issue"] += 1
                        moved = True
                if at["split"] < at["issue"]:
                    it = items[at["split"]]
                    if it["kind"] == "rawhold":
                        at["split"] += 1
                        moved = True
                    elif not wheld[it["w"]]:
                        s = it["w"]
                        wheld[s] = True
                        it["free"] = wfree[s]
                        if it["kind"] == "w":
                            n = it["kt"] * it["n"]
                            r = it["r"]
                            hi = ACT.run(lambda e, s=s, r=r, n=n: e.activation(wh[s][:, 0:n], raw[r][:, 0:n], ACTF.Copy),
                                         it["landed"], wfree[s])
                            lo = low_by[0].run(lambda e, s=s, r=r, n=n: e.tensor_tensor(
                                wl[s][:, 0:n], raw[r][:, 0:n], wh[s][:, 0:n].bitcast(F), SUB), hi)
                            it["ready"] = [hi, lo]
                            rfree[r] = [hi, lo]
                            rheld[r] = False
                        at["split"] += 1
                        moved = True
                if not moved:
                    return

        def take(name):
            while True:
                it = items[at["take"]]
                assert it["name"] == name, (it["name"], name)
                at["take"] += 1
                assert at["split"] >= at["take"], name
                return it

        def release(it, *marks):
            if it["kind"] in ("w", "hold"):
                wfree[it["w"]] = list(marks)
                wheld[it["w"]] = False
            else:
                rfree[it["r"]] = list(marks)
                rheld[it["r"]] = False

        def w_views(it):
            n = it["kt"] * it["n"]
            s = it["w"]
            return [t[s][:, 0:n].rearrange("p (k n) -> p k n", n=it["n"]) for t in (wh, wl)]

        hready = [None] * NT
        hfree = [[] for _ in range(NT)]

        def product(o, pairs, first, last, **kw):
            for i, ((ah, al), (bh, bl)) in enumerate(pairs):
                f, l = first and i == 0, last and i == len(pairs) - 1
                PE.quiet(lambda e, o=o, a=al, b=bh, f=f: e.matmul(o, a, b, start=f, stop=False, **kw))
                PE.quiet(lambda e, o=o, a=ah, b=bl: e.matmul(o, a, b, start=False, stop=False, **kw))
                m = lambda e, o=o, a=ah, b=bh, l=l: e.matmul(o, a, b, start=False, stop=l, **kw)
                if i == len(pairs) - 1 and last:
                    return PE.run(m)
                PE.quiet(m)

        def project(it, banks, xh=None, xl=None, ready=None, rows=None):
            a, b = w_views(it)
            xh = xh or (lambda k: hh[:, k, :])
            xl = xl or (lambda k: hl[:, k, :])
            ready = ready or (lambda k: hready[k])
            rows = rows or range(it["kt"])
            PE.wait(it["ready"])
            if rows[0] == 0:
                for bk in banks:
                    PE.wait(pfree[bk])
            marks = []
            for k in rows:
                PE.wait(ready(k))
                for j, bk in enumerate(banks):
                    c = slice(128 * j, 128 * j + 128)
                    m = product(ps[bk][:, :], [((a[:, k, c], b[:, k, c]), (xh(k), xl(k)))],
                                k == 0, k == it["kt"] - 1)
                    marks.append(m)
            return [m for m in marks if m]

        def project_tokens(it, c0, n, o, tt):
            a, b = w_views(it)
            PE.wait(it["ready"])
            for k in range(NT):
                PE.wait(hready[k])
                c = slice(128 * tt, 128 * tt + 128)
                m = product(o, [((hh[:, k, c], hl[:, k, c]), (a[:, k, c0:c0 + n], b[:, k, c0:c0 + n]))],
                            k == 0, k == NT - 1)
            return m

        def mm(o, a, b, start=True, stop=True, **kw):
            return lambda e: e.matmul(o, a, b, start=start, stop=stop, **kw)

        def split(hi, lo, src, *marks, eng=None):
            a = ACT.run(lambda e: e.activation(hi, src, ACTF.Copy), *marks)
            b = (eng or DVE).run(lambda e: e.tensor_tensor(lo, src, hi.bitcast(F), SUB), a)
            return [a, b]

        xready = [None] * NT
        sqfree = [[], []]
        STAT = 7
        stat = {}

        def token_sums(bank, src, cols, first, last, *marks, at=0):
            n = cols.shape[1]
            PE.wait(*marks)
            for tt in range(4):
                f = mm(ps[bank][:, at + n * tt:at + n * tt + n], src[:, 128 * tt:128 * tt + 128], cols, first and tt == 0, last,
                       skip_group_check=True)
                if tt == 3:
                    return PE.run(f)
                PE.quiet(f)

        rbfree = [[], []]
        rb_n = [0]

        def square_sum(j, gain=None):
            if j == 4:
                ACT.run(lambda e: e.activation(warm[:, :], eps[:, :], ACTF.Sqrt))
            kinds = [(0, sq, sqfree, 1.0)] + ([(1, ht, htfree, gain(j))] if gain else [])
            for i, buf, bfree, g in kinds:
                total = rb[i]
                if j == 0:
                    stat[i] = ACT.run(lambda e, total=total, g=g: e.activation(total[:, :], x[:, 0, :], ACTF.Square, scale=g),
                                      xready[0], rbfree[i])
                    continue
                b = buf[j % 2]
                m = ACT.run(lambda e, b=b, g=g: e.activation(b[:, :], x[:, j, :], ACTF.Square, scale=g), xready[j], bfree[j % 2])
                if j < NT - 2:
                    stat[i] = POOL.run(lambda e, total=total, b=b: e.tensor_tensor(total[:, :], total[:, :], b[:, :], ADD), m, stat[i])
                    bfree[j % 2] = [stat[i]]
                    continue
                if j == NT - 2:
                    PE.wait(pfree[STAT])
                    rbfree[i] = [token_sums(STAT, total, ones[:, 0:1], i == 0, False, stat[i], at=4 * i)]
                p = token_sums(STAT, b, ones[:, 0:1], False, j == NT - 1, m, at=4 * i)
                bfree[j % 2] = [p]
                stat["m"] = p

        def inverse_rms(bank, n, done, heads=1):
            i = rb_n[0] % 2
            rb_n[0] += 1
            w = 4 * heads
            a = ACT.run(lambda e: e.activation(rc[i][:, 0:w], ps[bank][:, 0:w], ACTF.Sqrt, bias=eps[:, 0:1], scale=1.0 / n), done)
            pfree[bank] = [a]
            m = DVE.run(lambda e: e.reciprocal(rc[i][:, 0:w], rc[i][:, 0:w]), a)
            wide = rb[i][:, :].rearrange("p (c f) -> p c f", c=w)
            m = DVE.run(lambda e: e.tensor_copy(wide, rc[i][:, 0:w].unsqueeze(2).broadcast_to([128, w, 128 // heads])), m, rbfree[i])
            return i, m

        def spread_rms(bank, im):
            i, m = im
            PE.wait(m, pfree[bank])
            for tt in range(4):
                f = mm(ps[bank][:, 128 * tt:128 * tt + 128], rb[i][:, 128 * tt:128 * tt + 128], ident[:, :], skip_group_check=True)
                if tt < 3:
                    PE.quiet(f)
            p = PE.run(f)
            rbfree[i] = [p]
            return p

        htfree = [[], []]

        def normalise(gain, shift=None):
            shifted(gain, shift, spread_rms(STAT, inverse_rms(STAT, D, stat["m"])))

        def shifted(gain, shift, r):
            for j in range(NT):
                t = ht[j % 2]
                m = DVE.run(lambda e, j=j, t=t: e.scalar_tensor_tensor(t[:, :], x[:, j, :], gain(j), ps[STAT][:, :], MUL, MUL),
                            r, xready[j], htfree[j % 2])
                pfree[STAT] = [m]
                if shift is None:
                    hready[j] = split(hh[:, j, :], hl[:, j, :], t[:, :], m, hfree[j], eng=POOL if j % 2 else DVE)
                elif j % 2:
                    m = POOL.run(lambda e, j=j, t=t: e.tensor_scalar(t[:, :], t[:, :], shift(j), 1.0, ADD, MUL), m)
                    hready[j] = split(hh[:, j, :], hl[:, j, :], t[:, :], m, hfree[j], eng=POOL)
                else:
                    hi = ACT.run(lambda e, j=j, t=t: e.activation(hh[:, j, :], t[:, :], ACTF.Identity, bias=shift(j)), m, hfree[j])
                    lo = DVE.run(lambda e, j=j, t=t: e.scalar_tensor_tensor(hl[:, j, :], t[:, :], shift(j), hh[:, j, :].bitcast(F),
                                                                            ADD, SUB), hi)
                    hready[j] = [hi, lo]
                htfree[j % 2] = hready[j]

        def add_residual(it, scale=None, stats=True, gain=None, **kw):
            for j0 in range(0, NT, 2):
                if j0:
                    it = take(it["name"])
                banks = (4, 5) if (j0 // 2) % 2 else (2, 3)
                if kw.get("banks"):
                    banks = kw["banks"][(j0 // 2) % 2]
                done = project(it, banks, **kw.get("rhs", {}))
                release(it, done[-1])
                for i in range(2):
                    j = j0 + i
                    b = banks[i]
                    if scale is None:
                        xready[j] = DVE.run(lambda e, j=j, b=b: e.tensor_tensor(x[:, j, :], x[:, j, :], ps[b][:, :], ADD),
                                            done[i], xready[j])
                    else:
                        xready[j] = DVE.run(lambda e, j=j, b=b: e.scalar_tensor_tensor(
                            x[:, j, :], ps[b][:, :], scale(j), x[:, j, :], MUL, ADD), done[i], xready[j])
                    pfree[b] = [xready[j]]
                if stats:
                    for i in range(2):
                        square_sum(j0 + i, gain)
                pump()
            return done[-1]

        stores = []

        def fence():
            return [e.last() for e in (PE, ACT, DVE, POOL)] + stores

        m_ones = POOL.run(lambda e: e.memset(ones[:, :], 1.0))
        m_eps = POOL.run(lambda e: e.memset(eps[:, :], EPS))
        st = ExitStack()
        xt = sb([128, 4, D], stack=st)
        oh, relb, bv = sb([32, 640], stack=st), sb([32, 16], stack=st), sb([16, 640], stack=st)
        m_oh = load(oh[:, :], A["c_onehot"], eng=ACT)
        m_rb = load(relb[:, :], A["rel_bias"], eng=ACT)
        m_vec = load(vec[:, :], A["vec"], eng=ACT)
        m_id = load(ident[:, :], A["c_ident"])
        m_xt = [load(xt[:, t, :], A["x"][0].rearrange("(t p) d -> p t d", p=128)[:, t, :]) for t in range(4)]

        scratch = nc.dram_tensor("bias_by_distance", (16, 128, 640), F, kind="Internal")
        m_bv = []
        for i in range(2):
            b = 5 + i
            m = PE.run(mm(ps[b][0:16, 0:320], relb[:, :], oh[:, 320 * i:320 * i + 320]), m_oh, m_rb, pfree[b])
            m_bv.append(DVE.run(lambda e, b=b, i=i: e.tensor_copy(bv[:, 320 * i:320 * i + 320], ps[b][0:16, 0:320]), m))
            pfree[b] = [m_bv[-1]]

        pump()
        ACT.wait(m_eps, m_vec)
        PE.wait(m_ones)
        DVE.wait(m_vec)
        PE.wait(m_id)
        squares = []
        for j in range(NT + 2):
            if j >= 2:
                p = token_sums(STAT, sq[j % 2], ones[:, 0:1], j == 2, j == NT + 1, squares[j - 2])
                sqfree[j % 2] = [p]
                stat["m"] = p
            if j == NT or j == NT + 1:
                continue
            b = j % 4
            PE.wait(pfree[b])
            for t in range(4):
                fn = lambda e, b=b, t=t, j=j: e.transpose(ps[b][:, 128 * t:128 * t + 128], xt[:, t, 128 * j:128 * j + 128], ident[:, :])
                PE.wait(m_xt[t])
                if t < 3:
                    PE.quiet(fn)
                else:
                    m = PE.run(fn)
            xready[j] = DVE.run(lambda e, b=b, j=j: e.tensor_copy(x[:, j, :], ps[b][:, :]), m)
            pfree[b] = [xready[j]]
            squares.append(DVE.run(lambda e, j=j: e.tensor_tensor(sq[j % 2][:, :], x[:, j, :], x[:, j, :], MUL), xready[j], sqfree[j % 2]))
        m_scratch = load(scratch.ap(), bv[:, :].unsqueeze(1).broadcast_to([16, 128, 640]), m_bv)
        stores.append(m_scratch)
        st.close()

        lbt = sb([128, 4, 8])

        def hgrn():
            st = ExitStack()
            begin = [fence(), m_scratch]
            NE = 4
            I = sb([128, 4, D], stack=st)
            M = sb([128, 8, L], stack=st)
            E = [sb([128, L], stack=st) for _ in range(NE)]
            Q, K, P, X = ([sb([128, L], stack=st) for _ in range(2)] for _ in range(4))
            S = [sb([128, L], stack=st) for _ in range(2)]
            SO = sb([128, 768], stack=st)
            masks = sb([128, 896], stack=st)
            m_masks = load(masks[:, :], A["c_masks"], *begin)

            m = DVE.run(lambda e: e.tensor_tensor(lbt[:, 0, :], v("lower", 0, 8), v("lower", 0, 8), SUB))
            m = ACT.run(lambda e: e.activation(lbt[:, 1, :], lbt[:, 0, :], ACTF.Exp), m)
            m = DVE.run(lambda e: e.reciprocal(lbt[:, 0, :], lbt[:, 1, :]), m)
            m = DVE.run(lambda e: e.tensor_tensor(lbt[:, 1, :], lbt[:, 1, :], lbt[:, 0, :], MUL), m)
            m = DVE.run(lambda e: e.tensor_tensor(lbt[:, 2, :], lbt[:, 1, :], lbt[:, 1, :], SUB), m)
            m_lb = DVE.run(lambda e: e.tensor_scalar(lbt[:, 3, :], lbt[:, 2, :], -1.0, 1.0, MUL, ADD), m)

            i_ready = []
            for c in range(4):
                it = take("i")
                a, b = w_views(it)
                PE.wait(it["ready"])
                for tt in range(4):
                    PE.wait(pfree[tt])
                for k in range(NT):
                    PE.wait(hready[k])
                    for tt in range(4):
                        t = slice(128 * tt, 128 * tt + 128)
                        m = product(ps[tt][:, 0:256], [((hh[:, k, t], hl[:, k, t]), (a[:, k, :], b[:, k, :]))], k == 0, k == NT - 1)
                        if k == NT - 1:
                            m = ACT.run(lambda e, tt=tt, c=c: e.copy(I[:, tt, 256 * c:256 * c + 256], ps[tt][:, 0:256]), m, begin[0][:4])
                            pfree[tt] = [m]
                            i_ready.append(m)
                release(it, PE.last())
                pump()
            sg_ready = []
            for c in range(4):
                it = take("g")
                banks = (0, 1) if c % 2 else (2, 3)
                done = project(it, banks)
                release(it, done[-1])
                for i in range(2):
                    j, b = 2 * c + i, banks[i]
                    m = ACT.run(lambda e, j=j, b=b: e.activation(M[:, j, :], ps[b][:, :], ACTF.Sigmoid), done[i], *begin)
                    m = DVE.run(lambda e, j=j, b=b: e.tensor_tensor(M[:, j, :], M[:, j, :], ps[b][:, :], MUL), m)
                    pfree[b] = [m]
                    sg_ready.append(m)
                pump()

            LEVEL_BANKS = (2, 4, 5, 6)
            OB, HB = 3, 7
            nlevel, nslot = [0], [0]
            efree = [[] for _ in range(NE)]
            qk_free, px_free, s_free, so_free = [[], []], [[], []], [[], []], []
            kw = dict(skip_group_check=True)

            def halves(t, n):
                return t[:, :].rearrange("p (m two b) -> p m two b", two=2, b=1 << n)

            def head_inputs(h, done):
                i = h % 2
                f = ACT.run(lambda e: e.activation(P[i][:, :], ps[0][:, :], ACTF.Sigmoid), done[0], px_free[i], *begin)
                k = ACT.run(lambda e: e.activation(K[i][:, :], ps[0][:, :], ACTF.Sigmoid, scale=-1.0), qk_free[i])
                pfree[0] = [k]
                q = ACT.run(lambda e: e.copy(Q[i][:, :], ps[1][:, :]), done[1])
                pfree[1] = [q]
                k = ACT.run(lambda e: e.activation(K[i][:, :], K[i][:, :], ACTF.Copy, scale=lbt[:, 3, h:h + 1]), m_lb, k)
                x_one = POOL.run(lambda e: e.memset(X[i][:, :], 1.0), px_free[i], *begin)
                return dict(h=h, f=f, k=k, q=q, x=x_one)

            def prepare(g):
                h, i = g["h"], g["h"] % 2
                a = DVE.run(lambda e: e.tensor_scalar(P[i][:, :], P[i][:, :], lbt[:, 3, h:h + 1], lbt[:, 2, h:h + 1], MUL, ADD), g["f"], m_lb)
                g["p"] = DVE.run(lambda e: e.tensor_scalar(P[i][:, :], P[i][:, :], TINY, None, ALU.max), a)

            def level(g, n):
                i = g["h"] % 2
                s = nslot[0] % NE
                nslot[0] += 1
                Ev, Qv, Kv, Pv, Xv = (halves(t, n) for t in (E[s], Q[i], K[i], P[i], X[i]))
                a = DVE.run(lambda e: e.tensor_tensor(Ev[:, :, 1, :], Qv[:, :, 1, :], Pv[:, :, 1, :], MUL), g["q"], g["p"], efree[s])
                b = DVE.run(lambda e: e.tensor_tensor(Ev[:, :, 0, :], Kv[:, :, 0, :], Xv[:, :, 0, :], MUL), g["k"], g["x"])
                if n < 8:
                    bl, nb = 1 << n, 256 >> n
                    g["x"] = DVE.run(lambda e: e.tensor_tensor(
                        Xv[:, :, 0, :], Xv[:, :, 0, :], Pv[:, :, 1, bl - 1:bl].broadcast_to([128, nb, bl]), MUL), g["p"], b)
                    g["p"] = DVE.run(lambda e: e.tensor_tensor(
                        Pv[:, :, 1, :], Pv[:, :, 1, :], Pv[:, :, 0, bl - 1:bl].broadcast_to([128, nb, bl]), MUL), a, g["x"])
                else:
                    px_free[i] = [b]
                return s, b

            def level_scores(g, n, sm):
                i = g["h"] % 2
                bk = LEVEL_BANKS[nlevel[0] % 4]
                nlevel[0] += 1
                PE.wait(pfree[bk])
                if n is None:
                    PE.wait(g["q"], g["k"])
                    a_, b_ = K[i], Q[i]
                else:
                    s, m = sm
                    PE.wait(m)
                    a_ = b_ = E[s]
                if n == 8:
                    fs = [mm(ps[bk][:, 256 * t:256 * t + 256], a_[:, 128 * t:128 * t + 128], b_[:, 256:512]) for t in range(2)]
                elif n == 7:
                    fs = [mm(ps[bk][:, 128 * t:128 * t + 128], a_[:, 256 * t:256 * t + 128], b_[:, 256 * t + 128:256 * t + 256]) for t in range(2)]
                else:
                    fs = [mm(ps[bk][:, 128 * t:128 * t + 128], a_[:, 128 * t:128 * t + 128], b_[:, 128 * t:128 * t + 128]) for t in range(4)]
                for f in fs[:-1]:
                    PE.quiet(f)
                p = PE.run(fs[-1])
                if n is None:
                    qk_free[i] = [p, g["last"]]
                else:
                    efree[s] = [p]
                return bk, p

            def collect(g, n, bk, p):
                i = g["h"] % 2
                if n == 8:
                    m = ACT.run(lambda e: e.copy(SO[:, 0:512], ps[bk][:, :]), p, so_free, *begin)
                    g["far"].append(m)
                elif n == 7:
                    m = ACT.run(lambda e: e.copy(SO[:, 512:768], ps[bk][:, 0:256]), p, so_free, *begin)
                    g["far"].append(m)
                else:
                    mask = (ident[:, :] if n is None else masks[:, 128 * n:128 * n + 128]).unsqueeze(1).broadcast_to([128, 4, 128])
                    o = S[i][:, :].rearrange("p (t q) -> p t q", t=4)
                    src = ps[bk][:, :].rearrange("p (t q) -> p t q", t=4)
                    if n == 0:
                        m = DVE.run(lambda e: e.tensor_tensor(o, src, mask, MUL), p, s_free[i], m_masks)
                    else:
                        m = DVE.run(lambda e: e.copy_predicated(o, mask.bitcast(mybir.dt.uint32), src), p, g["near"])
                    g["near"] = m
                pfree[bk] = [m]

            def values(g):
                h = g["h"]
                i = h % 2
                hc = slice(128 * h, 128 * h + 128)
                PE.wait(pfree[OB], i_ready, g["far"])
                for s in range(2):
                    PE.quiet(mm(ps[OB][:, 256:512], I[:, s, hc], SO[:, 256 * s:256 * s + 256], s == 0, False, **kw))
                PE.quiet(mm(ps[OB][:, 128:256], I[:, 0, hc], SO[:, 512:640], False, False, **kw))
                so_free[:] = [PE.run(mm(ps[OB][:, 384:512], I[:, 2, hc], SO[:, 640:768], False, False, **kw))]
                PE.wait(g["near"])
                for tt in range(4):
                    c = slice(128 * tt, 128 * tt + 128)
                    f = mm(ps[OB][:, c], I[:, tt, hc], S[i][:, c], False, tt == 3, **kw)
                    if tt < 3:
                        PE.quiet(f)
                p = PE.run(f)
                s_free[i] = [p]
                s2 = ACT.run(lambda e: e.activation(sq[i][:, :], ps[OB][:, :], ACTF.Square), p, sqfree[i])
                og = ACT.run(lambda e: e.activation(ht[i][:, :], ps[OB][:, :], ACTF.Copy, scale=v("gate_norm")), htfree[i])
                pfree[OB] = [og]
                g["sq"], g["og"] = s2, og

            def head_sums(g):
                i = g["h"] % 2
                PE.wait(pfree[HB])
                p = token_sums(HB, sq[i], ones[:, 0:1], True, True, g["sq"])
                sqfree[i] = [p]
                g["im"] = inverse_rms(HB, 128, p)

            def head_output(g):
                h, i = g["h"], g["h"] % 2
                r = spread_rms(HB, g["im"])
                m = DVE.run(lambda e: e.tensor_tensor(M[:, h, :], M[:, h, :], ht[i][:, :], MUL), g["og"], sg_ready[h])
                htfree[i] = [m]
                m = DVE.run(lambda e: e.tensor_tensor(M[:, h, :], M[:, h, :], ps[HB][:, :], MUL), m, r)
                pfree[HB] = [m]
                m_ready.append(m)

            m_ready = []
            it = take("fq")
            done = project(it, (0, 1))
            release(it, done[-1])
            g = head_inputs(0, done)
            pump()
            prev = None
            ORDER = [0, 1, 2, 3, 4, 5, 6, None, 7, 8]
            PIECES = {0: (0,), 1: (1,), 2: (2,), 3: (3,), 4: (4,), 5: (5,), 6: (6,), 7: (7,)}
            LAG = 2
            for h in range(8):
                g["far"], g["near"] = [], None
                prepare(g)
                made = {}
                queue = []
                nxt = None
                if h < 7:
                    it = take("fq")
                for i, n in enumerate(ORDER):
                    if n is not None:
                        made[n] = level(g, n)
                        g["last"] = made[n][1]
                    if h < 7 and i in PIECES:
                        done = project(it, (0, 1), rows=PIECES[i])
                        if PIECES[i][-1] == 7:
                            release(it, done[-1])
                            nxt = head_inputs(h + 1, done)
                    bk, p = level_scores(g, n, made.get(n))
                    queue.append((n, bk, p))
                    if len(queue) > LAG:
                        collect(g, *queue.pop(0))
                    if i == 3 and prev:
                        head_sums(prev)
                    if i == 6 and prev:
                        head_output(prev)
                for c in queue:
                    collect(g, *c)
                values(g)
                pump()
                prev = g
                g = nxt
            head_sums(prev)
            head_output(prev)
            last = PE.last()
            for j in range(NT):
                hready[j] = split(hh[:, j, :], hl[:, j, :], M[:, j, :], m_ready[j], last, eng=POOL if j % 2 else DVE)
            it = take("out")
            done = add_residual(it)
            for j in range(NT):
                hfree[j] = [done]
            st.close()

        ADA = [(l, j, half) for l in range(2) for j in range(24) for half in range(2)]
        NADA = 3
        s_ada = [semaphore(f"s_ada{i}") for i in range(NADA)]
        ada_at = dict(load=0, use=0, limit=0)
        ada_land, ada_free = {}, [[] for _ in range(NADA)]
        accfree = [[] for _ in acc]

        def ada_load(slots):
            n = ada_at["load"]
            if n == ada_at["limit"] or n - ada_at["use"] >= NADA:
                return
            ada_at["load"] += 1
            l, j, half = ADA[n]
            s = n % NADA
            view = A["ada_w_2"][l].rearrange("(k p) n -> p k n", p=128)[:, 4 * half:4 * half + 4, 256 * j:256 * j + 256]
            ada_land[n] = ACT.dma(s_ada[s], 16 * (n // NADA + 1), slots[s][:, :].rearrange("p (k n) -> p k n", n=256), view, ada_free[s])

        def ada_step(slots):
            n = ada_at["use"]
            if n == ada_at["load"]:
                return
            ada_at["use"] += 1
            l, j, half = ADA[n]
            a = acc[j % 4]
            w = slots[n % NADA][:, :].rearrange("p (k n) -> p k n", n=256)
            m = None
            for i in range(4):
                k = 4 * half + i
                if k == 0:
                    m = DVE.run(lambda e: e.tensor_scalar(a[:, :], w[:, 0, :], cact[:, 0:1], None, MUL), ada_land[n], accfree[j % 4], m_cact)
                else:
                    m = DVE.run(lambda e, k=k, i=i: e.scalar_tensor_tensor(a[:, :], w[:, i, :], cact[:, k:k + 1], a[:, :], MUL, ADD),
                                ada_land[n], m or ada_last[0])
            ada_last[0] = m
            ada_free[n % NADA] = [m]
            if half:
                ada_sum.append((l, j, m))

        def ada_finish():
            while ada_sum:
                l, j, m = ada_sum.pop(0)
                c = 48 * l + 2 * j
                a = acc[j % 4]
                PE.wait(pfree[6], m)
                PE.quiet(mm(ps[6][:, c:c + 1], a[:, 0:128], ones[:, 0:1], skip_group_check=True))
                p = PE.run(mm(ps[6][:, c + 1:c + 2], a[:, 128:256], ones[:, 0:1], skip_group_check=True))
                accfree[j % 4] = [p]

        def ada_collect(l):
            c = slice(48 * l, 48 * l + 48)
            m = DVE.run(lambda e: e.tensor_tensor(mod[:, c], ps[6][:, c], v("ada_b", 48 * l, 48), ADD), PE.last())
            pfree[6] = [m]
            ada_done.append(m)

        ada_last, ada_sum = [None], []
        ada_done = []
        m_cact = ACT.run(lambda e: e.activation(cact[:, :], v("c", 0, 8), ACTF.Silu))

        def ffn(convs, offset, scale=None, spare=False, gain=None):
            st = ExitStack()
            begin = fence()
            ah, al = sb([128, ACT_RING, L], R, st), sb([128, ACT_RING, L], R, st)
            yg, yu, sg = ([sb([128, L], stack=st) for _ in range(2)] for _ in range(3))
            a_ready, a_free = {}, [[] for _ in range(ACT_RING)]
            tfree = [[begin], [begin]]
            slots = []
            if spare:
                ada_at["limit"] += len(ADA) // 2
                slots += [sb([128, 1024], stack=st) for _ in range(NADA)]
                for i in range(NADA):
                    ada_free[i] = [begin]
                    ada_load(slots)

            def conv(cv, tile, b, done, dst, *free):
                wt, bias = cv
                m = ACT.run(lambda e: e.activation(dst[:, :], ps[b][:, :], ACTF.Identity, bias=bias(tile), scale=wt(offset, tile)), done, *free)
                for tap in range(3):
                    sh = tap - offset
                    if sh < 0:
                        o, i = dst[:, -sh:L], ps[b][:, 0:L + sh]
                    elif sh > 0:
                        o, i = dst[:, 0:L - sh], ps[b][:, sh:L]
                    else:
                        continue
                    m = DVE.run(lambda e, o=o, i=i, tap=tap: e.scalar_tensor_tensor(o, i, wt(tap, tile), o, MUL, ADD), m)
                return m

            def ada_steps(count):
                for _ in range(count if spare else 0):
                    ada_step(slots)
                    ada_load(slots)

            def up_pair(p):
                it = take("gate")
                dg = project(it, (0, 1))
                release(it, dg[-1])
                g = []
                for i in range(2):
                    t = 2 * p + i
                    m = conv(convs[0], t, i, dg[i], yg[i], tfree[i])
                    pfree[i] = [m]
                    g.append(ACT.run(lambda e, i=i: e.activation(sg[i][:, :], yg[i][:, :], ACTF.Silu), m, tfree[i]))
                pump()
                ada_steps(2)
                it = take("up")
                du = project(it, (2, 3))
                release(it, du[-1])
                for i in range(2):
                    t = 2 * p + i
                    b = 2 + i
                    if convs[1] is not None:
                        m = conv(convs[1], t, b, du[i], yu[i], tfree[i])
                        pfree[b] = [m]
                        m = DVE.run(lambda e, i=i: e.tensor_tensor(yu[i][:, :], sg[i][:, :], yu[i][:, :], MUL), m, g[i], tfree[i])
                    else:
                        m = DVE.run(lambda e, i=i, b=b: e.tensor_tensor(yu[i][:, :], sg[i][:, :], ps[b][:, :], MUL), du[i], g[i], tfree[i])
                        pfree[b] = [m]
                    s = t % ACT_RING
                    a_ready[t] = split(ah[:, s, :], al[:, s, :], yu[i][:, :], m, a_free[s], begin, eng=POOL)
                    tfree[i] = [m] + a_ready[t]
                pump()

            def down(gi):
                q0, q1 = GROUPS[gi]
                t0 = 2 * q0
                rhs = dict(xh=lambda k: ah[:, (t0 + k) % ACT_RING, :], xl=lambda k: al[:, (t0 + k) % ACT_RING, :],
                           ready=lambda k: a_ready[t0 + k])
                it = take("down")
                done = add_residual(it, scale, stats=gi == len(GROUPS) - 1, gain=gain, rhs=rhs, banks=((0, 1), (4, 5)))
                for t in range(t0, 2 * q1):
                    a_free[t % ACT_RING] = [done]

            for gi, (p0, p1) in enumerate(GROUPS):
                for p in range(p0, p1):
                    up_pair(p)
                    if spare:
                        ada_finish()
                    ada_steps(3)
                    if gi and p == p0:
                        down(gi - 1)
            last = PE.last()
            for j in range(NT):
                hfree[j] = [last]
            if spare:
                while ada_at["use"] < ada_at["load"]:
                    ada_step(slots)
            down(len(GROUPS) - 1)
            if spare:
                ada_finish()
                ada_collect(ada_at["limit"] // (len(ADA) // 2) - 1)
            st.close()

        def ffn1(layer):
            def wt(tap, tile):
                return v("cw0", 132 * layer + 44 * tap + tile)

            def bias(tile):
                return v("cb0", 44 * layer + tile)

            normalise(lambda j: v("ffn_norm", 8 * layer + j))
            ffn([(wt, bias), (lambda tap, tile: wt(tap, AF + tile), lambda tile: bias(AF + tile))], 2, spare=True,
                gain=(lambda j: v("final_norm", j)) if layer else None)

        def ffn2(layer):
            def wt(tap, tile):
                return v("cw1", 66 * layer + 22 * tap + tile)

            m = modulated(layer, "norm2", 3)
            ffn([(wt, lambda tile: v("cb1", 22 * layer + tile)), None], 1, scale=m)

        def modulated(layer, gain, first):
            base = 48 * layer + 8 * first
            m = DVE.run(lambda e: e.tensor_scalar(g1c[:, :], mod[:, base + 8:base + 16], 1.0, None, ADD), ada_done)
            m = DVE.run(lambda e: e.tensor_tensor(g1c[:, :], g1c[:, :], v(gain, 8 * layer, 8), MUL), m)
            DVE.wait(m)
            normalise(lambda j: g1c[:, j:j + 1], lambda j: mod[:, base + j:base + j + 1])
            return lambda j: mod[:, base + 16 + j:base + 17 + j]

        def end_and_modulated():
            m = DVE.run(lambda e: e.tensor_scalar(g1c[:, :], mod[:, 8:16], 1.0, None, ADD), ada_done)
            m = DVE.run(lambda e: e.tensor_tensor(g1c[:, :], g1c[:, :], v("norm1", 0, 8), MUL), m)
            m_g = DVE.run(lambda e: e.tensor_tensor(g1c[:, :], g1c[:, :], v("final_norm", 0, 8), MUL), m)
            r1, r2, t = rc[0][:, 0:4], rc[1][:, 0:4], rc[1][:, 4:8]
            a = ACT.run(lambda e: e.activation(r1, ps[STAT][:, 0:4], ACTF.Sqrt, bias=eps[:, 0:1], scale=1.0 / D), stat["m"])
            m = DVE.run(lambda e: e.reciprocal(r1, r1), a)
            n = DVE.run(lambda e: e.tensor_tensor(t, ps[STAT][:, 4:8], r1, MUL), m)
            n = DVE.run(lambda e: e.tensor_tensor(t, t, r1, MUL), n)
            pfree[STAT] = [n]
            a = ACT.run(lambda e: e.activation(r2, t, ACTF.Sqrt, bias=eps[:, 0:1], scale=1.0 / D), n)
            n = DVE.run(lambda e: e.reciprocal(r2, r2), a)
            n = DVE.run(lambda e: e.tensor_tensor(r2, r2, r1, MUL), n)
            spread = []
            for i, r, bank in ((1, r2, STAT), (0, r1, 6)):
                wide = rb[i][:, :].rearrange("p (c f) -> p c f", c=4)
                w = DVE.run(lambda e, wide=wide, r=r: e.tensor_copy(wide, r.unsqueeze(2).broadcast_to([128, 4, 128])), n, rbfree[i])
                spread.append(spread_rms(bank, (i, w)))
            DVE.wait(m_g)
            shifted(lambda j: g1c[:, j:j + 1], lambda j: mod[:, j:j + 1], spread[0])
            for j in range(NT):
                xready[j] = DVE.run(lambda e, j=j: e.scalar_tensor_tensor(x[:, j, :], x[:, j, :], v("final_norm", j), ps[6][:, :], MUL, MUL),
                                    spread[1], xready[j])
            pfree[6] = [xready[NT - 1]]
            return lambda j: mod[:, 16 + j:17 + j]

        def attend(units, logits, soften, value, o_of, finish, pool, begin):
            P, PT, mx, nm, sm, rs = pool
            pf, ptf = [begin for _ in P], [begin for _ in PT]
            LB, TB = (0, 1, 2), (3, 4)
            info, finished = {}, []

            def first(u):
                b = LB[u % 3]
                PE.wait(pfree[b])
                m = logits(units[u], b)
                k = u % len(P)
                c = slice(u % 8, u % 8 + 1)
                e = soften(units[u], b, m, P[k], mx[:, c], nm[:, c], sm[:, c], pf[k])
                info[u] = e

            def scale(u):
                k, S, e = u % len(P), units[u][2], info[u]
                c = slice(u % 8, u % 8 + 1)
                r = DVE.run(lambda e_: e_.reciprocal(rs[:, c], sm[:, c]), e)
                n = POOL.run(lambda e_: e_.tensor_scalar(P[k][:, 0:S], P[k][:, 0:S], rs[:, c], 1.0, MUL, MUL), r, e)
                info[u] = n

            def second(u):
                k, S, b = u % len(P), units[u][2], TB[u % 2]
                PE.wait(pfree[b], info[u])
                for s in range(S // 128):
                    f = lambda e, s=s: e.transpose(ps[b][:, 128 * s:128 * s + 128], P[k][:, 128 * s:128 * s + 128], ident[:, :])
                    if s < S // 128 - 1:
                        PE.quiet(f)
                m = PE.run(f)
                pf[k] = [m]
                q = u % len(PT)
                a = ACT.run(lambda e: e.copy(PT[q][:, 0:S], ps[b][:, 0:S]), m, ptf[q])
                pfree[b] = [a]
                info[u] = a

            def third(u):
                q, S = u % len(PT), units[u][2]
                o = o_of(units[u])
                PE.wait(info[u])
                n = S // 128
                for s in range(n):
                    f = mm(o, value(units[u], s), PT[q][:, 128 * s:128 * s + 128], s == 0, s == n - 1, skip_group_check=True)
                    if s < n - 1:
                        PE.quiet(f)
                m = PE.run(f)
                ptf[q] = [m]
                finished.append((u, units[u], m))

            n = len(units)
            lag = len(P) - 1
            for i in range(n + lag + 1):
                if 0 <= i - lag < n:
                    second(i - lag)
                if i < n:
                    first(i)
                if 0 <= i - 1 < n:
                    scale(i - 1)
                while finished and finished[0][0] <= i - lag - 3:
                    finish(*finished.pop(0))
                if 0 <= i - lag - 1 < n:
                    third(i - lag - 1)
            while finished:
                finish(*finished.pop(0))

        def softmax_pool(st, count=5, spare=[]):
            return ([sb([128, L], stack=st) for _ in range(count)] + spare, [sb([128, L], stack=st) for _ in range(2)],
                    *(sb([128, 8], stack=st) for _ in range(4)))

        OBANK = (5, 6)

        def finish_heads(u, unit, m):
            h, tt, S = unit
            if h % 2 == 1 and tt == 3:
                j, b = h // 2, OBANK[(h // 2) % 2]
                hi = ACT.run(lambda e: e.activation(hh[:, j, :], ps[b][:, :], ACTF.Copy), m, hfree[j])
                lo = DVE.run(lambda e: e.tensor_tensor(hl[:, j, :], ps[b][:, :], hh[:, j, :].bitcast(F), SUB), hi)
                hready[j] = [hi, lo]
                pfree[b] = [hi, lo]

        def o_region(unit):
            h, tt, S = unit
            b = OBANK[(h // 2) % 2]
            if h % 2 == 0 and tt == 0:
                PE.wait(pfree[b])
            return ps[b][64 * (h % 2):64 * (h % 2) + 64, 128 * tt:128 * tt + 128]

        def dsa():
            st = ExitStack()
            begin = fence()
            q = sb([128, 8, L], stack=st)
            k2 = sb([128, 2, L], stack=st)
            V = sb([128, 4, 128], stack=st)
            qi = sb([128, 4, L], stack=st)
            ki = sb([128, L], stack=st)
            wi = sb([128, 4, 8], stack=st)
            work = sb([128, 1280], stack=st)
            relu = [sb([128, L], stack=st) for _ in range(2)]
            T = [sb([128, L], stack=st) for _ in range(4)]
            Lg = [sb([128, L], stack=st) for _ in range(2)]
            cmin, cadd = sb([128, 128], stack=st), sb([128, 128], stack=st)
            m8 = sb([128, 8], stack=st)
            pool = softmax_pool(st, 3, relu)
            m_c = [load(cmin[:, :], A["c_cmin"], begin), load(cadd[:, :], A["c_cadd"], begin)]
            sel = [work[:, 128 * (tt * (tt + 1) // 2):128 * (tt * (tt + 1) // 2) + 128 * (tt + 1)] for tt in range(4)]
            Tsem = [semaphore(f"s_T{i}") for i in range(4)]
            Tfree = [[] for _ in range(4)]
            Tland = {}

            def load_bias(h):
                s = h % 4
                src = bass.AP(tensor=scratch, offset=128 * 640 * h + 127, ap=[[639, 128], [1, 512]])
                Tland[h] = ACT.dma(Tsem[s], 16 * (h // 4 + 1), T[s][:, :], src, Tfree[s], begin, m_scratch)

            for h in range(3):
                load_bias(h)

            qi_ready = []
            for c in range(2):
                it = take("ix")
                banks = (0, 1) if c else (2, 3)
                done = project(it, banks)
                release(it, done[-1])
                for i in range(2):
                    j, b = 2 * c + i, banks[i]
                    m = ACT.run(lambda e, j=j, b=b: e.copy(qi[:, j, :], ps[b][:, :]), done[i], begin)
                    pfree[b] = [m]
                    qi_ready.append(m)
                pump()
            it = take("kw")
            a, b = w_views(it)
            PE.wait(it["ready"], pfree[4], pfree[5])
            for k in range(NT):
                PE.wait(hready[k])
                done = [product(o, [((a[:, k, c], b[:, k, c]), (hh[:, k, :], hl[:, k, :]))], k == 0, k == NT - 1)
                        for o, c in ((ps[4][:, :], slice(0, 128)), (ps[5][0:8, :], slice(128, 136)))]
            release(it, done[1])
            m_ki = ACT.run(lambda e: e.copy(ki[:, :], ps[4][:, :]), done[0], begin)
            pfree[4] = [m_ki]
            m = ACT.run(lambda e: e.copy(relu[0][0:8, :], ps[5][0:8, :]), done[1])
            PE.wait(m)
            for tt in range(4):
                f = mm(ps[5][:, 8 * tt:8 * tt + 8], relu[0][0:8, 128 * tt:128 * tt + 128], ident[0:8, 0:8], skip_group_check=True)
                if tt < 3:
                    PE.quiet(f)
            m_turned = m = PE.run(f)
            m_wi = DVE.run(lambda e: e.tensor_scalar(wi[:, :, :].rearrange("p a b -> p (a b)"), ps[5][:, 0:32],
                                                     float(8 ** -0.5 * 64 ** -0.5), None, MUL), m, begin)
            pfree[5] = [m_wi]
            pump()
            rl = [[m_turned], []]
            n = 0
            m_sc = [None] * 4
            for tt in range(1, 4):
                S = 128 * (tt + 1)
                for h in range(8):
                    b = (4, 5, 6)[n % 3]
                    pr = slice(64 * (h % 2), 64 * (h % 2) + 64)
                    m = PE.run(mm(ps[b][:, 0:S], qi[pr, h // 2, 128 * tt:128 * tt + 128], ki[pr, 0:S]), qi_ready, m_ki, pfree[b])
                    s = n % 2
                    m = ACT.run(lambda e, b=b, s=s, S=S: e.activation(relu[s][:, 0:S], ps[b][:, 0:S], ACTF.Relu), m, rl[s], begin)
                    pfree[b] = [m]
                    o = sel[tt]
                    if h == 0:
                        m = DVE.run(lambda e, o=o, s=s, S=S, tt=tt, h=h: e.tensor_scalar(
                            o, relu[s][:, 0:S], wi[:, tt, h:h + 1], 0.0, MUL, ADD), m, m_wi)
                    else:
                        m = DVE.run(lambda e, o=o, s=s, S=S, tt=tt, h=h: e.scalar_tensor_tensor(
                            o, relu[s][:, 0:S], wi[:, tt, h:h + 1], o, MUL, ADD), m, m_sc[tt])
                    rl[s] = [m]
                    m_sc[tt] = m
                    n += 1
            m_sel = [DVE.run(lambda e: e.tensor_copy(sel[0], cadd[:, :]), m_c, begin)]
            m8m = None
            for tt in range(1, 4):
                o = sel[tt]
                m = DVE.run(lambda e, o=o, tt=tt: e.tensor_tensor(o[:, 128 * tt:128 * tt + 128], o[:, 128 * tt:128 * tt + 128],
                                                                cmin[:, :], ALU.min), m_sc[tt])
                for _ in range(TOPK // 8):
                    a = DVE.run(lambda e, o=o: e.max(m8[:, :], o), m)
                    m = DVE.run(lambda e, o=o: e.match_replace(o, m8[:, :], o, GONE), a)
                m = DVE.run(lambda e, o=o: e.tensor_scalar(o, o, GONE, NEG, ALU.is_gt, MUL), m)
                m_sel.append(m)
            it = take("kk")
            done = project(it, (0, 1))
            release(it, done[-1])
            m_k = []
            for i in range(2):
                m_k.append(ACT.run(lambda e, i=i: e.copy(k2[:, i, :], ps[i][:, :]), done[i], begin))
                pfree[i] = [m_k[-1]]
            pump()
            it = take("v")
            PE.wait(pfree[2])
            for tt in range(4):
                m = project_tokens(it, 0, 128, ps[2][:, 128 * tt:128 * tt + 128], tt)
            release(it, m)
            m_v = ACT.run(lambda e: e.copy(V[:, :, :].rearrange("p a b -> p (a b)"), ps[2][:, :]), m, begin)
            pfree[2] = [m_v]
            pump()
            m_q = []
            for c in range(4):
                it = take("q")
                banks = (0, 1) if c % 2 else (2, 3)
                done = project(it, banks)
                release(it, done[-1])
                for i in range(2):
                    j, b = 2 * c + i, banks[i]
                    m = ACT.run(lambda e, j=j, b=b: e.copy(q[:, j, :], ps[b][:, :]), done[i], begin)
                    pfree[b] = [m]
                    m_q.append(m)
                pump()
            for j in range(NT):
                hfree[j] = [done[-1]]
            lgf = [[], []]
            nun = [0]

            def logits(unit, b):
                h, tt, S = unit
                pr = slice(64 * (h % 2), 64 * (h % 2) + 64)
                return PE.run(mm(ps[b][:, 0:S], q[pr, h // 2, 128 * tt:128 * tt + 128], k2[pr, h // 8, 0:S]), m_q[h // 2], m_k)

            def soften(unit, b, m, P, mx, nm, sm, free):
                h, tt, S = unit
                if tt == 0 and h + 3 < 16:
                    load_bias(h + 3)
                s = nun[0] % 2
                nun[0] += 1
                lg = Lg[s][:, 0:S]
                Tv = T[h % 4][:, 384 - 128 * tt:512]
                m = DVE.run(lambda e: e.scalar_tensor_tensor(lg, ps[b][:, 0:S], 0.125, Tv, MUL, ADD), m, Tland[h], lgf[s])
                pfree[b] = [m]
                if tt == 3:
                    Tfree[h % 4] = [m]
                m = DVE.run(lambda e: e.tensor_tensor_reduce(lg, lg, sel[tt], 1.0, -3e38, ADD, ALU.max, mx), m, m_sel[tt])
                m2 = DVE.run(lambda e: e.tensor_scalar(nm, mx, -1.0, None, MUL), m)
                a = ACT.run(lambda e: e.activation(P[:, 0:S], lg, ACTF.Exp, bias=nm, scale=1.0, accum_out=sm), m2, free)
                lgf[s] = [a]
                return a

            def value(unit, s):
                g = unit[0] // 8
                return V[:, s, 64 * g:64 * g + 64]

            PE.wait(m_v)
            attend([(h, tt, 128 * (tt + 1)) for h in range(16) for tt in range(4)], logits, soften, value, o_region,
                   finish_heads, pool, [begin] + rl)
            it = take("out")
            done = add_residual(it)
            for j in range(NT):
                hfree[j] = [done]
            st.close()

        def attention(scale):
            st = ExitStack()
            begin = fence()
            q = sb([128, 8, L], stack=st)
            kr = sb([128, 4, L], stack=st)
            V = sb([128, 4, 256], stack=st)
            cos, sin = sb([128, L], stack=st), sb([128, L], stack=st)
            perm, pairs = sb([128, 128], stack=st), sb([128, 2], stack=st)
            qg = [sb([128, L], stack=st) for _ in range(2)]
            t2 = [sb([128, L], stack=st) for _ in range(2)]
            pool = softmax_pool(st)
            m_c = [load(d[:, :], A[n], begin) for d, n in ((cos, "c_cos"), (sin, "c_sin"), (perm, "c_perm"), (pairs, "c_pairs"))]
            gf, tf = [[], []], [[], []]
            n = [0]

            def rotate(dst, b, done, gain, marks):
                i = n[0] % 2
                n[0] += 1
                B1, B2 = ((4, 5), (6, 7))[i]
                a = ACT.run(lambda e: e.activation(qg[i][:, :], ps[b][:, :], ACTF.Copy, scale=gain), done, gf[i], begin)
                s = ACT.run(lambda e: e.activation(sq[i][:, :], ps[b][:, :], ACTF.Square), sqfree[i])
                pfree[b] = [s]

                def middle():
                    PE.wait(pfree[B1], m_c)
                    p1 = token_sums(B1, sq[i], pairs[:, :], True, True, s)
                    sqfree[i] = [p1]
                    p2 = PE.run(mm(ps[B2][:, :], perm[:, :], qg[i][:, :]), a, pfree[B2])
                    im = inverse_rms(B1, 64, p1, heads=2)
                    m = DVE.run(lambda e: e.tensor_tensor(t2[i][:, :], ps[B2][:, :], sin[:, :], MUL), p2, tf[i], m_c, begin)
                    pfree[B2] = [m]
                    m1 = DVE.run(lambda e: e.tensor_tensor(qg[i][:, :], qg[i][:, :], cos[:, :], MUL), p2)
                    m = DVE.run(lambda e: e.tensor_tensor(t2[i][:, :], t2[i][:, :], qg[i][:, :], ADD), m, m1)
                    gf[i] = [m]

                    def end():
                        r = spread_rms(B1, im)
                        m2 = DVE.run(lambda e: e.tensor_tensor(dst, t2[i][:, :], ps[B1][:, :], MUL), m, r, begin)
                        pfree[B1] = [m2]
                        tf[i] = [m2]
                        marks.append(m2)
                    return end
                return middle

            waiting = dict(middle=[], end=[])

            def turn(new):
                for f in waiting["end"]:
                    f()
                waiting["end"] = [f() for f in waiting["middle"]]
                waiting["middle"] = new()

            m_k = []
            for g in range(2):
                it = take("kk")
                banks = (0, 1) if g else (2, 3)
                done = project(it, banks)
                release(it, done[-1])
                turn(lambda: [rotate(kr[:, 2 * g + i, :], banks[i], done[i], v("k_gain"), m_k) for i in range(2)])
                pump()
            it = take("v")
            m_v = []
            for tt in range(4):
                b = tt % 2
                PE.wait(pfree[b])
                m = project_tokens(it, 0, 256, ps[b][:, 0:256], tt)
                m_v.append(ACT.run(lambda e, b=b, tt=tt: e.copy(V[:, tt, :], ps[b][:, 0:256]), m, begin))
                pfree[b] = [m_v[-1]]
            release(it, m)
            pump()
            m_q = []
            for c in range(4):
                it = take("q")
                banks = (0, 1) if c % 2 else (2, 3)
                done = project(it, banks)
                release(it, done[-1])
                turn(lambda: [rotate(q[:, 2 * c + i, :], banks[i], done[i], v("q_gain"), m_q) for i in range(2)])
                pump()
            turn(list)
            turn(list)
            for j in range(NT):
                hfree[j] = [done[-1]]

            def logits(unit, b):
                h, tt, S = unit
                pr = slice(64 * (h % 2), 64 * (h % 2) + 64)
                return PE.run(mm(ps[b][:, :], q[pr, h // 2, 128 * tt:128 * tt + 128], kr[pr, h // 4, :]), m_q[h // 2], m_k)

            def soften(unit, b, m, P, mx, nm, sm, free):
                m = DVE.run(lambda e: e.tensor_reduce(mx, ps[b][:, :], AX_X, ALU.max), m)
                m = DVE.run(lambda e: e.tensor_scalar(nm, mx, -0.125, None, MUL), m)
                a = ACT.run(lambda e: e.activation(P[:, :], ps[b][:, :], ACTF.Exp, bias=nm, scale=0.125, accum_out=sm), m, free)
                pfree[b] = [a]
                return a

            def value(unit, s):
                g = unit[0] // 4
                return V[:, s, 64 * g:64 * g + 64]

            PE.wait(m_v)
            attend([(h, tt, L) for h in range(16) for tt in range(4)], logits, soften, value, o_region, finish_heads, pool, begin)
            it = take("out")
            done = add_residual(it, scale)
            for j in range(NT):
                hfree[j] = [done]
            st.close()

        def hyena(scale):
            st = ExitStack()
            begin = fence()
            u = sb([128, 24, L], stack=st)
            aT, w3 = rb[0][0:64, :], rb[1][0:64, :]
            w1, w2 = sb([33, 64], stack=st), sb([64, 64], stack=st)
            dec = sb([128, 4, 256], stack=st)
            sf, df = sb([128, 1024], stack=st), sb([128, 1024], stack=st)
            Yt = acc4
            A4b = sb([128, 1024], stack=st)
            inv = sb([128, 8], stack=st)
            m_w1 = load(w1[:, :], A["hy_f_w1_2"][0], begin)
            m_w2 = load(w2[:, :], A["hy_f_w2_2"][0], begin)

            zt = sf[0:33, 0:L]
            m_z = load(zt, A["c_zT"], begin)
            C1 = 6.28125
            C2 = float(np.float32(2 * math.pi - C1))
            C3 = 2 * math.pi - C1 - C2
            MAGIC = 12582912.0

            def sine(dst, b, bias, m):
                t, k = df[0:64, 0:L], df[0:64, L:2 * L]
                m = DVE.run(lambda e: e.tensor_scalar(t, ps[b][0:64, :], bias, v("freq")[0:64], ADD, MUL), m, begin)
                pfree[b] = [m]
                n = DVE.run(lambda e: e.tensor_scalar(k, t, 1.0 / (2 * math.pi), MAGIC, MUL, ADD), m)
                n = DVE.run(lambda e: e.tensor_scalar(k, k, -MAGIC, None, ADD), n)
                for cst in (C1, C2, C3):
                    n = DVE.run(lambda e, cst=cst: e.scalar_tensor_tensor(t, k, -cst, t, MUL, ADD), n)
                n = DVE.run(lambda e: e.tensor_scalar(t, t, 3.1415925, -3.1415925, ALU.min, ALU.max), n)
                return ACT.run(lambda e: e.activation(dst, t, ACTF.Sin), n, begin)

            u_ready = []
            for c in range(12):
                it = take("hy")
                banks = ((0, 1), (2, 3))[c % 2]
                done = project(it, banks)
                release(it, done[-1])
                for i in range(2):
                    t, b = 2 * c + i, banks[i]
                    m = ACT.run(lambda e, t=t, b=b: e.activation(u[:, t, :], ps[b][:, :], ACTF.Identity, bias=v("hy_cb", t),
                                                                 scale=v("hy_cw", 24 + t)), done[i], begin)
                    m = DVE.run(lambda e, t=t, b=b: e.scalar_tensor_tensor(u[:, t, 1:L], ps[b][:, 0:L - 1], v("hy_cw", t),
                                                                          u[:, t, 1:L], MUL, ADD), m)
                    m = DVE.run(lambda e, t=t, b=b: e.scalar_tensor_tensor(u[:, t, 0:L - 1], ps[b][:, 1:L], v("hy_cw", 48 + t),
                                                                          u[:, t, 0:L - 1], MUL, ADD), m)
                    pfree[b] = [m]
                    u_ready.append(m)
                if c == 3:
                    m = PE.run(mm(ps[4][0:64, :], w1[:, :], zt), m_z, m_w1, pfree[4])
                    m_a = sine(aT[:, :], 4, v("fb1")[0:64], m)
                if c == 6:
                    m = PE.run(mm(ps[4][0:64, :], w2[:, :], aT[:, :]), m_a, m_w2, pfree[4])
                    m_a = sine(aT[:, :], 4, v("fb2")[0:64], m)
                pump()
            all_h = done[-1]

            fw_it, iv_it, hold = take("fw"), take("iv"), take("hold")
            held = [take("rawhold") for _ in range(3)]
            fwh, fwl = w_views(fw_it)
            ivh, ivl = w_views(iv_it)
            yh = wh[hold["w"]][:, :].rearrange("p (f q c) -> p f q c", f=2, q=4)
            yl = wl[hold["w"]][:, :].rearrange("p (f q c) -> p f q c", f=2, q=4)
            DVE.wait(*[h["raw_free"] for h in held])
            POOL.wait(*[h["raw_free"] for h in held])
            ACT.wait(hold["free"])
            POOL.wait(hold["free"])
            Fb = raw[held[0]["r"]][:, :].rearrange("p (t c) -> p t c", t=4)
            KK = raw[held[1]["r"]][:, :].rearrange("p (f q c) -> p f q c", f=2, q=4)
            XX = raw[held[2]["r"]][:, 0:1024].rearrange("p (q c) -> p q c", q=4)
            A4s = [raw[held[2]["r"]][:, 1024:2048].rearrange("p (q c) -> p q c", q=4), A4b[:, :].rearrange("p (q c) -> p q c", q=4)]
            hv, lv = (t[:, 0:6, :].rearrange("p a l -> p (a l)").rearrange("p (w t c) -> p w t c", w=3, t=4) for t in (hh, hl))
            Yv = Yt[:, :].rearrange("p (w f c) -> p w f c", w=2, f=2)
            sv, dv = (t[:, :].rearrange("p (t c) -> p t c", t=4) for t in (sf, df))
            ef, tv = [sq[0], sq[1]], [ht[0], ht[1]]
            efree, tfree = [sqfree[0], sqfree[1]], [htfree[0], htfree[1]]
            free = dict(w3=[], dec=[], Fb=[], s=[], d=[], sh=[all_h], dh=[all_h], zh=[all_h], KK=[[], []], XX=[], A4=[[], [begin]], Yt=[begin], y=[])
            nld = [0, 0]
            s_w3, s_dec = semaphore("s_w3"), semaphore("s_dec")
            cnt = [0]

            def filters(o, cq, eng=POOL, low=None):
                nld[0] += 2
                nld[1] += 1
                src = A["hy_f_w3_2"][0]
                for d_ in range(2):
                    c = 2048 * o + 1024 * d_ + 256 * cq
                    mw = SP.dma(s_w3, 16 * nld[0], w3[:, 256 * d_:256 * d_ + 256], src[:, c:c + 256], free["w3"], begin)
                md = SP.dma(s_dec, 16 * nld[1], dec[:, :, :], A["c_decay"][:, :, 256 * cq:256 * cq + 256], free["dec"], begin)
                ev = []
                for lt in range(4):
                    b = (6, 4, 5, 7)[lt]
                    PE.wait(mw, m_a, pfree[b])
                    p = PE.run(mm(ps[b][:, :], aT[:, 128 * lt:128 * lt + 128], w3[:, :]))
                    m = DVE.run(lambda e, b=b, lt=lt: e.tensor_tensor(
                        Fb[:, lt, :].rearrange("p (d c) -> p d c", d=2), ps[b][:, :].rearrange("p (d c) -> p d c", d=2),
                        dec[:, lt:lt + 1, :].broadcast_to([128, 2, 256]), MUL), p, md, free["Fb"])
                    pfree[b] = [m]
                    ev.append(m)
                free["w3"], free["dec"] = [p], [m]
                if low:
                    low()
                z0 = DVE.run(lambda e: e.memset(Fb[0:1, 0, 256:512], 0.0), ev)
                a = DVE.run(lambda e: e.tensor_tensor(sv, Fb[:, :, 0:256], Fb[:, :, 256:512], ADD), z0, free["s"])
                b_ = eng.run(lambda e: e.tensor_tensor(dv, Fb[:, :, 0:256], Fb[:, :, 256:512], SUB), z0, free["d"])
                s_r = split(hv[:, 0], lv[:, 0], sv, a, free["sh"], eng=eng)
                d_r = split(hv[:, 1], lv[:, 1], dv, b_, free["dh"], eng=eng)
                free["s"], free["d"] = s_r, d_r
                return dict(s=s_r, d=d_r, used=[a, b_], K={})

            def filter_sizes(fl, eng=POOL):
                ab = ACT.run(lambda e: e.activation(Fb[:, :, :], Fb[:, :, :], ACTF.Abs), fl["used"])
                ab = eng.run(lambda e: e.tensor_tensor(Fb[:, :, 0:256], Fb[:, :, 0:256], Fb[:, :, 256:512], ADD), ab)
                ab = eng.run(lambda e: e.tensor_tensor(Fb[:, 0:2, 0:256], Fb[:, 0:2, 0:256], Fb[:, 2:4, 0:256], ADD), ab)
                fl["ab"] = ab

            def filter_norm(fl):
                PE.wait(fl["ab"], pfree[7])
                for ct in range(2):
                    for lt in range(2):
                        f = mm(ps[7][:, ct:ct + 1], Fb[:, lt, 128 * ct:128 * ct + 128], ones[:, 0:1], lt == 0, lt == 1)
                        if lt == 0 or ct == 0:
                            PE.quiet(f)
                        else:
                            p = PE.run(f)
                free["Fb"] = [p]
                c = 2 * (cnt[0] % 4)
                cnt[0] += 1
                m = DVE.run(lambda e: e.reciprocal(inv[:, c:c + 2], ps[7][:, 0:2]), p)
                pfree[7] = [m]
                m = DVE.run(lambda e: e.tensor_scalar(inv[:, c:c + 2], inv[:, c:c + 2], 2.0 ** -9, None, MUL), m)
                fl["inv"], fl["minv"] = inv[:, c:c + 2], m

            def transform(srcs, ready, ft, dst, dfree, bA, bB):
                PE.wait(fw_it["ready"], *ready)
                out_marks = []
                for half, b in ((0, bA), (1, bB)):
                    PE.wait(pfree[b])
                    for q, sc in ((half, srcs[0]), (2 + half, srcs[1])):
                        cols = slice(256 * q + 128 * ft, 256 * q + 128 * ft + 128)
                        o = ps[b][:, 0:256] if q < 2 else ps[b][:, 256:512]
                        m = product(o, [((fwh[:, kt, cols], fwl[:, kt, cols]), (hv[:, sc, 2 * half + kt, :], lv[:, sc, 2 * half + kt, :]))
                                        for kt in range(2)], True, True)
                    out_marks.append(m)
                i = ft
                a = ACT.run(lambda e: e.copy(ef[i][:, :], ps[bA][:, :]), out_marks[0], efree[i])
                pfree[bA] = [a]
                m = DVE.run(lambda e: e.tensor_tensor(dst[:, 0:2, :].rearrange("p a c -> p (a c)"), ef[i][:, :], ps[bB][:, :], ADD),
                            a, out_marks[1], dfree)
                m2 = DVE.run(lambda e: e.tensor_tensor(dst[:, 2, :], ef[i][:, 0:256], ps[bB][:, 0:256], SUB), a)
                m3 = DVE.run(lambda e: e.tensor_tensor(dst[:, 3, :], ps[bB][:, 256:512], ef[i][:, 256:512], SUB))
                pfree[bB] = [m3]
                efree[i] = [m3]
                return m3, out_marks[1]

            def filter_transform(fl, ft):
                m, p = transform((0, 1), (fl["s"], fl["d"]), ft, KK[:, ft], free["KK"][ft], *((4, 5), (0, 1))[ft])
                fl["K"][ft] = m
                if ft:
                    free["sh"], free["dh"] = [p], [p]

            def tokens(cq):
                ready, parts = [], []
                for half in range(2):
                    b = 2 + half
                    PE.wait(pfree[b])
                    for t in range(2):
                        for ct in range(2):
                            j = 2 * cq + ct
                            src = u[:, j, half + 256 * t:256 * t + 256:2]
                            o = ps[b][:, 256 * t + 128 * ct:256 * t + 128 * ct + 128]
                            f = lambda e, o=o, src=src: e.transpose(o, src, ident[:, :])
                            PE.wait(u_ready[j])
                            if t == 1 and ct == 1:
                                p = PE.run(f)
                            else:
                                PE.quiet(f)
                    o = slice(2 * half, 2 * half + 2)
                    src = ps[b][:, :].rearrange("p (t c) -> p t c", t=2)
                    hi = ACT.run(lambda e, o=o, src=src: e.activation(hv[:, 2, o, :], src, ACTF.Copy), p, free["zh"])
                    parts.append((b, o, src, hi))

                def low():
                    for b, o, src, hi in parts:
                        lo = DVE.run(lambda e, o=o, src=src: e.tensor_tensor(lv[:, 2, o, :], src, hv[:, 2, o, :].bitcast(F), SUB), hi)
                        pfree[b] = [lo]
                        ready.extend((hi, lo))
                    return ready
                return low

            todo = [(o, cq) for o in range(2) for cq in range(4)]
            fl, zr, yr = {}, {}, {}

            def convolve(i, z, following, middle=None):
                sums = []
                for ft in range(2):
                    eng = DVE if ft and not following else POOL
                    bA, bB = ((4, 5), (0, 1))[ft]
                    m, p = transform((2, 2), (z,), ft, XX, free["XX"], bA, bB)
                    if following and ft == 0:
                        filter_sizes(following)
                    A4 = A4s[ft]
                    Kv = KK[:, ft].rearrange("p (f w) c -> p f w c", w=2)
                    Xv = XX.rearrange("p (f w) c -> p f w c", w=2)
                    Av = A4.rearrange("p (f w) c -> p f w c", w=2)
                    kc = Kv[:, :, 0:1, :].broadcast_to([128, 2, 2, 256])
                    ks = Kv[:, :, 1:2, :].broadcast_to([128, 2, 2, 256])
                    a = DVE.run(lambda e, Av=Av, kc=kc: e.tensor_tensor(Av, Xv, kc, MUL), m, fl[i]["K"][ft], free["A4"][ft])
                    b = DVE.run(lambda e, ks=ks: e.tensor_tensor(Xv, Xv, ks, MUL), a)
                    c_ = DVE.run(lambda e, Av=Av: e.tensor_tensor(Yv[:, 0], Av[:, :, 0, :], Xv[:, :, 1, :], SUB), a, b, free["Yt"])
                    s_ = DVE.run(lambda e, Av=Av: e.tensor_tensor(Yv[:, 1], Av[:, :, 1, :], Xv[:, :, 0, :], ADD), a, b)
                    free["XX"] = [s_]
                    free["KK"][ft] = [b]
                    if ft:
                        y0 = split(yh[:, 0], yl[:, 0], A4s[0], *sums, free["y"], eng=POOL)
                        free["A4"][0] = y0
                    UV = A4.rearrange("p (k w) c -> p k w c", w=2)
                    x1 = eng.run(lambda e, UV=UV: e.tensor_tensor(UV[:, 0], Yv[:, :, 0, :], Yv[:, :, 1, :], ADD), c_, s_)
                    x2 = eng.run(lambda e, UV=UV: e.tensor_tensor(UV[:, 1], Yv[:, :, 0, :], Yv[:, :, 1, :], SUB))
                    free["Yt"] = [x2]
                    sums = [x1, x2]
                    if ft == 0 and middle:
                        middle()
                free["zh"] = [p]
                if following:
                    if i + 2 == n:
                        zr[i + 1] = tokens(todo[i + 1][1])()
                    for ft in range(2):
                        filter_transform(following, ft)
                    filter_norm(following)
                    if i + 2 < n:
                        zr[i + 1] = tokens(todo[i + 1][1])
                y1 = split(yh[:, 1], yl[:, 1], A4s[1], *sums, free["y"], eng=eng)
                free["A4"][1] = y1
                return y0, y1

            skipped = [None, None]

            def skip(o, cq):
                for ct in range(2):
                    j, t = 2 * cq + ct, tv[ct]
                    skipped[ct] = ACT.run(lambda e, j=j, t=t: e.activation(t[:, :], u[:, j, :], ACTF.Copy, scale=v("skip", 8 * o + j)),
                                          u_ready[j], tfree[ct])

            def invert(o, cq, fl, yr):
                PE.wait(iv_it["ready"])
                done = [None, None]
                for ft in range(2):
                    PE.wait(yr[ft])
                    for ct in range(2):
                        b = 6 + ct
                        cs = slice(128 * ct, 128 * ct + 128)
                        PE.wait(pfree[b])
                        for half, (qc, qs) in enumerate(((0, 3), (2, 1))):
                            pairs = [((yh[:, ft, q, cs], yl[:, ft, q, cs]),
                                      (ivh[:, ft, 256 * g:256 * g + 256], ivl[:, ft, 256 * g:256 * g + 256]))
                                     for q, g in ((qc, half), (qs, 2 + half))]
                            done[ct] = product(ps[b][:, 256 * half:256 * half + 256], pairs, ft == 0 and half == 0, ft == 1,
                                               skip_group_check=True)
                for ct in range(2):
                    b = 6 + ct
                    j = 2 * cq + ct
                    p = done[ct]
                    t = tv[ct]
                    a = skipped[ct]
                    tw = t[:, :].rearrange("p (t two) -> p two t", two=2)
                    m = DVE.run(lambda e, b=b, ct=ct, tw=tw: e.scalar_tensor_tensor(
                        tw, ps[b][:, :].rearrange("p (two t) -> p two t", two=2), fl["inv"][:, ct:ct + 1], tw, MUL, ADD),
                        a, p, fl["minv"])
                    pfree[b] = [m]
                    u_ready[j] = DVE.run(lambda e, j=j, t=t: e.tensor_tensor(u[:, j, :], t[:, :], u[:, 8 * (o + 1) + j, :], MUL),
                                         m, u_ready[8 * (o + 1) + j])
                    tfree[ct] = [u_ready[j]]
                free["y"] = [p]
                return p

            n = len(todo)
            fl[0] = filters(*todo[0], eng=DVE)
            zr[0] = tokens(todo[0][1])()
            for ft in range(2):
                filter_transform(fl[0], ft)
            filter_sizes(fl[0], DVE)
            filter_norm(fl[0])
            fl[1] = filters(*todo[1])
            for i in range(n):
                before = (lambda: invert(*todo[i - 1], fl[i - 1], yr[i - 1])) if i else None
                if i and i < n - 1:
                    before()
                yr[i] = convolve(i, zr[i], fl.get(i + 1), before if i == n - 1 else None)
                if i + 1 < n:
                    skip(*todo[i])
                if i + 2 < n:
                    fl[i + 2] = filters(*todo[i + 2], low=lambda: zr.update({i + 1: zr[i + 1]()}))
                if i == n - 2:
                    release(held[0], *free["Fb"])
                    pump()
            skip(*todo[n - 1])
            release(held[1], free["KK"])
            release(held[2], free["XX"], free["A4"])
            release(fw_it, free["zh"])
            low_by[0] = DVE
            pump()
            for j in range(6):
                hready[j] = split(hh[:, j, :], hl[:, j, :], u[:, j, :], u_ready[j], free["zh"], free["sh"], free["dh"],
                                  eng=POOL if j % 2 else DVE)
            last = invert(*todo[n - 1], fl[n - 1], yr[n - 1])
            sqfree[0], sqfree[1] = efree
            htfree[0], htfree[1] = tfree
            end = fence()
            rbfree[0], rbfree[1] = [end], [end]
            release(iv_it, last)
            release(hold, last)
            pump()
            low_by[0] = POOL
            for j in (6, 7):
                hready[j] = split(hh[:, j, :], hl[:, j, :], u[:, j, :], u_ready[j], all_h, eng=POOL if j % 2 else DVE)
            it = take("out")
            done = add_residual(it, scale)
            for j in range(NT):
                hfree[j] = [done]
            st.close()

        def plain_norm(gain):
            r = spread_rms(STAT, inverse_rms(STAT, D, stat["m"]))
            for j in range(NT):
                xready[j] = DVE.run(lambda e, j=j: e.scalar_tensor_tensor(x[:, j, :], x[:, j, :], gain(j), ps[STAT][:, :], MUL, MUL),
                                    r, xready[j])
                pfree[STAT] = [xready[j]]

        steps = [
            lambda: (normalise(lambda j: v("attn_norm", j)), hgrn()),
            lambda: ffn1(0),
            lambda: (normalise(lambda j: v("attn_norm", 8 + j)), dsa()),
            lambda: ffn1(1),
            lambda: attention(end_and_modulated()),
            lambda: ffn2(0),
            lambda: hyena(modulated(1, "norm1", 0)),
            lambda: ffn2(1),
            lambda: plain_norm(lambda j: v("final2", j)),
        ]
        for step in steps[:stop]:
            step()

        begin = fence()
        st = ExitStack()
        ot = sb([128, 4, D], stack=st)
        for tt in range(4):
            stored = []
            for half in range(2):
                b = (2 * tt + half) % 4
                PE.wait(pfree[b])
                for i in range(4):
                    j = 4 * half + i
                    f = lambda e, b=b, i=i, j=j, tt=tt: e.transpose(ps[b][:, 128 * i:128 * i + 128], x[:, j, 128 * tt:128 * tt + 128], ident[:, :])
                    PE.wait(xready[j])
                    if i < 3:
                        PE.quiet(f)
                    else:
                        m = PE.run(f)
                eng = DVE if half else ACT
                o = ot[:, tt, 512 * half:512 * half + 512]
                fn = (lambda e, o=o, b=b: e.tensor_copy(o, ps[b][:, :])) if half else (lambda e, o=o, b=b: e.copy(o, ps[b][:, :]))
                m = eng.run(fn, m, begin)
                pfree[b] = [m]
                stored.append(m)
            SP.dma(s_out, 16 * (tt + 1), out[0, 128 * tt:128 * tt + 128, :], ot[:, tt, :], stored)
        SP.wait((s_out, 64))
        st.close()

        block = ctx.enter_context(nc.Block())

        @block.sync
        def _(e):
            for op in SP.ops:
                op(e)

        @block.scalar
        def _(e):
            for op in ACT.ops:
                op(e)

        @block.vector
        def _(e):
            for op in DVE.ops:
                op(e)

        @block.gpsimd
        def _(e):
            for op in POOL.ops:
                op(e)

        @block.tensor
        def _(e):
            for op in PE.ops:
                op(e)


_WEIGHTS = ["x", "hgrn_w_in", "hgrn_w_out", "dsa_w_in", "dsa_w_out", "rel_bias", "ffn_w_up", "ffn_w_down", "ada_w_2",
            "attn_w_qkv_2", "attn_w_o_2", "hy_w_in_2", "hy_f_w1_2", "hy_f_w2_2", "hy_f_w3_2", "hy_w_out_2",
            "ffn_w_up_2", "ffn_w_down_2"]


def lay_out(inputs):
    def by_feature(name):
        a = np.asarray(inputs[name])
        return a.reshape(-1, 128).T

    def twice(name):
        return np.tile(np.asarray(inputs[name]).reshape(-1, 1), (2, 1))

    parts = {
        "attn_norm": by_feature("attn_norm"), "ffn_norm": by_feature("ffn_norm"), "final_norm": by_feature("final_norm"),
        "gate_norm": by_feature("hgrn_gate_norm"), "lower": by_feature("hgrn_lower_bounds"), "c": by_feature("c_2"),
        "ada_b": by_feature("ada_b_2"), "norm1": by_feature("norm1_g_2"), "norm2": by_feature("norm2_g_2"),
        "final2": by_feature("final_g_2"), "q_gain": twice("attn_q_gain_2"), "k_gain": twice("attn_k_gain_2"),
        "hy_cw": by_feature("hy_conv_w_2"), "hy_cb": by_feature("hy_conv_b_2"), "skip": by_feature("hy_skip_2"),
        "cw0": by_feature("ffn_conv_w"), "cb0": by_feature("ffn_conv_b"), "cw1": by_feature("ffn_conv_w_2"),
        "cb1": by_feature("ffn_conv_b_2"), "fb1": twice("hy_f_b1_2"), "fb2": twice("hy_f_b2_2"), "freq": twice("hy_f_freq_2"),
    }
    arrays = {n: np.ascontiguousarray(inputs[n]) for n in _WEIGHTS}
    arrays["vec"] = np.ascontiguousarray(np.concatenate([parts[n] for n in VEC], axis=1))
    for n, a in shape_constants().items():
        arrays[f"c_{n}"] = a
    return arrays


def kernel(**inputs):
    import concourse.bacc as _bacc
    from concourse.bass_utils import run_bass_kernel_spmd as _run

    nc = _bacc.Bacc("TRN2", target_bir_lowering=False, num_devices=1)
    arrays, aps = {}, {}
    for name, a in lay_out(inputs).items():
        arrays[f"in_{name}"] = a
        aps[name] = nc.dram_tensor(f"in_{name}", a.shape, mybir.dt.from_np(a.dtype), kind="ExternalInput").ap()
    out = nc.dram_tensor("out_0", (1, L, D), F, kind="ExternalOutput").ap()
    build(nc, aps, out)
    r = _run(nc, [arrays], core_ids=[0])
    return r.results[0]["out_0"]
```
